# Optimizing a Trainium2 kernel written in Bass

```python
import jax, jax.numpy as jnp
from jax import lax
import numpy as np

D_MODEL = 2048
BATCH = 1
SEQ = 256
DEPTH = 1

N_MIXERS = 3
EXPAND = 2
D_INNER = EXPAND * D_MODEL
CHUNK = 128
A_GROUPS = 8
A_GROUP_DIM = D_INNER // A_GROUPS
B_GROUPS = 8
B_GROUP_DIM = D_INNER // B_GROUPS
POOL_WINDOWS = (2, 4, 8, 16)
C_GROUPS = len(POOL_WINDOWS)
C_GROUP_DIM = D_INNER // C_GROUPS
EPS = 1e-6


def _layers_of_kind(kind):
    return len(range(kind, DEPTH, N_MIXERS))

def rmsnorm(x, g):
    xf = x.astype(jnp.float32)
    y = xf * lax.rsqrt(jnp.mean(xf * xf, axis=-1, keepdims=True) + EPS)
    return (y * g.astype(jnp.float32)).astype(x.dtype)

def gmlp_mixer(h, w_in, v_gain, w_s, b_s):
    bsz, seq, _ = h.shape
    z = h @ w_in
    u, v, gate = jnp.split(z, 3, axis=-1)
    u = jax.nn.gelu(u)
    v = rmsnorm(jax.nn.gelu(v), v_gain)
    vc = v.reshape(bsz, seq // CHUNK, CHUNK, A_GROUPS, A_GROUP_DIM)
    sv = jnp.einsum('gpq,bnqgc->bnpgc', w_s, vc) + b_s.T[None, None, :, :, None]
    y = u * sv.reshape(bsz, seq, D_INNER)
    return y, gate

def fourier_mixer(h, w_in, w_mix):
    bsz, seq, _ = h.shape
    z = h @ w_in
    xb, gate = jnp.split(z, 2, axis=-1)
    xg = xb.reshape(bsz, seq, B_GROUPS, B_GROUP_DIM).astype(jnp.float32)
    f = jnp.fft.fft2(xg, axes=(1, 3), norm="ortho").real.astype(xb.dtype)
    y = jnp.einsum('bsgc,gcd->bsgd', f, w_mix).reshape(bsz, seq, D_INNER)
    return y, gate

def pool_mixer(h, w_in, w_mix, scale):
    bsz, seq, _ = h.shape
    z = h @ w_in
    xc, gate = jnp.split(z, 2, axis=-1)
    xg = xc.reshape(bsz, seq, C_GROUPS, C_GROUP_DIM)
    t = jnp.arange(seq)
    pooled = []
    for gi, w in enumerate(POOL_WINDOWS):
        xi = xg[:, :, gi, :].astype(jnp.float32)
        csum = jnp.pad(lax.cumsum(xi, axis=1), ((0, 0), (1, 0), (0, 0)))
        lo = jnp.clip(t - w // 2, 0, seq - 1)
        hi = jnp.clip(t + w - 1 - w // 2, 0, seq - 1)
        wsum = jnp.take(csum, hi + 1, axis=1) - jnp.take(csum, lo, axis=1)
        cnt = (hi - lo + 1).astype(jnp.float32)[None, :, None]
        pooled.append(wsum / cnt - xi)
    p = jnp.stack(pooled, axis=2).astype(xc.dtype)
    y = jnp.einsum('bsgc,gcd->bsgd', p, w_mix).reshape(bsz, seq, D_INNER) * scale
    return y, gate

def first_inputs(seed: int = 0) -> dict:
    key = jax.random.key(seed)
    ks = jax.random.split(key, 20)
    na, nb, nc = _layers_of_kind(0), _layers_of_kind(1), _layers_of_kind(2)
    f32 = jnp.float32
    nrm = lambda k, shape, s: jax.random.normal(k, shape, f32) * s
    din = D_MODEL ** -0.5
    dout = D_INNER ** -0.5
    return {
        "x": jax.random.normal(ks[0], (BATCH, SEQ, D_MODEL), f32),
        "a_norm": 1.0 + nrm(ks[1], (na, D_MODEL), 0.05),
        "a_w_in": nrm(ks[2], (na, D_MODEL, 3 * D_INNER), din),
        "a_v_gain": 1.0 + nrm(ks[3], (na, D_INNER), 0.05),
        "a_w_s": nrm(ks[4], (na, A_GROUPS, CHUNK, CHUNK), 0.5 * CHUNK ** -0.5),
        "a_b_s": 1.0 + nrm(ks[5], (na, A_GROUPS, CHUNK), 0.1),
        "a_w_out": nrm(ks[6], (na, D_INNER, D_MODEL), dout),
        "b_norm": 1.0 + nrm(ks[7], (nb, D_MODEL), 0.05),
        "b_w_in": nrm(ks[8], (nb, D_MODEL, 2 * D_INNER), din),
        "b_w_mix": nrm(ks[9], (nb, B_GROUPS, B_GROUP_DIM, B_GROUP_DIM), B_GROUP_DIM ** -0.5),
        "b_w_out": nrm(ks[10], (nb, D_INNER, D_MODEL), dout),
        "c_norm": 1.0 + nrm(ks[11], (nc, D_MODEL), 0.05),
        "c_w_in": nrm(ks[12], (nc, D_MODEL, 2 * D_INNER), din),
        "c_w_mix": nrm(ks[13], (nc, C_GROUPS, C_GROUP_DIM, C_GROUP_DIM), C_GROUP_DIM ** -0.5),
        "c_scale": 1.0 + nrm(ks[14], (nc, D_INNER), 0.1),
        "c_w_out": nrm(ks[15], (nc, D_INNER, D_MODEL), dout),
        "final_norm": 1.0 + nrm(ks[16], (D_MODEL,), 0.05),
    }

def first_block(x, a_norm, a_w_in, a_v_gain, a_w_s, a_b_s, a_w_out,
              b_norm, b_w_in, b_w_mix, b_w_out,
              c_norm, c_w_in, c_w_mix, c_scale, c_w_out, final_norm):
    for i in range(DEPTH):
        kind, j = i % N_MIXERS, i // N_MIXERS
        if kind == 0:
            h = rmsnorm(x, a_norm[j])
            y, gate = gmlp_mixer(h, a_w_in[j], a_v_gain[j], a_w_s[j], a_b_s[j])
            w_out = a_w_out[j]
        elif kind == 1:
            h = rmsnorm(x, b_norm[j])
            y, gate = fourier_mixer(h, b_w_in[j], b_w_mix[j])
            w_out = b_w_out[j]
        else:
            h = rmsnorm(x, c_norm[j])
            y, gate = pool_mixer(h, c_w_in[j], c_w_mix[j], c_scale[j])
            w_out = c_w_out[j]
        x = x + (y * jax.nn.silu(gate)) @ w_out
    return rmsnorm(x, final_norm)


FOX_HEADS = 8
FOX_HD = 128
FOX_WIDTH = FOX_HEADS * FOX_HD
Q_BLOCK = 128
MLSTM_HEADS = 4
MLSTM_DQK = 128
MLSTM_DV = 256
MLSTM_QK_WIDTH = MLSTM_HEADS * MLSTM_DQK
MLSTM_V_WIDTH = MLSTM_HEADS * MLSTM_DV
MLSTM_CHUNK = 64
D_FF = 5632
CONV_W = 3

OFF_FQ = 0
OFF_FK = OFF_FQ + FOX_WIDTH
OFF_FV = OFF_FK + FOX_WIDTH
OFF_FF = OFF_FV + FOX_WIDTH
OFF_MQ = OFF_FF + FOX_HEADS
OFF_MK = OFF_MQ + MLSTM_QK_WIDTH
OFF_MV = OFF_MK + MLSTM_QK_WIDTH
OFF_MO = OFF_MV + MLSTM_V_WIDTH
OFF_MI = OFF_MO + MLSTM_V_WIDTH
OFF_MF = OFF_MI + MLSTM_HEADS
OFF_GA = OFF_MF + MLSTM_HEADS
OFF_GM = OFF_GA + D_MODEL
D_IN = OFF_GM + D_MODEL


def rmsnorm_2(x, g):
    x32 = x.astype(jnp.float32)
    y = x32 * lax.rsqrt(jnp.mean(x32 * x32, axis=-1, keepdims=True) + EPS)
    return (y * g.astype(jnp.float32)).astype(x.dtype)

def forgetting_attention(q, k, v, log_f):
    B, S, H, D = q.shape
    F = jnp.cumsum(log_f, axis=1).transpose(0, 2, 1)
    scale = D ** -0.5
    outs = []
    for blk in range(S // Q_BLOCK):
        q0, q1 = blk * Q_BLOCK, (blk + 1) * Q_BLOCK
        qb = q[:, q0:q1].astype(jnp.float32)
        kb = k[:, :q1].astype(jnp.float32)
        vb = v[:, :q1]
        logits = jnp.einsum('bqhd,bkhd->bhqk', qb, kb) * scale
        logits = logits + F[:, :, q0:q1, None] - F[:, :, None, :q1]
        q_pos = q0 + jnp.arange(Q_BLOCK)
        k_pos = jnp.arange(q1)
        causal = k_pos[None, :] <= q_pos[:, None]
        logits = jnp.where(causal, logits, -jnp.inf)
        p = jax.nn.softmax(logits, axis=-1)
        outs.append(jnp.einsum('bhqk,bkhd->bqhd', p.astype(vb.dtype), vb))
    return jnp.concatenate(outs, axis=1)

def mlstm_chunkwise(q, k, v, i_pre, log_f):
    B, S, H, DK = q.shape
    DV = v.shape[-1]
    L = MLSTM_CHUNK
    NC = S // L
    f32 = jnp.float32

    def chunks(a):
        return a.astype(f32).reshape(B, NC, L, H, a.shape[-1]).transpose(1, 0, 3, 2, 4)

    def gchunks(a):
        return a.astype(f32).reshape(B, NC, L, H).transpose(1, 0, 3, 2)

    qc = chunks(q) * (DK ** -0.5)
    kc, vc = chunks(k), chunks(v)
    ic, fc = gchunks(i_pre), gchunks(log_f)
    causal = jnp.tril(jnp.ones((L, L), dtype=bool))

    def step(carry, inp):
        C, n, m = carry
        qt, kt, vt, it, ft = inp
        b = jnp.cumsum(ft, axis=-1)
        dlog = b[..., :, None] - b[..., None, :] + it[..., None, :]
        dlog = jnp.where(causal, dlog, -jnp.inf)
        inter = b + m[..., None]
        m_row = jnp.maximum(inter, dlog.max(axis=-1))
        s = jnp.einsum('bhtd,bhsd->bhts', qt, kt) * jnp.exp(dlog - m_row[..., None])
        inter_w = jnp.exp(inter - m_row)
        num = inter_w[..., None] * jnp.einsum('bhtd,bhde->bhte', qt, C) + jnp.einsum('bhts,bhse->bhte', s, vt)
        den = inter_w * jnp.einsum('bhtd,bhd->bht', qt, n) + s.sum(axis=-1)
        h = num / jnp.maximum(jnp.abs(den), jnp.exp(-m_row))[..., None]
        bL = b[..., -1]
        w_log = bL[..., None] - b + it
        m_new = jnp.maximum(bL + m, w_log.max(axis=-1))
        decay = jnp.exp(bL + m - m_new)
        ws = jnp.exp(w_log - m_new[..., None])
        C_new = decay[..., None, None] * C + jnp.einsum('bhs,bhsd,bhse->bhde', ws, kt, vt)
        n_new = decay[..., None] * n + jnp.einsum('bhs,bhsd->bhd', ws, kt)
        return (C_new, n_new, m_new), h

    init = (jnp.zeros((B, H, DK, DV), f32), jnp.zeros((B, H, DK), f32), jnp.zeros((B, H), f32))
    _, hs = lax.scan(step, init, (qc, kc, vc, ic, fc))
    return hs.transpose(1, 0, 3, 2, 4).reshape(B, S, H, DV).astype(v.dtype)

def causal_dwconv(u, w, b):
    S = u.shape[1]
    up = jnp.pad(u, ((0, 0), (CONV_W - 1, 0), (0, 0)))
    out = b
    for j in range(CONV_W):
        out = out + up[:, j:j + S] * w[j]
    return out

def second_inputs(seed: int = 0) -> dict:
    key = jax.random.key(seed)
    ks = jax.random.split(key, 20)
    nrm = lambda k, shape, s: jax.random.normal(k, shape, jnp.float32) * s
    L = DEPTH
    return {
        "x": nrm(ks[0], (BATCH, SEQ, D_MODEL), 1.0),
        "norm1_g": 1.0 + nrm(ks[1], (L, D_MODEL), 0.1),
        "w_in": nrm(ks[2], (L, D_MODEL, D_IN), D_MODEL ** -0.5),
        "fox_f_bias": jnp.linspace(1.0, 4.0, FOX_HEADS, dtype=jnp.float32)[None] + nrm(ks[3], (L, FOX_HEADS), 0.1),
        "q_norm_g": 1.0 + nrm(ks[4], (L, FOX_HD), 0.1),
        "k_norm_g": 1.0 + nrm(ks[5], (L, FOX_HD), 0.1),
        "m_i_bias": nrm(ks[6], (L, MLSTM_HEADS), 0.1),
        "m_f_bias": jnp.linspace(3.0, 6.0, MLSTM_HEADS, dtype=jnp.float32)[None] + nrm(ks[7], (L, MLSTM_HEADS), 0.1),
        "m_norm_g": 1.0 + nrm(ks[8], (L, MLSTM_HEADS, MLSTM_DV), 0.1),
        "w_proj_a": nrm(ks[9], (L, FOX_WIDTH, D_MODEL), FOX_WIDTH ** -0.5),
        "w_proj_m": nrm(ks[10], (L, MLSTM_V_WIDTH, D_MODEL), MLSTM_V_WIDTH ** -0.5),
        "w_out": nrm(ks[11], (L, D_MODEL, D_MODEL), D_MODEL ** -0.5),
        "norm2_g": 1.0 + nrm(ks[12], (L, D_MODEL), 0.1),
        "w_up": nrm(ks[13], (L, D_MODEL, 2 * D_FF), D_MODEL ** -0.5),
        "conv_w": nrm(ks[14], (L, CONV_W, 2 * D_FF), CONV_W ** -0.5),
        "conv_b": nrm(ks[15], (L, 2 * D_FF), 0.02),
        "w_down": nrm(ks[16], (L, D_FF, D_MODEL), D_FF ** -0.5),
    }

def second_block(x, norm1_g, w_in, fox_f_bias, q_norm_g, k_norm_g, m_i_bias, m_f_bias,
              m_norm_g, w_proj_a, w_proj_m, w_out, norm2_g, w_up, conv_w, conv_b, w_down):
    B, S, _ = x.shape

    for l in range(DEPTH):
        h = rmsnorm_2(x, norm1_g[l])
        z = jnp.einsum('bsd,de->bse', h, w_in[l])

        fq = rmsnorm_2(z[..., OFF_FQ:OFF_FK].reshape(B, S, FOX_HEADS, FOX_HD), q_norm_g[l])
        fk = rmsnorm_2(z[..., OFF_FK:OFF_FV].reshape(B, S, FOX_HEADS, FOX_HD), k_norm_g[l])
        fv = z[..., OFF_FV:OFF_FF].reshape(B, S, FOX_HEADS, FOX_HD)
        f_logf = jax.nn.log_sigmoid((z[..., OFF_FF:OFF_MQ] + fox_f_bias[l]).astype(jnp.float32))
        a_out = forgetting_attention(fq, fk, fv, f_logf).reshape(B, S, FOX_WIDTH)

        mq = z[..., OFF_MQ:OFF_MK].reshape(B, S, MLSTM_HEADS, MLSTM_DQK)
        mk = z[..., OFF_MK:OFF_MV].reshape(B, S, MLSTM_HEADS, MLSTM_DQK)
        mv = z[..., OFF_MV:OFF_MO].reshape(B, S, MLSTM_HEADS, MLSTM_DV)
        m_o = jax.nn.sigmoid(z[..., OFF_MO:OFF_MI]).reshape(B, S, MLSTM_HEADS, MLSTM_DV)
        m_ipre = (z[..., OFF_MI:OFF_MF] + m_i_bias[l]).astype(jnp.float32)
        m_logf = jax.nn.log_sigmoid((z[..., OFF_MF:OFF_GA] + m_f_bias[l]).astype(jnp.float32))
        hm = mlstm_chunkwise(mq, mk, mv, m_ipre, m_logf)
        m_out = (rmsnorm_2(hm, m_norm_g[l]) * m_o).reshape(B, S, MLSTM_V_WIDTH)

        g_a = jax.nn.sigmoid(z[..., OFF_GA:OFF_GM])
        g_m = jax.nn.sigmoid(z[..., OFF_GM:D_IN])
        merged = (g_a * jnp.einsum('bse,ed->bsd', a_out, w_proj_a[l])
                  + g_m * jnp.einsum('bse,ed->bsd', m_out, w_proj_m[l]))
        x = x + jnp.einsum('bsd,de->bse', merged, w_out[l])

        h2 = rmsnorm_2(x, norm2_g[l])
        u = causal_dwconv(jnp.einsum('bsd,df->bsf', h2, w_up[l]), conv_w[l], conv_b[l])
        u_gate, u_val = u[..., :D_FF], u[..., D_FF:]
        x = x + jnp.einsum('bsf,fd->bsd', jax.nn.silu(u_gate) * u_val, w_down[l])
    return x


def setup_inputs(seed=0):
    out = dict(first_inputs(seed))
    for name, value in second_inputs(seed + 1).items():
        if name != "x":
            out[name + "_2"] = value
    return out


def reference(
    x, a_norm, a_w_in, a_v_gain, a_w_s, a_b_s, a_w_out, b_norm, b_w_in, b_w_mix, b_w_out,
    c_norm, c_w_in, c_w_mix, c_scale, c_w_out, final_norm, norm1_g_2, w_in_2, fox_f_bias_2,
    q_norm_g_2, k_norm_g_2, m_i_bias_2, m_f_bias_2, m_norm_g_2, w_proj_a_2, w_proj_m_2, w_out_2,
    norm2_g_2, w_up_2, conv_w_2, conv_b_2, w_down_2,
):
    x = first_block(
        x, a_norm, a_w_in, a_v_gain, a_w_s, a_b_s, a_w_out, b_norm, b_w_in, b_w_mix, b_w_out,
        c_norm, c_w_in, c_w_mix, c_scale, c_w_out, final_norm,
    )
    return second_block(
        x, norm1_g_2, w_in_2, fox_f_bias_2, q_norm_g_2, k_norm_g_2, m_i_bias_2, m_f_bias_2,
        m_norm_g_2, w_proj_a_2, w_proj_m_2, w_out_2, norm2_g_2, w_up_2, conv_w_2, conv_b_2,
        w_down_2,
    )


_drawn_inputs = setup_inputs


def setup_inputs(seed=0):
    import zlib

    import numpy as np

    out = dict(_drawn_inputs(seed))
    spreads = {}
    factors = {'a_v_gain': 4.802,
     'q_norm_g_2': 3.874,
     'k_norm_g_2': 3.06,
     'm_i_bias_2': 64.0,
     'conv_b_2': 4.084}
    for name, (base, spread) in spreads.items():
        noise = np.random.default_rng([zlib.crc32(name.encode()), seed]).standard_normal(out[name].shape)
        drawn = base * np.exp(spread * noise) if base else spread * noise
        out[name] = __import__('jax').numpy.asarray(drawn.astype(out[name].dtype))
    for name, factor in factors.items():
        out[name] = (out[name] * factor).astype(out[name].dtype)
    return out
```

```python
import concourse.bass as bass
from concourse import mybir
import numpy as np

P = 128
S = 256
D = 2048
E = 4096
FF = 5632
KD, KE, KF = D // P, E // P, FF // P
GROUPS = 8
HEADS = 8
M_HEADS = 4
EPS = 1e-6
COLS = 512
ROWS_PER_CHUNK = 2
CHUNK = ROWS_PER_CHUNK * COLS
RING = 4

F32 = mybir.dt.float32
F32R = mybir.dt.float32r
ACT = mybir.ActivationFunctionType
ALU = mybir.AluOpType

FQ, FK, FV, FG, MQ, MK, MV, MO, MI, MF, GA, GM, END = (
    0, 1024, 2048, 3072, 3080, 3592, 4104, 5128, 6152, 6156, 6160, 8208, 10256)

PHASES = [
    ("v", 4, [8, 8]),
    ("ug", GROUPS, [8, 8]),
    ("out1", 2, [16, 16]),
    ("qk", 3, [8, 8]),
    ("vv", 2, [8, 8]),
    ("mo", 1, [8, 8]),
    ("merge", 4, [8, 8, 4, 4]),
    ("out2", 2, [8, 8]),
    ("up", FF // COLS, [8, 8]),
    ("down", 2, [22, 22]),
]
FIRST_CHUNK, FIRST_GROUP = {}, {}
_c = _g = 0
for _name, _turns, _counts in PHASES:
    FIRST_CHUNK[_name], FIRST_GROUP[_name] = _c, _g
    _c += _turns * sum(_counts)
    _g += _turns * len(_counts)
CHUNKS = _c
COUNTS = {name: counts for name, _, counts in PHASES}
TURNS = {name: turns for name, turns, _ in PHASES}

PARAMS = {}
_n = 0
for _name, _w in (("a_norm", KD), ("v_gain", KE), ("final_norm", KD), ("norm1", KD), ("norm2", KD),
                  ("conv0", 2 * KF), ("conv1", 2 * KF), ("conv2", 2 * KF), ("conv_b", 2 * KF),
                  ("q_norm", 1), ("k_norm", 1), ("m_norm", 2 * M_HEADS), ("gate_bias", 16)):
    PARAMS[_name] = (_n, _n + _w)
    _n += _w
N_PARAMS = _n


class Steps:

    def __init__(self, engine, sem):
        self.engine, self.sem, self.done, self.turn, self.per = engine, sem, 0, None, 0

    def enter(self, turn, per):
        self.turn, self.per, self.before = turn, per, self.done

    def leave(self, turns):
        assert self.done - self.before == self.per, (self.done - self.before, self.per)
        self.done = self.before + self.per * turns
        self.turn = None

    def link(self, instruction):
        instruction.then_inc(self.sem, 1)
        self.done += 1
        self.engine.wait_ge(self.sem, self.done if self.turn is None else self.turn * self.per + self.done)


def build(nc, x, stream, w_s, b_s, params, gate_w, consts, out):
    base = (nc.sbuf_base + 31) // 32 * 32
    kib = 1024
    at = {}
    where = base
    for region, size in (("ring", 48 * kib), ("h", 32 * kib), ("x", 16 * kib), ("y", 96 * kib),
                         ("mix", 8 * kib), ("small", 8 * kib - 160)):
        at[region] = where
        where += size
    assert where <= nc.sbuf_usable_end, (where, nc.sbuf_usable_end)

    def sb(name, region, offset, shape, dt=F32):
        return nc.alloc_sbuf_tensor_at(name, shape, dt, offset=at[region] + offset)

    raw = sb("raw", "ring", 0, [P, RING, CHUNK])
    w_hi = sb("w_hi", "ring", 16 * kib, [P, RING, CHUNK], F32R)
    w_lo = sb("w_lo", "ring", 32 * kib, [P, RING, CHUNK], F32R)
    h_hi = sb("h_hi", "h", 0, [P, KD, S], F32R)
    h_lo = sb("h_lo", "h", 16 * kib, [P, KD, S], F32R)
    xres = sb("xres", "x", 0, [P, KD, S])
    u_act = sb("u_act", "x", 0, [P, 4, S])
    t1 = sb("t1", "x", 4 * kib, [P, 4, S])
    t2 = sb("t2", "x", 8 * kib, [P, 4, S])
    v_group = sb("v_group", "x", 12 * kib, [P, 2, COLS])
    y_hi = sb("y_hi", "y", 0, [P, KE, S], F32R)
    y_lo = sb("y_lo", "y", 32 * kib, [P, KE, S], F32R)
    v_all = sb("v_all", "y", 64 * kib, [P, 2, E])
    ws_t = sb("ws_t", "mix", 0, [P, GROUPS, P])
    bs_b = sb("bs_b", "mix", 4 * kib, [P, GROUPS, P])
    sum_a = sb("sum_a", "y", 64 * kib, [P, 4, S])
    sum_b = sb("sum_b", "y", 68 * kib, [P, 4, S])
    sq_a = sb("sq_a", "y", 72 * kib, [P, 4, S])
    sq_b = sb("sq_b", "y", 76 * kib, [P, 4, S])
    norm_t = [sb("norm_t0", "y", 80 * kib, [P, 4, S]), sb("norm_t1", "y", 84 * kib, [P, 4, S])]
    qk = sb("qk", "y", 0, [P, 24, S])
    vv = sb("vv", "y", 24 * kib, [P, 2, 2 * 1024])
    mo = sb("mo", "y", 40 * kib, [P, 8, S])
    am_hi = sb("am_hi", "y", 64 * kib, [P, 16, S], F32R)
    am_lo = sb("am_lo", "y", 80 * kib, [P, 16, S], F32R)
    qsq = [sb(f"qsq{i}", "y", (64 + 4 * i) * kib, [P, 4 * S]) for i in range(2)]
    qms = [sb(f"qms{i}", "y", (72 + 4 * i) * kib, [P, 4 * S]) for i in range(2)]
    minus_half_wide = sb("minus_half_wide", "y", 80 * kib, [P, 4 * S])
    tmp = 48 * kib
    logits = sb("logits", "y", tmp, [P, 384])
    probs = sb("probs", "y", tmp + 1536, [P, 384])
    probs_t = sb("probs_t", "y", tmp + 3072, [P, 384])
    hm = sb("hm", "y", tmp + 4608, [P, 2 * S])
    hm_sq = sb("hm_sq", "y", tmp + 6656, [P, 2 * S])
    gz = sb("gz", "y", tmp + 8704, [P, 2, 16])
    gn = sb("gn", "y", tmp + 8832, [P, 2, 16])
    gl = sb("gl", "y", tmp + 8960, [P, 2, 16])
    gr = sb("gr", "y", tmp + 9088, [P, 2, 16])
    b_cum = sb("b_cum", "y", tmp + 9216, [P, 2, M_HEADS])
    col = sb("col", "y", tmp + 9280, [P, 16])
    gw_raw = sb("gw_raw", "mix", 0, [P, KD * 16])
    gw_hi = sb("gw_hi", "mix", kib, [P, KD, 16], F32R)
    gw_lo = sb("gw_lo", "mix", 2 * kib, [P, KD, 16], F32R)
    late = sb("late", "mix", 3 * kib, [P, 512])
    mask, ident, tri = late[:, 0:256], late[:, 256:384], late[:, 384:512]
    rows = sb("rows", "mix", 5 * kib, [16, S])
    row_of = sb("row_of", "mix", 6 * kib, [16, 12, 16])
    head_row = [sb(f"head_row{i}", "mix", (6 + i) * kib, [16, S]) for i in range(2)]
    g_hi = sb("g_hi", "y", 0, [P, KD, S], F32R)
    g_lo = sb("g_lo", "y", 16 * kib, [P, KD, S], F32R)
    gate_a = sb("gate_a", "y", 32 * kib, [P, 4, S])
    gate_m = sb("gate_m", "y", 36 * kib, [P, 4, S])
    f_hi = sb("f_hi", "y", 0, [P, KF, S], F32R)
    f_lo = sb("f_lo", "y", 44 * kib, [P, KF, S], F32R)
    cg = sb("cg", "y", 88 * kib, [P, 4, S])
    cv = sb("cv", "y", 92 * kib, [P, 4, S])
    silu_t = sb("silu_t", "mix", 0, [P, 4, S])
    par = sb("par", "small", 0, [P, N_PARAMS])
    off = (N_PARAMS * 4 + 31) // 32 * 32
    ones = sb("ones", "small", off, [P, P])
    minus_half = sb("minus_half", "small", off + 512, [P, S])
    ms = sb("ms", "small", off + 1536, [P, S])
    r1 = sb("r1", "small", off + 2560, [P, S])
    r2 = sb("r2", "small", off + 3584, [P, S])
    ws_scaled = sb("ws_scaled", "small", off + 4608, [P, 2, P])
    gains = sb("gains", "small", off + 5632, [P, KD])
    rv = sb("rv", "small", off + 5696, [P, 8])
    q_gain = sb("q_gain", "small", off + 5728, [P, 1])

    def param(name, k=0, n=1):
        a, b = PARAMS[name]
        return par[:, a + k:a + k + n] if isinstance(k, int) else par[:, bass.ds(k + a, n)]

    G = [nc.alloc_psum_tensor(f"g{i}", [P, 4 * S], F32) for i in range(2)]
    X = [nc.alloc_psum_tensor(f"x{i}", [P, COLS], F32) for i in range(2)]
    SV = nc.alloc_psum_tensor("sv", [P, 4, S], F32)

    class Sems:

        def __init__(self):
            self.made = {}

        def __getitem__(self, name):
            if name not in self.made:
                self.made[name] = nc.alloc_semaphore(name)
            return self.made[name]

    sem = Sems()
    raw_full = [sem[f"raw_full{i}"] for i in range(RING)]
    hi_ready, lo_ready, mm_done = sem["hi_ready"], sem["lo_ready"], sem["mm_done"]
    group_read = [sem["group_read0"], sem["group_read1"]]

    def chunk_of(phase, turn, k):
        return FIRST_CHUNK[phase] + k + turn * sum(COUNTS[phase])

    def group_of(phase, turn, k):
        return FIRST_GROUP[phase] + k + turn * len(COUNTS[phase])

    def group_waits(phase, turn, g):
        first = sum(COUNTS[phase][:g])
        end = chunk_of(phase, turn, first + COUNTS[phase][g])
        half = len(COUNTS[phase]) // 2
        read = FIRST_GROUP[phase] // 2 + g // 2 + 2 + turn * half
        return g % 2, end, read

    block = nc.Block()
    with block:

        @block.sync
        def _(sp):
            sp.dma_start(xres[:], x).then_inc(sem["x_in"], 16)
            sp.dma_start(par[:], params).then_inc(sem["params_in"], 16)
            for k in range(RING):
                sp.dma_start(raw[:, k, :], stream[k]).then_inc(raw_full[k], 16)
            sp.dma_start(ws_t[:], w_s).then_inc(sem["mix_in"], 16)
            sp.dma_start(bs_b[:], b_s).then_inc(sem["mix_in"], 16)
            with sp.Fori(0, CHUNKS // RING - 1) as i:
                for k in range(RING):
                    sp.wait_ge(lo_ready, i * RING + k + 1)
                    sp.dma_start(raw[:, k, :], stream[i * RING + (RING + k)]).then_inc(raw_full[k], 16)

        @block.tensor
        def _(pe):
            mm = nc.tensor.matmul

            def feature_chunk(buf, slot, a_hi, a_lo, k, last):
                for j in range(ROWS_PER_CHUNK):
                    kt = k * ROWS_PER_CHUNK + j
                    for b in range(4):
                        at_w = slice(j * COLS + b * P, j * COLS + (b + 1) * P)
                        to = G[buf][:, b * S:(b + 1) * S]
                        for n, (w, a) in enumerate(((w_hi, a_hi), (w_hi, a_lo), (w_lo, a_hi))):
                            ins = mm(to, w[:, slot, at_w], a[:, kt, :],
                                     start=(kt == 0 and n == 0 and b % 2 == 0),
                                     stop=(last and j == ROWS_PER_CHUNK - 1 and n == 2),
                                     skip_group_check=True)
                return ins

            def token_chunk(buf, slot, k, last):
                for j in range(ROWS_PER_CHUNK):
                    kt = k * ROWS_PER_CHUNK + j
                    at_w = slice(j * COLS, (j + 1) * COLS)
                    for t in range(2):
                        to = G[buf][:, t * COLS:(t + 1) * COLS]
                        at_t = slice(t * P, (t + 1) * P)
                        for n, (a, w) in enumerate(((h_hi, w_hi), (h_hi, w_lo), (h_lo, w_hi))):
                            ins = mm(to, a[:, kt, at_t], w[:, slot, at_w],
                                     start=(kt == 0 and n == 0),
                                     stop=(last and j == ROWS_PER_CHUNK - 1 and n == 2))
                return ins

            def group(phase, turn, g, chunk):
                buf, end, read = group_waits(phase, turn, g)
                n = COUNTS[phase][g]
                pe.wait_ge(group_read[buf], read - 1)
                for k in range(n):
                    pe.wait_ge(lo_ready, end + (k + 1 - n))
                    slot = (sum(COUNTS[phase][:g]) + k) % RING
                    if isinstance(turn, int):
                        slot = chunk_of(phase, turn, sum(COUNTS[phase][:g]) + k) % RING
                    chunk(buf, slot, k, k == n - 1).then_inc(mm_done, 1)

            def on(a_hi, a_lo, n_before=0):
                def chunk(buf, slot, k, last):
                    return feature_chunk(buf, slot, a_hi, a_lo, k, last)
                return chunk

            def on_new_h(quads_before):
                def chunk(buf, slot, k, last):
                    if k % 2 == 0:
                        pe.wait_ge(sem["h_lo_ready"], quads_before + k // 2 + 1)
                    return feature_chunk(buf, slot, h_hi, h_lo, k, last)
                return chunk

            def sums(to, parts):
                for b in range(4):
                    ins = mm(to, ones[:], parts[:, b, :], start=(b == 0), stop=(b == 3))
                return ins

            pe.wait_ge(sem["ones_ready"], 1)
            pe.wait_ge(sem["sums_ready"], 1)
            sums(X[0][:, 0:S], sum_a).then_inc(sem["stat_ready"], 1)

            def v_chunk(buf, slot, k, last):
                if k % 2 == 0:
                    pe.wait_ge(sem["h_lo_ready"], k // 2 + 1)
                return token_chunk(buf, slot, k, last)

            with pe.Fori(0, TURNS["v"]) as i:
                group("v", i, 0, v_chunk)
                group("v", i, 1, token_chunk)

            with pe.Fori(0, TURNS["ug"]) as i:
                group("ug", i, 0, on(h_hi, h_lo))
                pe.wait_ge(sem["ws_scaled"], i + 1)
                pe.wait_ge(sem["v_group_ready"], i + 1)
                for t in range(2):
                    for b in range(4):
                        ins = mm(SV[:, b, t * P:(t + 1) * P], v_group[:, t, b * P:(b + 1) * P],
                                 ws_scaled[:, t, :], start=True, stop=True)
                ins.then_inc(sem["sv_ready"], 1)
                group("ug", i, 1, on(h_hi, h_lo))

            pe.wait_ge(sem["y_lo_ready"], GROUPS)
            with pe.Fori(0, TURNS["out1"]) as i:
                group("out1", i, 0, on(y_hi, y_lo))
                group("out1", i, 1, on(y_hi, y_lo))
            pe.wait_ge(sem["sums_ready"], 2)
            sums(X[0][:, 0:S], sum_a).then_inc(sem["stat_ready"], 1)
            sums(X[1][:, 0:S], sum_b).then_inc(sem["stat_ready"], 1)

            with pe.Fori(0, TURNS["qk"]) as i:
                group("qk", i, 0, on_new_h(4))
                group("qk", i, 1, on(h_hi, h_lo))
            with pe.Fori(0, TURNS["vv"]) as i:
                group("vv", i, 0, token_chunk)
                group("vv", i, 1, token_chunk)
            with pe.Fori(0, TURNS["mo"]) as i:
                group("mo", i, 0, on(h_hi, h_lo))
                group("mo", i, 1, on(h_hi, h_lo))

            pe.wait_ge(sem["gw_ready"], 1)
            for t in range(2):
                to = X[0][:, t * 16:(t + 1) * 16]
                for kt in range(KD):
                    for n, (a, w) in enumerate(((h_hi, gw_hi), (h_hi, gw_lo), (h_lo, gw_hi))):
                        ins = mm(to, a[:, kt, t * P:(t + 1) * P], w[:, kt, :],
                                 start=(kt == 0 and n == 0), stop=(kt == KD - 1 and n == 2))
            ins.then_inc(sem["gz_ready"], 1)
            for n in range(4):
                pe.wait_ge(sem["qsq_ready"], n + 1)
                if n == 0:
                    pe.wait_ge(sem["gz_read"], 1)
                else:
                    pe.wait_ge(sem["qstat_read"], n)
                for half in range(2):
                    ins = mm(X[half][:], ones[:], qsq[n % 2][:, half * COLS:(half + 1) * COLS],
                             start=True, stop=True)
                ins.then_inc(sem["qstat_ready"], 1)
            pe.wait_ge(sem["gl_ready"], 1)
            pe.wait_ge(sem["qstat_read"], 4)
            mm(X[0][:, 0:12], tri, gl[:, 0, 0:12], start=True, stop=True)
            mm(X[0][:, 16:28], ones[:], gl[:, 0, 0:12], start=True, stop=False)
            mm(X[0][:, 16:28], tri, gl[:, 1, 0:12], start=False, stop=True).then_inc(sem["cum_ready"], 1)
            pe.wait_ge(sem["gr_ready"], 1)
            for t in range(2):
                ins = nc.tensor.transpose(X[1][0:16, t * P:(t + 1) * P], gr[:, t, :], ident)
            ins.then_inc(sem["rows_t_ready"], 1)

            def weigh(n):
                pe.wait_ge(sem["probs_ready"], n + 1)
                if n:
                    pe.wait_ge(sem["stat_m_read"] if n > HEADS else sem["probs_t_ready"],
                               n - HEADS if n > HEADS else n)
                for a, b in ((0, 0), (128, 128), (256, 256)):
                    ins = nc.tensor.transpose(PT[:, b:b + P], probs[:, a:a + P], ident)
                ins.then_inc(sem["probs_t_psum"], 1)

            PT = SV[:, 0:2, :].rearrange("p a b -> p (a b)")
            OUT = SV[:, 2:4, :].rearrange("p a b -> p (a b)")

            def scores(n):
                pe.wait_ge(sem["head_row_ready"], n + 1)
                r = head_row[n % 2]
                fox = n < HEADS
                q = qk[:, n, :] if fox else qk[:, 16 + n - HEADS, :]
                k = qk[:, 8 + n, :] if fox else qk[:, 20 + n - HEADS, :]
                if n:
                    pe.wait_ge(sem["scores_read"], n)
                for a, w, t in ((0, P, 0), (P, S, 1)):
                    to = X[0][:, a:a + w]
                    if fox:
                        mm(to, q[:, t * P:(t + 1) * P], k[:, 0:w], start=True, stop=False)
                    ins = mm(to, ones[0:16, :], r[:, 0:w], start=not fox, stop=True)
                    if not fox:
                        ins = mm(X[1][:, a:a + w], q[:, t * P:(t + 1) * P], k[:, 0:w], start=True, stop=True)
                ins.then_inc(sem["scores_ready"], 1)

            def values(n):
                pe.wait_ge(sem["probs_t_ready"], n + 1)
                fox = n < HEADS
                if 0 < n <= HEADS:
                    pe.wait_ge(sem["am_lo_ready"], n)
                elif n:
                    pe.wait_ge(sem["heads_read"], n - HEADS)
                for e in range(1 if fox else 2):
                    c = n * P if fox else 1024 + (n - HEADS) * S + e * P
                    mm(OUT[:, e * S:(e + 1) * S], vv[:, 0, c:c + P], probs_t[:, 0:S], start=True, stop=False)
                    ins = mm(OUT[:, e * S + P:(e + 1) * S], vv[:, 1, c:c + P], probs_t[:, S:S + P],
                             start=False, stop=True)
                ins.then_inc(sem["head_ready"], 1)

            pe.wait_ge(sem["qk_normed"], 4)
            scores(0)
            for n in range(HEADS + M_HEADS):
                if n + 1 < HEADS + M_HEADS:
                    scores(n + 1)
                weigh(n)
                values(n)
                if n >= HEADS:
                    pe.wait_ge(sem["hm_sq_ready"], n - HEADS + 1)
                    mm(PT[:, 0:S], ones[:], hm_sq[:, 0:S], start=True, stop=False)
                    mm(PT[:, 0:S], ones[:], hm_sq[:, S:2 * S], start=False, stop=True).then_inc(
                        sem["stat_m_ready"], 1)

            pe.wait_ge(sem["am_lo_ready"], HEADS + M_HEADS)
            with pe.Fori(0, TURNS["merge"]) as i:
                group("merge", i, 0, on(h_hi, h_lo))
                group("merge", i, 1, on(h_hi, h_lo))
                group("merge", i, 2, on(am_hi[:, 0:8, :], am_lo[:, 0:8, :]))
                group("merge", i, 3, on(am_hi[:, 8:16, :], am_lo[:, 8:16, :]))
            pe.wait_ge(sem["g_lo_ready"], 4)
            with pe.Fori(0, TURNS["out2"]) as i:
                group("out2", i, 0, on(g_hi, g_lo))
                group("out2", i, 1, on(g_hi, g_lo))
            pe.wait_ge(sem["sums_ready"], 3)
            sums(X[0][:, 0:S], sum_a).then_inc(sem["stat_ready"], 1)
            with pe.Fori(0, TURNS["up"]) as i:
                group("up", i, 0, on_new_h(8))
                group("up", i, 1, on(h_hi, h_lo))
            pe.wait_ge(sem["f_lo_ready"], TURNS["up"])
            for i in range(TURNS["down"]):
                group("down", i, 0, on(f_hi, f_lo))
                group("down", i, 1, on(f_hi, f_lo))

        @block.scalar
        def _(act):
            activation = nc.scalar.activation
            steps = Steps(act, sem["act_step"])

            def splits(phase, turn, g):
                first = sum(COUNTS[phase][:g])
                for k in range(COUNTS[phase][g]):
                    now = chunk_of(phase, turn, first + k)
                    slot = (FIRST_CHUNK[phase] + first + k + (turn * sum(COUNTS[phase]) if isinstance(turn, int) else 0)) % RING
                    if isinstance(now, int) and now + RING >= CHUNKS:
                        continue
                    split(slot, now)

            def split(slot, now):
                arrived = (now - slot) // RING + 2 if isinstance(now, int) else None
                if arrived is None:
                    phase_turn, const, per = now_parts[0]
                    arrived_at = phase_turn * (per // RING * 16) + ((const - slot) // RING + 2) * 16
                    act.wait_ge(raw_full[slot], arrived_at)
                else:
                    act.wait_ge(raw_full[slot], arrived * 16)
                act.wait_ge(mm_done, now + 1)
                activation(w_hi[:, slot, :], raw[:, slot, :], ACT.Copy).then_inc(hi_ready, 1)

            now_parts = [None]

            def splits_in_loop(phase, turn, g):
                first = sum(COUNTS[phase][:g])
                per = sum(COUNTS[phase])
                for k in range(COUNTS[phase][g]):
                    const = FIRST_CHUNK[phase] + first + k
                    now_parts[0] = (turn, const, per)
                    split(const % RING, turn * per + const)

            def done(phase, turn, g):
                buf, end, read = group_waits(phase, turn, g)
                act.wait_ge(mm_done, end)
                return G[buf], group_read[buf], read

            def split_high(to, of, count, **kw):
                activation(to, of, ACT.Copy, **kw).then_inc(sem[count], 1)

            def quads_high(before):
                for q in range(4):
                    act.wait_ge(sem["norm_ready"], before + q + 1)
                    split_high(h_hi[:, 4 * q:4 * q + 4, :], norm_t[q % 2][:], "h_hi_ready")

            act.wait_ge(sem["x_in"], 16)
            activation(sum_a[:], xres[:, 0:4, :], ACT.Square).then_inc(sem["sq_ready"], 1)
            for q in range(1, 4):
                to = (sq_a, sq_b, norm_t[0])[q - 1]
                activation(to[:], xres[:, 4 * q:4 * q + 4, :], ACT.Square).then_inc(sem["sq_ready"], 1)
            for k in range(RING):
                act.wait_ge(raw_full[k], 16)
                activation(w_hi[:, k, :], raw[:, k, :], ACT.Copy).then_inc(hi_ready, 1)
            quads_high(0)

            with act.Fori(0, TURNS["v"]) as i:
                for g in range(2):
                    splits_in_loop("v", i, g)
                    product, read, _ = done("v", i, g)
                    at_v = v_all[:, :, bass.ds(i * (2 * COLS) + g * COLS, COLS)]
                    activation(at_v, product[:].rearrange("p (t c) -> p t c", t=2),
                               ACT.Gelu_apprx_tanh).then_inc(read, 1)
            for buf in range(2):
                act.wait_ge(group_read[buf], 1 + TURNS["v"])
            activation(y_hi[:, 0:16, :], v_all[:, 0, :], ACT.Square,
                       accum_out=rv[:, 0:1]).then_inc(sem["v_sq_ready"], 1)

            with act.Fori(0, TURNS["ug"]) as i:
                splits_in_loop("ug", i, 0)
                product, read, _ = done("ug", i, 0)
                activation(u_act[:], product[:], ACT.Gelu_apprx_tanh).then_inc(read, 1)
                splits_in_loop("ug", i, 1)
                product, read, _ = done("ug", i, 1)
                activation(t2[:], product[:], ACT.Tanh, scale=0.5).then_inc(sem["gate_t_ready"], 1)
                act.wait_ge(sem["y_ready"], i + 1)
                split_high(y_hi[:, bass.ds(i * 4, 4), :], t1[:], "y_hi_ready")

            act.wait_ge(sem["y_lo_ready"], GROUPS)
            act.dma_start(xres[:], x).then_inc(sem["x_in"], 16)
            act.dma_start(gw_raw[:], gate_w).then_inc(sem["late_in"], 16)
            act.dma_start(late[:], consts).then_inc(sem["late_in"], 16)

            def squares(phase, turn, g, first, with_gain):
                buf, end, read = group_waits(phase, turn, g)
                act.wait_ge(group_read[buf], read)
                k0 = (turn * len(COUNTS[phase]) + g) * 4
                activation(sq_a[:], xres[:, bass.ds(k0, 4), :], ACT.Square).then_inc(sem["sq_ready"], 1)
                if with_gain:
                    for b in range(4):
                        ins = activation(sq_b[:, b, :], xres[:, bass.ds(k0 + b, 1), :].rearrange("p a s -> p (a s)"),
                                         ACT.Square, scale=param("final_norm", k0 + b))
                    ins.then_inc(sem["sq_ready"], 1)

            with act.Fori(0, TURNS["out1"]) as i:
                for g in range(2):
                    splits_in_loop("out1", i, g)
                    squares("out1", i, g, 0, True)
            quads_high(4)

            with act.Fori(0, TURNS["qk"]) as i:
                for g in range(2):
                    splits_in_loop("qk", i, g)
                    product, read, _ = done("qk", i, g)
                    activation(qk[:, bass.ds(i * 8 + 4 * g, 4), :], product[:], ACT.Copy).then_inc(read, 1)
            with act.Fori(0, TURNS["vv"]) as i:
                for g in range(2):
                    splits_in_loop("vv", i, g)
                    product, read, _ = done("vv", i, g)
                    activation(vv[:, :, bass.ds(i * (2 * COLS) + g * COLS, COLS)],
                               product[:].rearrange("p (t c) -> p t c", t=2), ACT.Copy).then_inc(read, 1)
            for g in range(2):
                splits("mo", 0, g)
                product, read, _ = done("mo", 0, g)
                activation(mo[:, 4 * g:4 * g + 4, :], product[:], ACT.Tanh, scale=0.5).then_inc(read, 1)

            act.wait_ge(sem["late_in"], 32)
            activation(gw_hi[:], gw_raw[:], ACT.Copy).then_inc(sem["gw_hi_ready"], 1)
            last_qk = FIRST_GROUP["qk"] // 2 + TURNS["qk"] + 1
            for buf in range(2):
                act.wait_ge(group_read[buf], last_qk)
            for n in range(4):
                if n >= 2:
                    act.wait_ge(sem["qstat_ready"], n - 1)
                at_q = qk[:, 4 * n:4 * n + 4, :]
                activation(qsq[n % 2][:], at_q, ACT.Square).then_inc(sem["qsq_ready"], 1)
            act.wait_ge(sem["gn_ready"], 1)
            steps.link(activation(gr[:], gn[:], ACT.Exp))
            activation(gl[:], gr[:], ACT.Ln, bias=1.0).then_inc(sem["ln_ready"], 1)
            act.wait_ge(sem["rows_t_ready"], 1)
            activation(rows[:], X[1][0:16, 0:S], ACT.Copy).then_inc(sem["rows_ready"], 1)

            PT = SV[:, 0:2, :].rearrange("p a b -> p (a b)")
            OUT = SV[:, 2:4, :].rearrange("p a b -> p (a b)")
            for n in range(HEADS + M_HEADS):
                fox = n < HEADS
                act.wait_ge(sem["max_ready"], n + 1)
                for a, w, t in ((0, P, 0), (P, S, 1)):
                    ins = activation(probs[:, a:a + w], logits[:, a:a + w], ACT.Exp, bias=col[:, 2 + t:3 + t],
                                     accum_out=col[:, 4 + t:5 + t] if fox else None)
                if not fox:
                    ins = activation(col[:, 6:8], col[:, 8:10], ACT.Exp)
                ins.then_inc(sem["exp_ready"], 1)
                act.wait_ge(sem["probs_t_psum"], n + 1)
                if n:
                    act.wait_ge(sem["head_ready"], n)
                activation(probs_t[:], PT[:, 0:384], ACT.Copy).then_inc(sem["probs_t_ready"], 1)
                act.wait_ge(sem["head_ready"], n + 1)
                if fox:
                    activation(am_hi[:, n, :], OUT[:, 0:S], ACT.Copy).then_inc(sem["am_hi_ready"], 1)
                else:
                    m = n - HEADS
                    activation(hm_sq[:], OUT[:], ACT.Square).then_inc(sem["hm_sq_ready"], 1)
                    act.wait_ge(sem["hm_ready"], m + 1)
                    activation(am_hi[:, 8 + 2 * m:10 + 2 * m, :], hm[:], ACT.Copy).then_inc(sem["am_hi_ready"], 1)

            with act.Fori(0, TURNS["merge"]) as i:
                for g, to in ((0, gate_a), (1, gate_m)):
                    splits_in_loop("merge", i, g)
                    product, read, _ = done("merge", i, g)
                    activation(to[:], product[:], ACT.Tanh, scale=0.5).then_inc(read, 1)
                splits_in_loop("merge", i, 2)
                splits_in_loop("merge", i, 3)
                act.wait_ge(sem["merged_ready"], i + 1)
                split_high(g_hi[:, bass.ds(i * 4, 4), :], gate_a[:], "g_hi_ready", scale=0.5)
            with act.Fori(0, TURNS["out2"]) as i:
                for g in range(2):
                    splits_in_loop("out2", i, g)
                    squares("out2", i, g, 0, False)
            quads_high(8)

            def conv_start(product, to, k0, half):
                for b in range(4):
                    ins = activation(to[:, b, :], product[:, b * S:(b + 1) * S], ACT.Identity,
                                     scale=param("conv2", k0 + b + half), bias=param("conv_b", k0 + b + half))
                return ins

            with act.Fori(0, TURNS["up"]) as i:
                splits_in_loop("up", i, 0)
                product, _, _ = done("up", i, 0)
                conv_start(product, cg, i * 4, 0).then_inc(sem["conv_g_started"], 1)
                act.wait_ge(group_read[0], group_waits("up", i, 0)[2])
                activation(silu_t[:], cg[:], ACT.Tanh, scale=0.5).then_inc(sem["silu_t_ready"], 1)
                splits_in_loop("up", i, 1)
                product, _, _ = done("up", i, 1)
                conv_start(product, cv, i * 4, KF).then_inc(sem["conv_v_started"], 1)
                act.wait_ge(sem["f_ready"], i + 1)
                split_high(f_hi[:, bass.ds(i * 4, 4), :], cv[:], "f_hi_ready")
            for i in range(TURNS["down"]):
                splits("down", i, 0)
                splits("down", i, 1)

        @block.vector
        def _(dve):
            v = nc.vector
            steps = Steps(dve, sem["dve_step"])
            link = steps.link

            def split(slot, count):
                dve.wait_ge(hi_ready, count)
                v.tensor_tensor(w_lo[:, slot, :], raw[:, slot, :], w_hi[:, slot, :].bitcast(F32),
                                ALU.subtract).then_inc(lo_ready, 1)

            def splits(phase, turn, g):
                first = sum(COUNTS[phase][:g])
                for k in range(COUNTS[phase][g]):
                    now = chunk_of(phase, turn, first + k)
                    const = FIRST_CHUNK[phase] + first + k
                    if isinstance(now, int):
                        if now + RING >= CHUNKS:
                            continue
                        const = now
                    split(const % RING, now + RING + 1)

            def done(phase, turn, g):
                buf, end, read = group_waits(phase, turn, g)
                dve.wait_ge(mm_done, end)
                return G[buf], group_read[buf], read

            def rest(to, of, hi, count, value, after):
                dve.wait_ge(sem[count], value)
                v.tensor_tensor(to, of, hi.bitcast(F32), ALU.subtract).then_inc(sem[after], 1)

            def mean_square(to, of, n):
                return v.tensor_scalar(to, of, 1.0 / n, EPS, ALU.mult, ALU.add)

            def normalise(before, gain, scale):
                for q in range(5):
                    if q < 4:
                        if q >= 2:
                            dve.wait_ge(sem["h_lo_ready"], before + q - 1)
                        for b in range(4):
                            k = 4 * q + b
                            ins = v.scalar_tensor_tensor(norm_t[q % 2][:, b, :], xres[:, k, :], gain(k), scale[:],
                                                         ALU.mult, ALU.mult)
                        ins.then_inc(sem["norm_ready"], 1)
                    if q:
                        p = q - 1
                        rest(h_lo[:, 4 * p:4 * p + 4, :], norm_t[p % 2][:], h_hi[:, 4 * p:4 * p + 4, :],
                             "h_hi_ready", before + p + 1, "h_lo_ready")

            v.memset(ones[:], 1.0).then_inc(sem["ones_ready"], 1)
            v.memset(minus_half[:], -0.5).then_inc(sem["minus_half_ready"], 1)
            for buf in range(2):
                dve.sem_inc(group_read[buf], 1)

            for q in range(1, 4):
                dve.wait_ge(sem["sq_ready"], q + 1)
                of = (sq_a, sq_b, norm_t[0])[q - 1]
                ins = v.tensor_tensor(sum_a[:], sum_a[:], of[:], ALU.add)
                if q < 3:
                    link(ins)
            ins.then_inc(sem["sums_ready"], 1)
            for k in range(RING):
                split(k, k + 1)
            dve.wait_ge(sem["stat_ready"], 1)
            mean_square(ms[:], X[0][:, 0:S], D).then_inc(sem["ms_ready"], 1)
            dve.wait_ge(sem["params_in"], 16)
            dve.wait_ge(sem["rstd_ready"], 1)
            normalise(0, lambda k: param("a_norm", k), r1)

            with dve.Fori(0, TURNS["v"]) as i:
                splits("v", i, 0)
                splits("v", i, 1)
            for buf in range(2):
                dve.wait_ge(group_read[buf], 1 + TURNS["v"])
            link(v.tensor_tensor_reduce(y_lo[:, 0:16, :].rearrange("p a b -> p (a b)"), v_all[:, 1, :], v_all[:, 1, :],
                                        scale=1.0, scalar=0.0,
                                        op0=ALU.mult, op1=ALU.add, accum_out=rv[:, 1:2]))
            dve.wait_ge(sem["v_sq_ready"], 1)
            mean_square(rv[:, 2:4], rv[:, 0:2], E).then_inc(sem["ms_ready"], 1)
            dve.wait_ge(sem["rstd_ready"], 2)
            dve.wait_ge(sem["mix_in"], 32)

            with dve.Fori(0, TURNS["ug"]) as i:
                steps.enter(i, 2)
                for t in range(2):
                    ins = v.tensor_scalar(ws_scaled[:, t, :], ws_t[:, bass.ds(i, 1), :].rearrange("p a b -> p (a b)"),
                                          rv[:, 4 + t:5 + t], None, ALU.mult)
                ins.then_inc(sem["ws_scaled"], 1)
                splits("ug", i, 0)
                splits("ug", i, 1)
                dve.wait_ge(sem["sv_ready"], i + 1)
                bias = bs_b[:, bass.ds(i, 1), :].rearrange("p a b -> p (a b)")
                for b in range(4):
                    for t in range(2):
                        ins = v.scalar_tensor_tensor(t1[:, b, t * P:(t + 1) * P], SV[:, b, t * P:(t + 1) * P],
                                                     param("v_gain", i * 4 + b), bias, ALU.mult, ALU.add)
                link(ins)
                _, _, read = group_waits("ug", i, 0)
                dve.wait_ge(group_read[0], read)
                link(v.tensor_tensor(t1[:], t1[:], u_act[:], ALU.mult))
                product, gate_read, read = done("ug", i, 1)
                dve.wait_ge(sem["gate_t_ready"], i + 1)
                v.scalar_tensor_tensor(t2[:].rearrange("p a b -> p (a b)"), t2[:].rearrange("p a b -> p (a b)"), 1.0,
                                       product[:], ALU.add, ALU.mult).then_inc(gate_read, 1)
                dve.wait_ge(gate_read, read)
                v.scalar_tensor_tensor(t1[:], t1[:], 0.5, t2[:], ALU.mult, ALU.mult).then_inc(sem["y_ready"], 1)
                rest(y_lo[:, bass.ds(i * 4, 4), :], t1[:], y_hi[:, bass.ds(i * 4, 4), :], "y_hi_ready", i + 1,
                     "y_lo_ready")
                dve.wait_ge(sem["y_lo_ready"], i + 1)
                steps.leave(TURNS["ug"])

            def residual(phase, turn, g, n_sq, sq_before, accs):
                product, read, value = done(phase, turn, g)
                k0 = (turn * len(COUNTS[phase]) + g) * 4
                at_x = xres[:, bass.ds(k0, 4), :]
                v.tensor_tensor(at_x, product[:].rearrange("p (b s) -> p b s", b=4), at_x, ALU.add).then_inc(read, 1)
                for n, (acc, of) in enumerate(accs):
                    dve.wait_ge(sem["sq_ready"], (turn * len(COUNTS[phase]) + g) * n_sq + (sq_before + n + 1))
                    link(v.tensor_tensor(acc[:], acc[:], of[:], ALU.add))

            for acc in (sum_a, sum_b):
                link(v.memset(acc[:], 0.0))
            link(v.tensor_tensor(gains[:], param("final_norm", 0, KD), param("norm1", 0, KD), ALU.mult))
            dve.wait_ge(sem["x_in"], 32)
            with dve.Fori(0, TURNS["out1"]) as i:
                steps.enter(i, 4)
                for g in range(2):
                    splits("out1", i, g)
                    residual("out1", i, g, 2, 4, ((sum_a, sq_a), (sum_b, sq_b)))
                steps.leave(TURNS["out1"])
            dve.sem_inc(sem["sums_ready"], 1)
            dve.wait_ge(sem["stat_ready"], 2)
            mean_square(ms[:], X[0][:, 0:S], D).then_inc(sem["ms_ready"], 1)
            dve.wait_ge(sem["rstd_ready"], 3)
            link(v.tensor_tensor(r2[:], r1[:], r1[:], ALU.mult))
            dve.wait_ge(sem["stat_ready"], 3)
            link(v.scalar_tensor_tensor(ms[:], X[1][:, 0:S], 1.0 / D, r2[:], ALU.mult, ALU.mult))
            v.tensor_scalar(ms[:], ms[:], EPS, None, ALU.add).then_inc(sem["ms_ready"], 1)
            dve.wait_ge(sem["rstd_ready"], 4)
            link(v.tensor_tensor(ms[:], r1[:], r2[:], ALU.mult))
            normalise(4, lambda k: gains[:, k:k + 1], ms)
            for k in range(KD):
                ins = v.scalar_tensor_tensor(xres[:, k, :], xres[:, k, :], param("final_norm", k), r1[:],
                                             ALU.mult, ALU.mult)
            link(ins)

            with dve.Fori(0, TURNS["qk"]) as i:
                splits("qk", i, 0)
                splits("qk", i, 1)
            with dve.Fori(0, TURNS["vv"]) as i:
                splits("vv", i, 0)
                splits("vv", i, 1)
            for g in range(2):
                splits("mo", 0, g)

            rest(gw_lo[:].rearrange("p a b -> p (a b)"), gw_raw[:], gw_hi[:].rearrange("p a b -> p (a b)"),
                 "gw_hi_ready", 1, "gw_ready")
            link(v.tensor_scalar(q_gain[:], param("q_norm"), float(P) ** -0.5, None, ALU.mult))
            v.memset(minus_half_wide[:], -0.5).then_inc(sem["minus_half_ready"], 1)
            dve.wait_ge(sem["gz_ready"], 1)
            bias = param("gate_bias", 0, 16)
            for t in range(2):
                ins = v.tensor_tensor(gz[:, t, :], X[0][:, t * 16:(t + 1) * 16], bias, ALU.add)
            ins.then_inc(sem["gz_read"], 1)
            dve.wait_ge(sem["gz_read"], 1)
            v.scalar_tensor_tensor(gn[:], gz[:], -1.0, gz[:], ALU.mult, ALU.min).then_inc(sem["gn_ready"], 1)
            for n in range(5):
                if n < 4:
                    dve.wait_ge(sem["qstat_ready"], n + 1)
                    if n >= 2:
                        dve.wait_ge(sem["qk_normed"], n - 1)
                    for half in range(2):
                        ins = mean_square(qms[n % 2][:, half * COLS:(half + 1) * COLS], X[half][:], P)
                    ins.then_inc(sem["qstat_read"], 1)
                if n:
                    p = n - 1
                    dve.wait_ge(sem["q_rstd_ready"], p + 1)
                    at_q = qk[:, 4 * p:4 * p + 4, :].rearrange("p a b -> p (a b)")
                    gain = q_gain[:, 0:1] if p < 2 else param("k_norm")
                    v.scalar_tensor_tensor(at_q, at_q, gain, qms[p % 2][:], ALU.mult, ALU.mult).then_inc(
                        sem["qk_normed"], 1)
            dve.wait_ge(sem["ln_ready"], 1)
            v.scalar_tensor_tensor(gl[:], gz[:], 0.0, gl[:], ALU.min, ALU.subtract).then_inc(sem["gl_ready"], 1)
            dve.wait_ge(sem["cum_ready"], 1)
            cum = X[0][:, 0:32].rearrange("p (t c) -> p t c", t=2)
            v.tensor_scalar(gr[:, :, 0:8], cum[:, :, 0:8], -1.0, None, ALU.mult)
            v.tensor_copy(b_cum[:], cum[:, :, 8:12])
            v.tensor_copy(gr[:, :, 12:16], gz[:, :, 12:16])
            v.tensor_tensor(gr[:, :, 8:12], gz[:, :, 12:16], cum[:, :, 8:12], ALU.subtract).then_inc(sem["gr_ready"], 1)

            def row(n):
                v.tensor_scalar(head_row[n % 2][:], rows[:], ident[0:16, n:n + 1], None, ALU.mult).then_inc(
                    sem["head_row_ready"], 1)

            dve.wait_ge(sem["rows_ready"], 1)
            row(0)
            row(1)
            OUT = SV[:, 2:4, :].rearrange("p a b -> p (a b)")
            PT = SV[:, 0:2, :].rearrange("p a b -> p (a b)")
            for n in range(HEADS + M_HEADS):
                fox = n < HEADS
                dve.wait_ge(sem["scores_ready"], n + 1)
                for a, w, t in ((0, P, 0), (P, S, 1)):
                    ins = v.tensor_tensor_reduce(logits[:, a:a + w], X[0][:, a:a + w], mask[:, S - w:S],
                                                 scale=1.0, scalar=-3e38, op0=ALU.add, op1=ALU.max,
                                                 accum_out=col[:, t:t + 1])
                if fox:
                    ins.then_inc(sem["scores_read"], 1)
                    dve.wait_ge(sem["scores_read"], n + 1)
                    v.tensor_scalar(col[:, 2:4], col[:, 0:2], -1.0, None, ALU.mult).then_inc(sem["max_ready"], 1)
                    dve.wait_ge(sem["exp_ready"], n + 1)
                    link(v.reciprocal(col[:, 10:12], col[:, 4:6]))
                else:
                    link(ins)
                    link(v.tensor_scalar(col[:, 2:4], col[:, 0:2], -1.0, 0.0, ALU.mult, ALU.min))
                    m = n - HEADS
                    v.tensor_tensor(col[:, 8:10], col[:, 2:4], b_cum[:, :, m], ALU.subtract).then_inc(
                        sem["max_ready"], 1)
                    dve.wait_ge(sem["exp_ready"], n + 1)
                    for a, w, t in ((0, P, 0), (P, S, 1)):
                        ins = v.tensor_tensor_reduce(probs[:, a:a + w], X[1][:, a:a + w], probs[:, a:a + w],
                                                     scale=float(P) ** -0.5, scalar=0.0, op0=ALU.mult, op1=ALU.add,
                                                     accum_out=col[:, 4 + t:5 + t])
                    ins.then_inc(sem["scores_read"], 1)
                    dve.wait_ge(sem["scores_read"], n + 1)
                    link(v.scalar_tensor_tensor(col[:, 0:2], col[:, 4:6], -1.0, col[:, 4:6], ALU.mult, ALU.max))
                    link(v.tensor_tensor(col[:, 0:2], col[:, 0:2], col[:, 6:8], ALU.max))
                    link(v.reciprocal(col[:, 10:12], col[:, 0:2]))
                for a, w, t in ((0, P, 0), (P, S, 1)):
                    ins = v.tensor_scalar(probs[:, a:a + w], probs[:, a:a + w], col[:, 10 + t:11 + t], None, ALU.mult)
                ins.then_inc(sem["probs_ready"], 1)
                if n + 2 < HEADS + M_HEADS:
                    row(n + 2)
                if fox:
                    dve.wait_ge(sem["head_ready"], n + 1)
                    dve.wait_ge(sem["am_hi_ready"], n + 1)
                    v.tensor_tensor(am_lo[:, n, :], OUT[:, 0:S], am_hi[:, n, :].bitcast(F32),
                                    ALU.subtract).then_inc(sem["am_lo_ready"], 1)
                else:
                    m = n - HEADS
                    dve.wait_ge(sem["stat_m_ready"], m + 1)
                    mean_square(ms[:], PT[:, 0:S], 2 * P).then_inc(sem["stat_m_read"], 1)
                    dve.wait_ge(sem["m_rstd_ready"], m + 1)
                    dve.wait_ge(sem["am_lo_ready"], n)
                    for e in range(2):
                        ins = v.scalar_tensor_tensor(hm[:, e * S:(e + 1) * S], OUT[:, e * S:(e + 1) * S],
                                                     param("m_norm", 2 * m + e), r2[:], ALU.mult, ALU.mult)
                    ins.then_inc(sem["heads_read"], 1)
                    dve.wait_ge(sem["heads_read"], m + 1)
                    gate = mo[:, 2 * m:2 * m + 2, :].rearrange("p a b -> p (a b)")
                    link(v.scalar_tensor_tensor(hm[:], gate, 1.0, hm[:], ALU.add, ALU.mult))
                    v.tensor_scalar(hm[:], hm[:], 0.5, None, ALU.mult).then_inc(sem["hm_ready"], 1)
                    rest(am_lo[:, 8 + 2 * m:10 + 2 * m, :].rearrange("p a b -> p (a b)"), hm[:],
                         am_hi[:, 8 + 2 * m:10 + 2 * m, :].rearrange("p a b -> p (a b)"), "am_hi_ready", n + 1,
                         "am_lo_ready")

            with dve.Fori(0, TURNS["merge"]) as i:
                splits("merge", i, 0)
                splits("merge", i, 1)
                for g, gate in ((2, gate_a), (3, gate_m)):
                    splits("merge", i, g)
                    buf, _, read = group_waits("merge", i, g - 2)
                    dve.wait_ge(group_read[buf], read)
                    product, projected_read, read = done("merge", i, g)
                    flat = gate[:].rearrange("p a b -> p (a b)")
                    v.scalar_tensor_tensor(flat, flat, 1.0, product[:], ALU.add, ALU.mult).then_inc(projected_read, 1)
                    dve.wait_ge(projected_read, read)
                v.tensor_tensor(gate_a[:], gate_a[:], gate_m[:], ALU.add).then_inc(sem["merged_ready"], 1)
                dve.wait_ge(sem["g_hi_ready"], i + 1)
                at_g = bass.ds(i * 4, 4)
                v.scalar_tensor_tensor(g_lo[:, at_g, :], gate_a[:], 0.5, g_hi[:, at_g, :].bitcast(F32),
                                       ALU.mult, ALU.subtract).then_inc(sem["g_lo_ready"], 1)

            link(v.memset(sum_a[:], 0.0))
            with dve.Fori(0, TURNS["out2"]) as i:
                steps.enter(i, 2)
                for g in range(2):
                    splits("out2", i, g)
                    residual("out2", i, g, 1, 12, ((sum_a, sq_a),))
                steps.leave(TURNS["out2"])
            dve.sem_inc(sem["sums_ready"], 1)
            dve.wait_ge(sem["stat_ready"], 4)
            mean_square(ms[:], X[0][:, 0:S], D).then_inc(sem["ms_ready"], 1)
            dve.wait_ge(sem["rstd_ready"], 5)
            normalise(8, lambda k: param("norm2", k), r1)

            def conv_taps(product, to, k0, half):
                for tap, late_by in (("conv1", 1), ("conv0", 2)):
                    for b in range(4):
                        ins = v.scalar_tensor_tensor(to[:, b, late_by:S], product[:, b * S:(b + 1) * S - late_by],
                                                     param(tap, k0 + b + half), to[:, b, late_by:S],
                                                     ALU.mult, ALU.add)
                    if late_by == 1:
                        link(ins)
                return ins

            with dve.Fori(0, TURNS["up"]) as i:
                steps.enter(i, 3)
                splits("up", i, 0)
                product, read, value = done("up", i, 0)
                dve.wait_ge(sem["conv_g_started"], i + 1)
                conv_taps(product, cg, i * 4, 0).then_inc(read, 1)
                dve.wait_ge(read, value)
                dve.wait_ge(sem["silu_t_ready"], i + 1)
                link(v.scalar_tensor_tensor(cg[:], silu_t[:], 1.0, cg[:], ALU.add, ALU.mult))
                splits("up", i, 1)
                product, read, value = done("up", i, 1)
                dve.wait_ge(sem["conv_v_started"], i + 1)
                conv_taps(product, cv, i * 4, KF).then_inc(read, 1)
                dve.wait_ge(read, value)
                v.scalar_tensor_tensor(cv[:], cv[:], 0.5, cg[:], ALU.mult, ALU.mult).then_inc(sem["f_ready"], 1)
                rest(f_lo[:, bass.ds(i * 4, 4), :], cv[:], f_hi[:, bass.ds(i * 4, 4), :], "f_hi_ready", i + 1,
                     "f_lo_ready")
                steps.leave(TURNS["up"])

            for i in range(TURNS["down"]):
                for g in range(2):
                    splits("down", i, g)
                    product, read, value = done("down", i, g)
                    k0 = (2 * i + g) * 4
                    at_x = xres[:, k0:k0 + 4, :]
                    v.tensor_tensor(at_x, product[:].rearrange("p (b s) -> p b s", b=4), at_x, ALU.add).then_inc(read, 1)

        @block.gpsimd
        def _(pool):
            p = nc.gpsimd

            def rstd(to, of, minus_half, count, after):
                pool.wait_ge(sem["ms_ready"] if after == "rstd_ready" else sem[count[0]], count[1])
                p.tensor_tensor(to, of, minus_half, ALU.pow).then_inc(sem[after], 1)

            pool.wait_ge(sem["minus_half_ready"], 1)
            rstd(r1[:], ms[:], minus_half[:], (None, 1), "rstd_ready")
            rstd(rv[:, 4:6], rv[:, 2:4], minus_half[:, 0:2], (None, 2), "rstd_ready")
            p.tensor_copy(v_group[:], v_all[:, :, 0:COLS]).then_inc(sem["v_group_ready"], 1)
            with pool.Fori(1, GROUPS) as i:
                pool.wait_ge(sem["sv_ready"], i)
                p.tensor_copy(v_group[:], v_all[:, :, bass.ds(i * COLS, COLS)]).then_inc(sem["v_group_ready"], 1)
            rstd(r1[:], ms[:], minus_half[:], (None, 3), "rstd_ready")
            rstd(r2[:], ms[:], minus_half[:], (None, 4), "rstd_ready")
            pool.wait_ge(sem["minus_half_ready"], 2)
            for n in range(4):
                rstd(qms[n % 2][:], qms[n % 2][:], minus_half_wide[:], ("qstat_read", n + 1), "q_rstd_ready")
            for m in range(M_HEADS):
                rstd(r2[:], ms[:], minus_half[:], ("stat_m_read", m + 1), "m_rstd_ready")
            rstd(r1[:], ms[:], minus_half[:], (None, 5), "rstd_ready")
            for q in range(4):
                buf, _, read = group_waits("down", q // 2, q % 2)
                pool.wait_ge(group_read[buf], read)
                p.dma_start(out[:, 4 * q:4 * q + 4, :], xres[:, 4 * q:4 * q + 4, :]).then_inc(sem["stored"], 16)
            pool.wait_ge(sem["stored"], 64)


def chunks_of(w):
    k, n = w.shape
    w = w.reshape(k // CHUNK_ROWS, ROWS_PER_CHUNK, P, n // COLS, COLS)
    return np.ascontiguousarray(w.transpose(3, 0, 2, 1, 4)).reshape(n // COLS, k // CHUNK_ROWS, P, CHUNK)


CHUNK_ROWS = ROWS_PER_CHUNK * P


def feature_major(a):
    return np.ascontiguousarray(a.T.reshape(-1, P, a.shape[0]).transpose(1, 0, 2))


def lay_out(i):
    w_in, w2, w_up = i["a_w_in"][0], i["w_in_2"][0], i["w_up_2"][0]
    u, v, gate = (chunks_of(w_in[:, k * E:(k + 1) * E]) for k in range(3))
    qk = [chunks_of(w2[:, a:b]) for a, b in ((FQ, FV), (MQ, MV))]
    vv = [chunks_of(w2[:, a:b]) for a, b in ((FV, FG), (MV, MO))]
    ga, gm = chunks_of(w2[:, GA:GM]), chunks_of(w2[:, GM:END])
    pa, pm = chunks_of(i["w_proj_a_2"][0]), chunks_of(i["w_proj_m_2"][0])
    up_g, up_v = chunks_of(w_up[:, :FF]), chunks_of(w_up[:, FF:])
    parts = [v]
    for g in range(GROUPS):
        parts += [u[g], gate[g]]
    parts += [chunks_of(i["a_w_out"][0])] + qk + vv + [chunks_of(w2[:, MO:MI])]
    for g in range(4):
        parts += [ga[g], gm[g], pa[g], pm[g]]
    parts += [chunks_of(i["w_out_2"][0])]
    for g in range(FF // COLS):
        parts += [up_g[g], up_v[g]]
    parts += [chunks_of(i["w_down_2"][0])]
    stream = np.concatenate([a.reshape(-1, P, CHUNK) for a in parts])
    assert stream.shape[0] == CHUNKS

    def cols(a):
        return a.reshape(-1, P).T

    conv = i["conv_w_2"][0]
    bias = np.concatenate([i["fox_f_bias_2"][0], i["m_f_bias_2"][0], i["m_i_bias_2"][0]])
    params = np.concatenate([
        cols(i["a_norm"][0]), cols(i["a_v_gain"][0]), cols(i["final_norm"]), cols(i["norm1_g_2"][0]),
        cols(i["norm2_g_2"][0]), cols(conv[0]), cols(conv[1]), cols(conv[2]), cols(i["conv_b_2"][0]),
        cols(i["q_norm_g_2"][0]), cols(i["k_norm_g_2"][0]), cols(i["m_norm_g_2"][0].reshape(-1)),
        np.broadcast_to(bias, (P, 16))], axis=1)
    w_gates = np.concatenate([w2[:, FG:MQ], w2[:, MF:GA], w2[:, MI:MF]], axis=1)
    gate_w = w_gates.reshape(KD, P, 16).transpose(1, 0, 2).reshape(P, KD * 16)
    t, s = np.arange(P)[:, None], np.arange(P)[None, :]
    consts = np.concatenate([np.zeros((P, P)), np.where(s > t, -1e30, 0.0), np.eye(P), np.where(t <= s, 1.0, 0.0)],
                            axis=1).astype(np.float32)
    return {
        "x": feature_major(i["x"][0]),
        "stream": stream,
        "w_s": i["a_w_s"][0].transpose(2, 0, 1),
        "b_s": np.broadcast_to(i["a_b_s"][0], (P, GROUPS, P)),
        "params": params,
        "gate_w": gate_w,
        "consts": consts,
    }


def kernel(**inputs):
    import concourse.bacc as bacc
    from concourse.bass_utils import run_bass_kernel_spmd

    arrays = {f"in_{k}": np.ascontiguousarray(v) for k, v in
              lay_out({k: np.asarray(v) for k, v in inputs.items()}).items()}
    nc = bacc.Bacc("TRN2", target_bir_lowering=False, num_devices=1)
    args = [nc.dram_tensor(k, v.shape, F32, kind="ExternalInput").ap() for k, v in arrays.items()]
    out = nc.dram_tensor("out", (P, KD, S), F32, kind="ExternalOutput").ap()
    build(nc, *args, out)
    got = run_bass_kernel_spmd(nc, [arrays], core_ids=[0]).results[0]["out"]
    return got.transpose(2, 1, 0).reshape(1, S, D)
```

```python
import concourse.bass as bass
from concourse import mybir
import numpy as np

P = 128
S = 256
D = 2048
E = 4096
FF = 5632
KD, KE, KF = D // P, E // P, FF // P
GROUPS = 8
HEADS = 8
M_HEADS = 4
EPS = 1e-6
COLS = 512
ROWS_PER_CHUNK = 2
CHUNK = ROWS_PER_CHUNK * COLS
RING = 4

F32 = mybir.dt.float32
F32R = mybir.dt.float32r
ACT = mybir.ActivationFunctionType
ALU = mybir.AluOpType

FQ, FK, FV, FG, MQ, MK, MV, MO, MI, MF, GA, GM, END = (
    0, 1024, 2048, 3072, 3080, 3592, 4104, 5128, 6152, 6156, 6160, 8208, 10256)

PHASES = [
    ("v", 4, [8, 8]),
    ("ug", GROUPS, [8, 8]),
    ("out1", 2, [16, 16]),
    ("vv", 2, [8, 8]),
    ("side", 1, [8] * 12),
    ("merge", 2, [8, 4, 4, 8, 4, 4]),
    ("out2", 2, [8, 8]),
    ("up", FF // COLS, [8, 8]),
    ("down", 2, [22, 22]),
]
FIRST_CHUNK, FIRST_GROUP = {}, {}
_c = _g = 0
for _name, _turns, _counts in PHASES:
    FIRST_CHUNK[_name], FIRST_GROUP[_name] = _c, _g
    _c += _turns * sum(_counts)
    _g += _turns * len(_counts)
CHUNKS = _c
COUNTS = {name: counts for name, _, counts in PHASES}
TURNS = {name: turns for name, turns, _ in PHASES}

PARAMS = {}
_n = 0
for _name, _w in (("a_norm", KD), ("v_gain", KE), ("final_norm", KD), ("norm1", KD), ("norm2", KD),
                  ("conv0", 2 * KF), ("conv1", 2 * KF), ("conv2", 2 * KF), ("conv_b", 2 * KF),
                  ("q_norm", 1), ("k_norm", 1), ("m_norm", 2 * M_HEADS), ("gate_bias", 16)):
    PARAMS[_name] = (_n, _n + _w)
    _n += _w
N_PARAMS = _n


class Steps:

    def __init__(self, engine, sem):
        self.engine, self.sem, self.done, self.turn, self.per = engine, sem, 0, None, 0

    def enter(self, turn, per, first=0):
        self.turn, self.per, self.before, self.first = turn, per, self.done, first

    def leave(self, turns):
        assert self.done - self.before == self.per, (self.done - self.before, self.per)
        self.done = self.before + self.per * turns
        self.turn = None

    def link(self, instruction):
        instruction.then_inc(self.sem, 1)
        self.done += 1
        self.engine.wait_ge(self.sem, self.done if self.turn is None else
                            self.turn * self.per + (self.done - self.first * self.per))


HEAD_AT = 22
AM_SPLITS = (80, 82, 84, 86)


def build(nc, x, stream, w_s, b_s, params, gate_w, identity, consts, out):
    kib = 1024
    where = (nc.sbuf_base + 31) // 32 * 32
    at = {}
    for region, size in (("ring", 48 * kib), ("h", 32 * kib), ("x", 16 * kib), ("y", 96 * kib),
                         ("mix", 8 * kib), ("small", 8 * kib - 160)):
        at[region] = where
        where += size
    assert where <= nc.sbuf_usable_end, (where, nc.sbuf_usable_end)

    def sb(name, region, offset, shape, dt=F32):
        return nc.alloc_sbuf_tensor_at(name, shape, dt, offset=at[region] + int(offset))

    raw = sb("raw", "ring", 0, [P, RING, CHUNK])
    w_hi = sb("w_hi", "ring", 16 * kib, [P, RING, CHUNK], F32R)
    w_lo = sb("w_lo", "ring", 32 * kib, [P, RING, CHUNK], F32R)
    h_hi = sb("h_hi", "h", 0, [P, KD, S], F32R)
    h_lo = sb("h_lo", "h", 16 * kib, [P, KD, S], F32R)
    xres = sb("xres", "x", 0, [P, KD, S])

    class Norm:

        def __init__(self, name, own, own_at, tmp, tmp_at):
            self.hi = sb(f"{name}_hi", own, own_at * kib, [P, KD, S], F32R)
            self.lo = sb(f"{name}_lo", own, (own_at + 16) * kib, [P, KD, S], F32R)
            names = ("sum_a", "sum_b", "sq_a", "sq_b", "val0", "val1")
            t = [sb(f"{name}_{k}", tmp, (tmp_at + 4 * n) * kib, [P, 4, S]) for n, k in enumerate(names)]
            self.sums, self.squares, self.values = t[0:2], t[2:4], t[4:6]

    norm_in = Norm("in", "y", 0, "y", 32)
    norm_mid = Norm("mid", "y", 64, "h", 0)
    norm_mlp = Norm("mlp", "y", 32, "y", 0)
    mid_values = [sb(f"mid_final{k}", "y", (48 + 4 * k) * kib, [P, 4, S]) for k in range(2)]
    u_act = sb("u_act", "x", 0, [P, 4, S])
    t1 = sb("t1", "x", 4 * kib, [P, 4, S])
    t2 = sb("t2", "x", 8 * kib, [P, 4, S])
    v_group = sb("v_group", "x", 12 * kib, [P, 2, COLS])
    y_hi = sb("y_hi", "y", 0, [P, KE, S], F32R)
    y_lo = sb("y_lo", "y", 32 * kib, [P, KE, S], F32R)
    v_all = sb("v_all", "y", 64 * kib, [P, 2, E])
    ws_t = sb("ws_t", "mix", 0, [P, GROUPS, P])
    bs_b = sb("bs_b", "mix", 4 * kib, [P, GROUPS, P])
    qk = sb("qk", "y", 0, [P, 24, S])
    vv = sb("vv", "y", 24 * kib, [P, 2, 2 * 1024])
    mo = sb("mo", "y", 40 * kib, [P, 8, S])
    ga = sb("ga", "y", 48 * kib, [P, KD, S])
    am = sb("am", "y", 64 * kib, [P, KD, S])
    qsq = sb("qsq", "y", 80 * kib, [P, 4 * S])
    hm_sq = sb("hm_sq", "y", 80 * kib, [P, 2 * S])
    q_diag = sb("q_diag", "y", 84 * kib, [P, 8, P])
    m_diag = sb("m_diag", "y", 82 * kib, [P, 2, P])
    hm_pair = [sb(f"hm{k}", "y", (84 + 2 * k) * kib, [P, 2 * S]) for k in range(2)]
    logits = sb("logits", "y", 88 * kib, [P, 384])
    probs = sb("probs", "y", 89.5 * kib, [P, 384])
    probs_t = sb("probs_t", "y", 91 * kib, [P, 384])
    tiny = 93 * kib
    gz = sb("gz", "y", tiny, [P, 2, 16])
    gn = sb("gn", "y", tiny + 128, [P, 2, 16])
    gl = sb("gl", "y", tiny + 256, [P, 2, 16])
    gr = sb("gr", "y", tiny + 384, [P, 2, 16])
    b_cum = sb("b_cum", "y", tiny + 512, [P, 2, M_HEADS])
    col = sb("col", "y", tiny + 544, [P, 16])
    q_ms = sb("q_ms", "y", tiny + 608, [P, 8])
    q_rstd = sb("q_rstd", "y", tiny + 640, [P, 8])
    m_ms = sb("m_ms", "y", tiny + 672, [P, 2])
    m_rstd = sb("m_rstd", "y", tiny + 704, [P, 2])
    gw_raw = sb("gw_raw", "mix", 0, [P, KD * 16])
    gw_hi = sb("gw_hi", "mix", kib, [P, KD, 16], F32R)
    gw_lo = sb("gw_lo", "mix", 2 * kib, [P, KD, 16], F32R)
    late = sb("late", "mix", 3 * kib, [P, 384])
    mask, tri = late[:, 0:256], late[:, 256:384]
    rows = sb("rows", "mix", 4.5 * kib, [16, S])
    head_row = [sb(f"head_row{i}", "mix", (5.5 + i) * kib, [16, S]) for i in range(2)]
    am_hi = sb("am_hi", "y", 0, [P, KD, S], F32R)
    am_lo = sb("am_lo", "y", 16 * kib, [P, KD, S], F32R)
    gate_a = sb("gate_a", "y", 32 * kib, [P, 4, S])
    gate_m = sb("gate_m", "y", 36 * kib, [P, 4, S])
    g_hi = sb("g_hi", "y", 64 * kib, [P, KD, S], F32R)
    g_lo = sb("g_lo", "y", 80 * kib, [P, KD, S], F32R)
    f_hi = sb("f_hi", "y", 0, [P, KF, S], F32R)
    f_lo = sb("f_lo", "y", 44 * kib, [P, KF, S], F32R)
    cg = sb("cg", "y", 88 * kib, [P, 4, S])
    cv = sb("cv", "y", 92 * kib, [P, 4, S])
    silu_t = sb("silu_t", "mix", 0, [P, 4, S])
    par = sb("par", "small", 0, [P, N_PARAMS])
    off = (N_PARAMS * 4 + 31) // 32 * 32
    ones = sb("ones", "small", off, [P, P])
    ident = sb("ident", "small", off + 512, [P, P])
    diag = [sb(f"diag{k}", "small", off + kib * (1 + k), [P, 2, P]) for k in range(2)]
    ws_scaled = sb("ws_scaled", "small", off + 3 * kib, [P, 2, P])
    r_sbuf = sb("r_sbuf", "small", off + 4 * kib, [P, S])
    tail = off + 5 * kib
    gains = sb("gains", "small", tail, [P, KD])
    minus_half = sb("minus_half", "small", tail + 64, [P, 8])
    v_stat = sb("v_stat", "small", tail + 96, [P, 8])
    n_ms = sb("n_ms", "small", tail + 128, [P, 8])
    n_rstd = sb("n_rstd", "small", tail + 160, [P, 8])
    q_gain = sb("q_gain", "small", tail + 192, [P, 1])
    m_gain = sb("m_gain", "small", tail + 224, [P, 2 * M_HEADS])

    def param(name, k=0, n=1):
        a, _ = PARAMS[name]
        return par[:, a + k:a + k + n] if isinstance(k, int) else par[:, bass.ds(k + a, n)]

    G = [nc.alloc_psum_tensor(f"g{i}", [P, 4 * S], F32) for i in range(2)]
    X = nc.alloc_psum_tensor("x_banks", [P, 2, COLS], F32)
    SV = nc.alloc_psum_tensor("sv", [P, 4, S], F32)
    PT = SV[:, 0:2, :].rearrange("p a b -> p (a b)")
    OUT = SV[:, 2:4, :].rearrange("p a b -> p (a b)")
    TILES = ((0, P, 0), (P, S, 1))

    class Sems:

        def __init__(self):
            self.made = {}

        def __getitem__(self, name):
            if name not in self.made:
                self.made[name] = nc.alloc_semaphore(name)
            return self.made[name]

    sem = Sems()
    raw_full = [sem[f"raw_full{i}"] for i in range(RING)]
    hi_ready, lo_ready, mm_done = sem["hi_ready"], sem["lo_ready"], sem["mm_done"]
    group_read = [sem["group_read0"], sem["group_read1"]]

    def chunk_of(phase, turn, k):
        return turn * sum(COUNTS[phase]) + (FIRST_CHUNK[phase] + k)

    def slot_of(phase, turn, k):
        return (FIRST_CHUNK[phase] + k + (turn * sum(COUNTS[phase]) if isinstance(turn, int) else 0)) % RING

    def group_waits(phase, turn, g):
        end = chunk_of(phase, turn, sum(COUNTS[phase][:g + 1]))
        half = len(COUNTS[phase]) // 2
        return g % 2, end, turn * half + (FIRST_GROUP[phase] // 2 + g // 2 + 2)

    block = nc.Block()
    with block:

        @block.sync
        def _(sp):
            for k in range(RING):
                sp.dma_start(raw[:, k, :], stream[k]).then_inc(raw_full[k], 16)
            sp.dma_start(ident[:], identity).then_inc(sem["ident_in"], 16)
            with sp.Fori(0, CHUNKS // RING - 1) as i:
                for k in range(RING):
                    sp.wait_ge(lo_ready, i * RING + (k + 1))
                    sp.dma_start(raw[:, k, :], stream[i * RING + (RING + k)]).then_inc(raw_full[k], 16)

        @block.tensor
        def _(pe):
            mm = nc.tensor.matmul

            def features(a_hi, a_lo, quads=None, before=0):
                def chunk(buf, slot, k, last):
                    if quads and k % 2 == 0:
                        pe.wait_ge(sem[quads], before + k // 2 + 1)
                    for j in range(ROWS_PER_CHUNK):
                        kt = k * ROWS_PER_CHUNK + j
                        for b in range(4):
                            at_w = slice(j * COLS + b * P, j * COLS + (b + 1) * P)
                            to = G[buf][:, b * S:(b + 1) * S]
                            for n, (w, a) in enumerate(((w_hi, a_hi), (w_hi, a_lo), (w_lo, a_hi))):
                                ins = mm(to, w[:, slot, at_w], a[:, kt, :],
                                         start=(kt == 0 and n == 0 and b % 2 == 0),
                                         stop=(last and j == ROWS_PER_CHUNK - 1 and n == 2),
                                         skip_group_check=True)
                    return ins
                return chunk

            def tokens(a_hi, a_lo, quads=None, before=0):
                def chunk(buf, slot, k, last):
                    if quads and k % 2 == 0:
                        pe.wait_ge(sem[quads], before + k // 2 + 1)
                    for j in range(ROWS_PER_CHUNK):
                        kt = k * ROWS_PER_CHUNK + j
                        for t in range(2):
                            to = G[buf][:, t * COLS:(t + 1) * COLS]
                            at_t = slice(t * P, (t + 1) * P)
                            for n, (a, w) in enumerate(((a_hi, w_hi), (a_hi, w_lo), (a_lo, w_hi))):
                                ins = mm(to, a[:, kt, at_t], w[:, slot, j * COLS:(j + 1) * COLS],
                                         start=(kt == 0 and n == 0),
                                         stop=(last and j == ROWS_PER_CHUNK - 1 and n == 2))
                    return ins
                return chunk

            def one(phase, turn, g, k, chunk):
                buf, end, read = group_waits(phase, turn, g)
                n = COUNTS[phase][g]
                if k == 0:
                    pe.wait_ge(group_read[buf], read - 1)
                pe.wait_ge(lo_ready, end + (k + 1 - n))
                slot = slot_of(phase, turn, sum(COUNTS[phase][:g]) + k)
                chunk(buf, slot, k, k == n - 1).then_inc(mm_done, 1)

            def group(phase, turn, g, chunk):
                for k in range(COUNTS[phase][g]):
                    one(phase, turn, g, k, chunk)

            def token_sums(to, parts):
                for t in range(2):
                    for n, part in enumerate(parts):
                        ins = mm(to[:, t:t + 1], part[:, t * P:(t + 1) * P], ones[:, 0:1],
                                 start=(n == 0), stop=(n == len(parts) - 1))
                return ins

            def spread(to, diagonal):
                for t in range(2):
                    ins = mm(to[:, t * P:(t + 1) * P], ones[:], diagonal[:, t, :], start=True, stop=True)
                return ins

            def blocks(part):
                return [part[:, b, :] for b in range(4)]

            pe.wait_ge(sem["ones_ready"], 1)
            for c in range(16):
                one("v", 0, c // 8, c % 8, tokens(norm_in.hi, norm_in.lo, "g_lo_ready" if c < 8 else None))
                if c == 5:
                    pe.wait_ge(sem["sums_ready"], 1)
                    token_sums(X[:, 0, 0:2], blocks(norm_in.sums[0])).then_inc(sem["stat_ready"], 1)
                if c == 8:
                    pe.wait_ge(sem["diag_ready"], 1)
                    spread(X[:, 1, 0:S], diag[0]).then_inc(sem["spread_ready"], 1)
            with pe.Fori(1, TURNS["v"]) as i:
                group("v", i, 0, tokens(norm_in.hi, norm_in.lo))
                group("v", i, 1, tokens(norm_in.hi, norm_in.lo))

            with pe.Fori(0, TURNS["ug"]) as i:
                group("ug", i, 0, features(h_hi, h_lo, "h_lo_ready"))
                pe.wait_ge(sem["ws_scaled"], i + 1)
                pe.wait_ge(sem["v_group_ready"], i + 1)
                for t in range(2):
                    for b in range(4):
                        ins = mm(SV[:, b, t * P:(t + 1) * P], v_group[:, t, b * P:(b + 1) * P],
                                 ws_scaled[:, t, :], start=True, stop=True)
                ins.then_inc(sem["sv_ready"], 1)
                group("ug", i, 1, features(h_hi, h_lo))

            with pe.Fori(0, TURNS["out1"]) as i:
                group("out1", i, 0, features(y_hi, y_lo, "y_lo_ready"))
                group("out1", i, 1, features(y_hi, y_lo))

            for c in range(32):
                one("vv", c // 16, c // 8 % 2, c % 8,
                    tokens(norm_mid.hi, norm_mid.lo, "g_lo_ready" if c < 8 else None, 4))
                if c == 3:
                    pe.wait_ge(sem["sums_ready"], 2)
                    token_sums(X[:, 0, 0:2], blocks(norm_mid.sums[0]))
                    token_sums(X[:, 0, 2:4], blocks(norm_mid.sums[1])).then_inc(sem["stat_ready"], 1)
                if c == 7:
                    pe.wait_ge(sem["diag_ready"], 2)
                    spread(X[:, 0, 0:S], diag[0])
                    spread(X[:, 1, 0:S], diag[1]).then_inc(sem["spread_ready"], 1)

            def gate_logits():
                pe.wait_ge(sem["gw_ready"], 1)
                for kt in range(KD):
                    for n, (w, a) in enumerate(((gw_hi, h_hi), (gw_hi, h_lo), (gw_lo, h_hi))):
                        ins = mm(OUT[0:16, 0:S], w[:, kt, :], a[:, kt, :],
                                 start=(kt == 0 and n == 0), stop=(kt == KD - 1 and n == 2))
                ins.then_inc(sem["gate_z_ready"], 1)

            def gates_by_token():
                pe.wait_ge(sem["gate_z_read"], 1)
                for t in range(2):
                    ins = nc.tensor.transpose(PT[:, t * 16:(t + 1) * 16], rows[:, t * P:(t + 1) * P], ident[0:16, 0:16])
                ins.then_inc(sem["gz_ready"], 1)

            def running_sums():
                pe.wait_ge(sem["gl_ready"], 1)
                pe.wait_ge(sem["late_in"], 16)
                mm(OUT[:, 0:12], tri, gl[:, 0, 0:12], start=True, stop=True)
                mm(OUT[:, 16:28], ones[:], gl[:, 0, 0:12], start=True, stop=False)
                mm(OUT[:, 16:28], tri, gl[:, 1, 0:12], start=False, stop=True).then_inc(sem["cum_ready"], 1)

            def gate_rows():
                pe.wait_ge(sem["gr_ready"], 1)
                for t in range(2):
                    ins = nc.tensor.transpose(OUT[0:16, t * P:(t + 1) * P], gr[:, t, :], ident[:])
                ins.then_inc(sem["rows_t_ready"], 1)

            def q_sums(n):
                pe.wait_ge(sem["qsq_ready"], n + 1)
                if n == 0:
                    pe.wait_ge(sem["rows_ready"], 1)
                if (8 * n + 9 - HEAD_AT - 4) // 4 >= 0:
                    pe.wait_ge(sem["fox_read"], (8 * n + 9 - HEAD_AT - 4) // 4 + 1)
                for b in range(4):
                    ins = token_sums(OUT[:, 2 * b:2 * b + 2], [qsq[:, b * S:(b + 1) * S]])
                ins.then_inc(sem["q_sums_ready"], 1)

            def q_spread(n):
                pe.wait_ge(sem["q_diag_ready"], n + 1)
                if 8 * n + 12 > HEAD_AT:
                    pe.wait_ge(sem["scores_read"], (8 * n + 12 - HEAD_AT) // 4 + 1)
                for b in range(4):
                    ins = spread(X[:, b // 2, b % 2 * S:b % 2 * S + S], q_diag[:, 2 * b:2 * b + 2, :])
                ins.then_inc(sem["q_spread_ready"], 1)

            def scores(n):
                pe.wait_ge(sem["head_row_ready"], n + 1)
                if n:
                    pe.wait_ge(sem["scores_read"], n)
                if n < HEADS:
                    pe.wait_ge(sem["qk_normed"], min(4, (HEAD_AT + 4 * n - 12) // 8 + 1))
                    q, k = qk[:, n, :], qk[:, 8 + n, :]
                else:
                    buf, _, read = group_waits("side", 0, 5)
                    pe.wait_ge(group_read[buf], read)
                    q, k = qk[:, 8 + n, :], qk[:, 12 + n, :]
                r = head_row[n % 2]
                for a, w, t in TILES:
                    to = X[:, 0, a:a + w]
                    if n < HEADS:
                        mm(to, q[:, t * P:(t + 1) * P], k[:, 0:w], start=True, stop=False)
                    ins = mm(to, ones[0:16, :], r[:, 0:w], start=n >= HEADS, stop=True)
                    if n >= HEADS:
                        ins = mm(X[:, 1, a:a + w], q[:, t * P:(t + 1) * P], k[:, 0:w], start=True, stop=True)
                ins.then_inc(sem["scores_ready"], 1)

            def transposes(n):
                pe.wait_ge(sem["probs_ready"], n + 1)
                if n:
                    pe.wait_ge(sem["probs_t_ready"], n)
                if n - HEADS >= 2:
                    pe.wait_ge(sem["m_done"], n - HEADS - 1)
                for a in range(0, 384, P):
                    ins = nc.tensor.transpose(PT[:, a:a + P], probs[:, a:a + P], ident[:])
                ins.then_inc(sem["probs_t_psum"], 1)

            def values(n):
                pe.wait_ge(sem["probs_t_ready"], n + 1)
                pe.wait_ge(sem["q_ms_ready"], min(4, (HEAD_AT + 4 + 4 * n - 9) // 8 + 1))
                if 0 < n <= HEADS:
                    pe.wait_ge(sem["fox_read"], n)
                elif n:
                    pe.wait_ge(sem["m_values_read"], n - HEADS)
                    pe.wait_ge(sem["m_ms_ready"], n - HEADS)
                for e in range(1 if n < HEADS else 2):
                    c = n * P if n < HEADS else 1024 + (n - HEADS) * S + e * P
                    mm(OUT[:, e * S:(e + 1) * S], vv[:, 0, c:c + P], probs_t[:, 0:S], start=True, stop=False)
                    ins = mm(OUT[:, e * S + P:(e + 1) * S], vv[:, 1, c:c + P], probs_t[:, S:S + P],
                             start=False, stop=True)
                ins.then_inc(sem["head_ready"], 1)

            def m_sums(m):
                pe.wait_ge(sem["m_values_read"], m + 1)
                token_sums(OUT[:, 0:2], [hm_sq[:, 0:S], hm_sq[:, S:2 * S]]).then_inc(sem["m_sums_ready"], 1)

            def m_spread(m):
                pe.wait_ge(sem["m_diag_ready"], m + 1)
                pe.wait_ge(sem["probs_t_ready"], min(HEADS + M_HEADS, HEADS + m + 2))
                spread(PT[:, 0:S], m_diag).then_inc(sem["m_spread_ready"], 1)

            side = [features(h_hi, h_lo, "h_lo_ready", 4)] + [features(h_hi, h_lo)] * 11
            for c in range(96):
                one("side", 0, c // 8, c % 8, side[c // 8])
                if c == 1:
                    gate_logits()
                if c == 2:
                    gates_by_token()
                if c == 5:
                    running_sums()
                if c == 7:
                    gate_rows()
                if c % 8 == 1 and 9 <= c <= 33:
                    q_sums(c // 8 - 1)
                if c % 8 == 4 and 12 <= c <= 36:
                    q_spread(c // 8 - 1)
                n, step = divmod(c - HEAD_AT, 4)
                if step == 0 and 0 <= n < HEADS + M_HEADS:
                    scores(n)
                if step == 3 and 0 <= n < HEADS + M_HEADS:
                    transposes(n)
                if step == 0 and 0 <= n - 1 < HEADS + M_HEADS:
                    values(n - 1)
                if step == 2 and 0 <= n - 1 - HEADS < M_HEADS:
                    m_sums(n - 1 - HEADS)
                if step == 1 and 0 <= n - 2 - HEADS < M_HEADS:
                    m_spread(n - 2 - HEADS)

            with pe.Fori(0, TURNS["merge"]) as i:
                for j in range(2):
                    group("merge", i, 3 * j, features(h_hi, h_lo))
                    group("merge", i, 3 * j + 1, features(am_hi[:, 0:8, :], am_lo[:, 0:8, :], "am_lo_ready"))
                    group("merge", i, 3 * j + 2, features(am_hi[:, 8:16, :], am_lo[:, 8:16, :], "am_lo_ready", 2))
            with pe.Fori(0, TURNS["out2"]) as i:
                group("out2", i, 0, features(g_hi, g_lo, "merged_lo_ready"))
                group("out2", i, 1, features(g_hi, g_lo))
            for c in range(16):
                one("up", 0, c // 8, c % 8,
                    features(norm_mlp.hi, norm_mlp.lo, "g_lo_ready" if c < 8 else None, 8))
                if c == 3:
                    pe.wait_ge(sem["sums_ready"], 3)
                    token_sums(X[:, 0, 0:2], blocks(norm_mlp.sums[0])).then_inc(sem["stat_ready"], 1)
                if c == 6:
                    pe.wait_ge(sem["diag_ready"], 3)
                    spread(X[:, 1, 0:S], diag[0]).then_inc(sem["spread_ready"], 1)
            with pe.Fori(1, TURNS["up"]) as i:
                group("up", i, 0, features(h_hi, h_lo, "h_lo_ready", 8))
                group("up", i, 1, features(h_hi, h_lo))
            with pe.Fori(0, TURNS["down"]) as i:
                group("down", i, 0, features(f_hi, f_lo, "f_lo_ready"))
                group("down", i, 1, features(f_hi, f_lo))

        @block.scalar
        def _(act):
            activation = nc.scalar.activation
            steps = Steps(act, sem["act_step"])

            def split(phase, turn, k):
                now = chunk_of(phase, turn, k)
                if isinstance(now, int) and now + RING >= CHUNKS:
                    return
                slot = slot_of(phase, turn, k)
                if isinstance(turn, int):
                    act.wait_ge(raw_full[slot], 16 * (now // RING + 2))
                else:
                    act.wait_ge(raw_full[slot], turn * (16 * sum(COUNTS[phase]) // RING)
                                + 16 * ((FIRST_CHUNK[phase] + k) // RING + 2))
                act.wait_ge(mm_done, now + 1)
                activation(w_hi[:, slot, :], raw[:, slot, :], ACT.Copy).then_inc(hi_ready, 1)

            def splits(phase, turn, g):
                for k in range(COUNTS[phase][g]):
                    split(phase, turn, sum(COUNTS[phase][:g]) + k)

            def done(phase, turn, g):
                buf, end, read = group_waits(phase, turn, g)
                act.wait_ge(mm_done, end)
                return G[buf], group_read[buf], read

            def high(to, of, count, value, after, **kw):
                act.wait_ge(sem[count], value)
                activation(to, of, ACT.Copy, **kw).then_inc(sem[after], 1)

            def high_h(q, values, before):
                high(h_hi[:, 4 * q:4 * q + 4, :], values[q % 2][:], "norm_ready", before + q + 1, "h_hi_ready")

            def squares(norm, q, with_gain):
                at_x = xres[:, 4 * q:4 * q + 4, :]
                activation((norm.squares if q else norm.sums)[0][:], at_x, ACT.Square).then_inc(sem["sq_ready"], 1)
                if with_gain:
                    for b in range(4):
                        ins = activation((norm.squares if q else norm.sums)[1][:, b, :], xres[:, 4 * q + b, :],
                                         ACT.Square, scale=param("final_norm", 4 * q + b))
                    ins.then_inc(sem["sq_ready"], 1)

            act.dma_start(par[:], params).then_inc(sem["params_in"], 16)
            for q in range(4):
                act.dma_start(xres[:, 4 * q:4 * q + 4, :], x[:, 4 * q:4 * q + 4, :]).then_inc(sem[f"x_in{q}"], 16)
            act.dma_start(ws_t[:], w_s).then_inc(sem["ws_in"], 16)
            act.dma_start(bs_b[:], b_s).then_inc(sem["bs_in"], 16)
            for q in range(4):
                high(norm_in.hi[:, 4 * q:4 * q + 4, :], norm_in.values[q % 2][:], "gained_ready", q + 1, "g_hi_ready")
                act.wait_ge(raw_full[q], 16)
                activation(w_hi[:, q, :], raw[:, q, :], ACT.Copy).then_inc(hi_ready, 1)

            def v_out(turn, g):
                product, read, _ = done("v", turn, g)
                for t in range(2):
                    at_v = (v_all[:, t, (2 * turn + g) * COLS:(2 * turn + g + 1) * COLS] if isinstance(turn, int) else
                            v_all[:, t, bass.ds(turn * (2 * COLS) + g * COLS, COLS)])
                    ins = activation(at_v, product[:, t * COLS:(t + 1) * COLS], ACT.Gelu_apprx_tanh,
                                     scale=n_rstd[:, t:t + 1])
                ins.then_inc(read, 1)

            for c in range(16):
                split("v", 0, c)
                if c < 4:
                    if c >= 2:
                        act.wait_ge(sem["sq_added"], c - 1)
                    squares(norm_in, c, False)
                if c == 7:
                    act.wait_ge(sem["rstd_ready"], 1)
                    v_out(0, 0)
                if c % 2 == 1 and c >= 9:
                    high_h((c - 9) // 2, norm_in.values, 0)
            v_out(0, 1)
            with act.Fori(1, TURNS["v"]) as i:
                for g in range(2):
                    splits("v", i, g)
                    v_out(i, g)
            for buf in range(2):
                act.wait_ge(group_read[buf], 1 + TURNS["v"])
            activation(y_hi[:, 0:16, :], v_all[:, 0, :], ACT.Square,
                       accum_out=v_stat[:, 0:1]).then_inc(sem["v_sq_ready"], 1)

            with act.Fori(0, TURNS["ug"]) as i:
                splits("ug", i, 0)
                product, read, _ = done("ug", i, 0)
                activation(u_act[:], product[:], ACT.Gelu_apprx_tanh).then_inc(read, 1)
                splits("ug", i, 1)
                product, read, _ = done("ug", i, 1)
                activation(t2[:], product[:], ACT.Tanh, scale=0.5).then_inc(sem["gate_t_ready"], 1)
                high(y_hi[:, bass.ds(i * 4, 4), :], t1[:], "y_ready", i + 1, "y_hi_ready")

            act.wait_ge(sem["y_lo_ready"], GROUPS)
            act.dma_start(xres[:], x).then_inc(sem["x_again"], 16)
            act.dma_start(gw_raw[:], gate_w).then_inc(sem["gw_in"], 16)
            act.dma_start(late[:], consts).then_inc(sem["late_in"], 16)

            def residual(phase, turn, g, norm, before, with_gain):
                splits(phase, turn, g)
                q = 2 * turn + g
                high(norm.hi[:, 4 * q:4 * q + 4, :], norm.values[q % 2][:], "gained_ready", before + q + 1,
                     "g_hi_ready")
                squares(norm, q, with_gain)

            for q in range(4):
                residual("out1", q // 2, q % 2, norm_mid, 4, True)

            for c in range(32):
                split("vv", c // 16, c % 16)
                if c % 8 == 7:
                    product, read, _ = done("vv", c // 16, c // 8 % 2)
                    if c == 7:
                        act.wait_ge(sem["rstd_both_ready"], 1)
                    for t in range(2):
                        ins = activation(vv[:, t, c // 8 * COLS:(c // 8 + 1) * COLS],
                                         product[:, t * COLS:(t + 1) * COLS], ACT.Copy, scale=n_rstd[:, 4 + t:5 + t])
                    ins.then_inc(read, 1)
                if c in (8, 10, 12, 14):
                    high_h((c - 8) // 2, mid_values, 4)

            side_out = ([(qk, 4 * b, ACT.Copy, 1.0) for b in (0, 2, 1, 3, 4, 5)]
                        + [(mo, 4 * b, ACT.Tanh, 0.5) for b in range(2)] + [(ga, 4 * b, ACT.Tanh, 0.5) for b in range(4)])
            for c in range(96):
                split("side", 0, c)
                if c == 0:
                    act.wait_ge(sem["gw_in"], 16)
                    activation(gw_hi[:], gw_raw[:], ACT.Copy).then_inc(sem["gw_hi_ready"], 1)
                if c == 1:
                    act.wait_ge(sem["gate_z_ready"], 1)
                    activation(rows[:], OUT[0:16, 0:S], ACT.Copy).then_inc(sem["gate_z_read"], 1)
                if c == 3:
                    act.wait_ge(sem["gn_ready"], 1)
                    steps.link(activation(gr[:], gn[:], ACT.Exp))
                    activation(gl[:], gr[:], ACT.Ln, bias=1.0).then_inc(sem["ln_ready"], 1)
                if c == 8:
                    act.wait_ge(sem["rows_t_ready"], 1)
                    activation(rows[:], OUT[0:16, 0:S], ACT.Copy).then_inc(sem["rows_ready"], 1)
                if c % 8 == 7:
                    product, read, _ = done("side", 0, c // 8)
                    to, b, func, scale = side_out[c // 8]
                    activation(to[:, b:b + 4, :], product[:], func, scale=scale).then_inc(read, 1)
                if c % 8 == 0 and 8 <= c <= 32:
                    n = c // 8 - 1
                    buf, _, read = group_waits("side", 0, n)
                    act.wait_ge(group_read[buf], read)
                    if n:
                        act.wait_ge(sem["q_sums_ready"], n)
                    b = side_out[n][1]
                    activation(qsq[:], qk[:, b:b + 4, :], ACT.Square).then_inc(sem["qsq_ready"], 1)
                n, step = divmod(c - HEAD_AT, 4)
                if step == 1 and 0 <= n < HEADS + M_HEADS:
                    act.wait_ge(sem["max_ready"], n + 1)
                    if n:
                        act.wait_ge(sem["probs_t_psum"], n)
                    for a, w, t in TILES:
                        ins = activation(probs[:, a:a + w], logits[:, a:a + w], ACT.Exp, bias=col[:, 2 + t:3 + t],
                                         accum_out=col[:, 4 + t:5 + t] if n < HEADS else None)
                    if n >= HEADS:
                        ins = activation(col[:, 6:8], col[:, 8:10], ACT.Exp)
                    ins.then_inc(sem["exp_ready"], 1)
                if step == 3 and 0 <= n < HEADS + M_HEADS:
                    act.wait_ge(sem["probs_t_psum"], n + 1)
                    if n:
                        act.wait_ge(sem["head_ready"], n)
                    activation(probs_t[:], PT[:, 0:384], ACT.Copy).then_inc(sem["probs_t_ready"], 1)
                if step == 0 and 0 <= n - 1 < HEADS + M_HEADS:
                    n -= 1
                    act.wait_ge(sem["head_ready"], n + 1)
                    if n < HEADS:
                        activation(am[:, n, :], OUT[:, 0:S], ACT.Copy).then_inc(sem["fox_read"], 1)
                    else:
                        if n > HEADS:
                            act.wait_ge(sem["m_sums_ready"], n - HEADS)
                        activation(hm_sq[:], OUT[:], ACT.Square).then_inc(sem["hm_sq_ready"], 1)
                if c in AM_SPLITS:
                    q = AM_SPLITS.index(c)
                    act.wait_ge(sem["m_done"], M_HEADS)
                    activation(am_hi[:, 4 * q:4 * q + 4, :], am[:, 4 * q:4 * q + 4, :],
                               ACT.Copy).then_inc(sem["am_hi_ready"], 1)

            with act.Fori(0, TURNS["merge"]) as i:
                for j in range(2):
                    splits("merge", i, 3 * j)
                    product, read, _ = done("merge", i, 3 * j)
                    activation(gate_m[:], product[:], ACT.Tanh, scale=0.5).then_inc(read, 1)
                    splits("merge", i, 3 * j + 1)
                    splits("merge", i, 3 * j + 2)
                    high(g_hi[:, bass.ds(i * 8 + 4 * j, 4), :], gate_a[:], "merged_ready", i * 2 + (j + 1),
                         "merged_hi_ready", scale=0.5)
            for q in range(4):
                residual("out2", q // 2, q % 2, norm_mlp, 8, False)

            def conv_start(turn, g, to):
                product, _, _ = done("up", turn, g)
                for b in range(4):
                    k = turn * 4 + (b + g * KF)
                    ins = activation(to[:, b, :], product[:, b * S:(b + 1) * S], ACT.Identity,
                                     scale=param("conv2", k), bias=param("conv_b", k))
                ins.then_inc(sem[("conv_g_started", "conv_v_started")[g]], 1)

            def gate_tanh(turn):
                act.wait_ge(sem["cg_ready"], turn + 1)
                activation(silu_t[:], cg[:], ACT.Tanh, scale=0.5).then_inc(sem["silu_t_ready"], 1)

            def f_high(turn):
                high(f_hi[:, bass.ds(turn * 4, 4), :], cv[:], "f_ready", turn + 1, "f_hi_ready")

            for c in range(16):
                split("up", 0, c)
                if c in (8, 10, 12, 14):
                    high_h((c - 8) // 2, norm_mlp.values, 8)
                if c == 9:
                    act.wait_ge(sem["scaled_ready"], 1)
                    conv_start(0, 0, cg)
                if c == 11:
                    gate_tanh(0)
            act.wait_ge(sem["scaled_ready"], 2)
            with act.Fori(1, TURNS["up"]) as i:
                for k in range(16):
                    split("up", i, k)
                    if k == 0:
                        conv_start(i - 1, 1, cv)
                    if k == 3:
                        f_high(i - 1)
                    if k == 8:
                        conv_start(i, 0, cg)
                    if k == 10:
                        gate_tanh(i)
            for i in range(TURNS["down"]):
                for k in range(44):
                    split("down", i, k)
                    if i == 0 and k == 0:
                        conv_start(TURNS["up"] - 1, 1, cv)
                    if i == 0 and k == 3:
                        f_high(TURNS["up"] - 1)

        @block.vector
        def _(dve):
            v = nc.vector
            steps = Steps(dve, sem["dve_step"])
            link = steps.link

            def split(phase, turn, k):
                now = chunk_of(phase, turn, k)
                if isinstance(now, int) and now + RING >= CHUNKS:
                    return
                low_of_chunk(slot_of(phase, turn, k), now + (RING + 1))

            def low_of_chunk(slot, count):
                dve.wait_ge(hi_ready, count)
                v.tensor_tensor(w_lo[:, slot, :], raw[:, slot, :], w_hi[:, slot, :].bitcast(F32),
                                ALU.subtract).then_inc(lo_ready, 1)

            def splits(phase, turn, g):
                for k in range(COUNTS[phase][g]):
                    split(phase, turn, sum(COUNTS[phase][:g]) + k)

            def done(phase, turn, g):
                buf, end, read = group_waits(phase, turn, g)
                dve.wait_ge(mm_done, end)
                return G[buf], group_read[buf], read

            def low(to, of, hi, count, value, after):
                dve.wait_ge(sem[count], value)
                return v.tensor_tensor(to, of, hi.bitcast(F32), ALU.subtract).then_inc(sem[after], 1)

            def mean_square(to, of, n):
                return v.tensor_scalar(to, of, 1.0 / n, EPS, ALU.mult, ALU.add)

            def diagonals(to, rstd):
                for t in range(2):
                    ins = v.tensor_scalar(to[:, t, :], ident[:], rstd[:, t:t + 1], None, ALU.mult)
                return ins

            def gained(norm, q, gain, before):
                if before + q >= 2 and q >= 2:
                    dve.wait_ge(sem["g_lo_ready"], before + q - 1)
                for b in range(4):
                    ins = v.tensor_scalar(norm.values[q % 2][:, b, :], xres[:, 4 * q + b, :], gain(4 * q + b), None,
                                          ALU.mult)
                ins.then_inc(sem["gained_ready"], 1)
                low(norm.lo[:, 4 * q:4 * q + 4, :], norm.values[q % 2][:], norm.hi[:, 4 * q:4 * q + 4, :],
                    "g_hi_ready", before + q + 1, "g_lo_ready")

            def normalise(q, values, gain, scale, before):
                if q >= 2:
                    dve.wait_ge(sem["h_lo_ready"], before + q - 1)
                for b in range(4):
                    ins = v.scalar_tensor_tensor(values[q % 2][:, b, :], xres[:, 4 * q + b, :], gain(4 * q + b), scale,
                                                 ALU.mult, ALU.mult)
                ins.then_inc(sem["norm_ready"], 1)

            def low_h(q, values, before):
                low(h_lo[:, 4 * q:4 * q + 4, :], values[q % 2][:], h_hi[:, 4 * q:4 * q + 4, :],
                    "h_hi_ready", before + q + 1, "h_lo_ready")

            v.memset(ones[:], 1.0).then_inc(sem["ones_ready"], 1)
            v.memset(minus_half[:], -0.5).then_inc(sem["minus_half_ready"], 1)
            for buf in range(2):
                dve.sem_inc(group_read[buf], 1)
            dve.wait_ge(sem["params_in"], 16)
            link(v.tensor_tensor(gains[:], param("final_norm", 0, KD), param("norm1", 0, KD), ALU.mult))
            link(v.tensor_scalar(q_gain[:], param("q_norm"), float(P) ** -0.5, None, ALU.mult))
            link(v.tensor_scalar(m_gain[:], param("m_norm", 0, 2 * M_HEADS), 0.5, None, ALU.mult))

            for q in range(4):
                dve.wait_ge(sem[f"x_in{q}"], 16)
                gained(norm_in, q, lambda k: param("a_norm", k), 0)
                low_of_chunk(q, q + 1)
            for c in range(16):
                split("v", 0, c)
                if 1 <= c < 4:
                    dve.wait_ge(sem["sq_ready"], c + 1)
                    if c > 1:
                        dve.wait_ge(sem["sq_added"], c - 1)
                    v.tensor_tensor(norm_in.sums[0][:], norm_in.sums[0][:], norm_in.squares[0][:],
                                    ALU.add).then_inc(sem["sq_added"] if c < 3 else sem["sums_ready"], 1)
                if c == 5:
                    dve.wait_ge(sem["stat_ready"], 1)
                    mean_square(n_ms[:, 0:2], X[:, 0, 0:2], D).then_inc(sem["ms_ready"], 1)
                if c == 6:
                    dve.wait_ge(sem["rstd_ready"], 1)
                    dve.wait_ge(sem["ident_in"], 16)
                    diagonals(diag[0], n_rstd[:, 0:2]).then_inc(sem["diag_ready"], 1)
                if c >= 8 and c % 2 == 0:
                    if c == 8:
                        dve.wait_ge(sem["spread_ready"], 1)
                    normalise((c - 8) // 2, norm_in.values, lambda k: param("a_norm", k), X[:, 1, 0:S], 0)
                if c >= 9 and c % 2 == 1:
                    low_h((c - 9) // 2, norm_in.values, 0)
            with dve.Fori(1, TURNS["v"]) as i:
                splits("v", i, 0)
                splits("v", i, 1)
            for buf in range(2):
                dve.wait_ge(group_read[buf], 1 + TURNS["v"])
            dve.wait_ge(sem["h_lo_ready"], 4)
            link(v.tensor_tensor_reduce(y_lo[:, 0:16, :].rearrange("p a b -> p (a b)"), v_all[:, 1, :],
                                        v_all[:, 1, :], scale=1.0, scalar=0.0, op0=ALU.mult, op1=ALU.add,
                                        accum_out=v_stat[:, 1:2]))
            dve.wait_ge(sem["v_sq_ready"], 1)
            mean_square(v_stat[:, 2:4], v_stat[:, 0:2], E).then_inc(sem["v_ms_ready"], 1)
            dve.wait_ge(sem["v_rstd_ready"], 1)
            dve.wait_ge(sem["ws_in"], 16)
            dve.wait_ge(sem["bs_in"], 16)

            with dve.Fori(0, TURNS["ug"]) as i:
                steps.enter(i, 2)
                for k in range(16):
                    split("ug", i, k)
                    if k == 3:
                        for t in range(2):
                            ins = v.tensor_scalar(ws_scaled[:, t, :],
                                                  ws_t[:, bass.ds(i, 1), :].rearrange("p a b -> p (a b)"),
                                                  v_stat[:, 4 + t:5 + t], None, ALU.mult)
                        ins.then_inc(sem["ws_scaled"], 1)
                    if k == 9:
                        dve.wait_ge(sem["sv_ready"], i + 1)
                        bias = bs_b[:, bass.ds(i, 1), :].rearrange("p a b -> p (a b)")
                        for b in range(4):
                            for t in range(2):
                                ins = v.scalar_tensor_tensor(t1[:, b, t * P:(t + 1) * P], SV[:, b, t * P:(t + 1) * P],
                                                             param("v_gain", i * 4 + b), bias, ALU.mult, ALU.add)
                        link(ins)
                    if k == 11:
                        _, _, read = group_waits("ug", i, 0)
                        dve.wait_ge(group_read[0], read)
                        link(v.tensor_tensor(t1[:], t1[:], u_act[:], ALU.mult))
                product, gate_read, read = done("ug", i, 1)
                dve.wait_ge(sem["gate_t_ready"], i + 1)
                v.scalar_tensor_tensor(t2[:].rearrange("p a b -> p (a b)"), t2[:].rearrange("p a b -> p (a b)"), 1.0,
                                       product[:], ALU.add, ALU.mult).then_inc(gate_read, 1)
                dve.wait_ge(gate_read, read)
                v.scalar_tensor_tensor(t1[:], t1[:], 0.5, t2[:], ALU.mult, ALU.mult).then_inc(sem["y_ready"], 1)
                low(y_lo[:, bass.ds(i * 4, 4), :], t1[:], y_hi[:, bass.ds(i * 4, 4), :], "y_hi_ready", i + 1,
                    "y_lo_ready")
                dve.wait_ge(sem["y_lo_ready"], i + 1)
                steps.leave(TURNS["ug"])

            def residual(phase, turn, g, norm, gain, before, sq_before, n_sq):
                splits(phase, turn, g)
                q = 2 * turn + g
                if phase == "out1" and q == 0:
                    dve.wait_ge(sem["x_again"], 16)
                product, read, value = done(phase, turn, g)
                at_x = xres[:, 4 * q:4 * q + 4, :]
                v.tensor_tensor(at_x, product[:].rearrange("p (b s) -> p b s", b=4), at_x, ALU.add).then_inc(read, 1)
                dve.wait_ge(read, value)
                gained(norm, q, gain, before)
                for n in range(n_sq):
                    dve.wait_ge(sem["sq_ready"], sq_before + q * n_sq + n + 1)
                    if q:
                        link(v.tensor_tensor(norm.sums[n][:], norm.sums[n][:], norm.squares[n][:], ALU.add))

            for q in range(4):
                residual("out1", q // 2, q % 2, norm_mid, lambda k: gains[:, k:k + 1], 4, 4, 2)
            dve.sem_inc(sem["sums_ready"], 1)

            for c in range(32):
                split("vv", c // 16, c % 16)
                if c == 3:
                    dve.wait_ge(sem["stat_ready"], 2)
                    mean_square(n_ms[:, 0:2], X[:, 0, 0:2], D).then_inc(sem["ms_ready"], 1)
                if c == 4:
                    dve.wait_ge(sem["rstd_ready"], 2)
                    link(v.tensor_tensor(n_ms[:, 4:6], n_rstd[:, 0:2], n_rstd[:, 0:2], ALU.mult))
                    link(v.scalar_tensor_tensor(n_ms[:, 6:8], X[:, 0, 2:4], 1.0 / D, n_ms[:, 4:6], ALU.mult, ALU.mult))
                    v.tensor_scalar(n_ms[:, 2:4], n_ms[:, 6:8], EPS, None, ALU.add).then_inc(sem["ms_ready"], 1)
                if c == 5:
                    dve.wait_ge(sem["rstd_ready"], 3)
                    v.tensor_tensor(n_rstd[:, 4:6], n_rstd[:, 0:2], n_rstd[:, 2:4], ALU.mult).then_inc(
                        sem["rstd_both_ready"], 1)
                    dve.wait_ge(sem["rstd_both_ready"], 1)
                    diagonals(diag[0], n_rstd[:, 4:6])
                    diagonals(diag[1], n_rstd[:, 0:2]).then_inc(sem["diag_ready"], 1)
                if c in (7, 9, 11, 13):
                    if c == 7:
                        dve.wait_ge(sem["spread_ready"], 2)
                    normalise((c - 7) // 2, mid_values, lambda k: gains[:, k:k + 1], X[:, 0, 0:S], 4)
                if c in (8, 10, 12, 14):
                    low_h((c - 8) // 2, mid_values, 4)
                if c in (16, 18, 20, 22):
                    for b in range(4):
                        k = 2 * (c - 16) + b
                        ins = v.scalar_tensor_tensor(xres[:, k, :], xres[:, k, :], param("final_norm", k),
                                                     X[:, 1, 0:S], ALU.mult, ALU.mult)
                    link(ins)

            def row(n):
                v.tensor_scalar(head_row[n % 2][:], rows[:], ident[0:16, n:n + 1], None, ALU.mult).then_inc(
                    sem["head_row_ready"], 1)

            for c in range(96):
                split("side", 0, c)
                if c == 0:
                    low(gw_lo[:].rearrange("p a b -> p (a b)"), gw_raw[:], gw_hi[:].rearrange("p a b -> p (a b)"),
                        "gw_hi_ready", 1, "gw_ready")
                if c == 2:
                    dve.wait_ge(sem["gz_ready"], 1)
                    for t in range(2):
                        ins = v.tensor_tensor(gz[:, t, :], PT[:, t * 16:(t + 1) * 16], param("gate_bias", 0, 16), ALU.add)
                    link(ins)
                    v.scalar_tensor_tensor(gn[:], gz[:], -1.0, gz[:], ALU.mult, ALU.min).then_inc(sem["gn_ready"], 1)
                if c == 4:
                    dve.wait_ge(sem["ln_ready"], 1)
                    v.scalar_tensor_tensor(gl[:], gz[:], 0.0, gl[:], ALU.min, ALU.subtract).then_inc(sem["gl_ready"], 1)
                if c == 6:
                    dve.wait_ge(sem["cum_ready"], 1)
                    cum = OUT[:, 0:32].rearrange("p (t c) -> p t c", t=2)
                    v.tensor_scalar(gr[:, :, 0:8], cum[:, :, 0:8], -1.0, None, ALU.mult)
                    v.tensor_copy(b_cum[:], cum[:, :, 8:12])
                    v.tensor_copy(gr[:, :, 12:16], gz[:, :, 12:16])
                    v.tensor_tensor(gr[:, :, 8:12], gz[:, :, 12:16], cum[:, :, 8:12],
                                    ALU.subtract).then_inc(sem["gr_ready"], 1)
                if c == 10:
                    dve.wait_ge(sem["rows_ready"], 1)
                    dve.wait_ge(sem["late_in"], 16)
                    row(0)
                    row(1)
                if c % 8 == 1 and 9 <= c <= 33:
                    dve.wait_ge(sem["q_sums_ready"], c // 8)
                    mean_square(q_ms[:], OUT[:, 0:8], P).then_inc(sem["q_ms_ready"], 1)
                if c % 8 == 2 and 10 <= c <= 34:
                    n = c // 8 - 1
                    dve.wait_ge(sem["q_rstd_ready"], n + 1)
                    for k in range(8):
                        ins = v.tensor_scalar(q_diag[:, k, :], ident[:], q_rstd[:, k:k + 1], None, ALU.mult)
                    ins.then_inc(sem["q_diag_ready"], 1)
                if c % 8 == 4 and 12 <= c <= 36:
                    n = c // 8 - 1
                    dve.wait_ge(sem["q_spread_ready"], n + 1)
                    at_q = qk[:, 4 * (0, 2, 1, 3)[n]:4 * (0, 2, 1, 3)[n] + 4, :].rearrange("p a b -> p (a b)")
                    gain = q_gain[:, 0:1] if n % 2 == 0 else param("k_norm")
                    v.scalar_tensor_tensor(at_q, at_q, gain, X[:].rearrange("p a b -> p (a b)"),
                                           ALU.mult, ALU.mult).then_inc(sem["qk_normed"], 1)
                n, step = divmod(c - HEAD_AT, 4)
                if step == 0 and 0 <= n < HEADS + M_HEADS:
                    dve.wait_ge(sem["scores_ready"], n + 1)
                    if n:
                        dve.wait_ge(sem["exp_ready"], n)
                        dve.wait_ge(sem["probs_ready"], n)
                    for a, w, t in TILES:
                        ins = v.tensor_tensor_reduce(logits[:, a:a + w], X[:, 0, a:a + w], mask[:, S - w:S],
                                                     scale=1.0, scalar=-3e38, op0=ALU.add, op1=ALU.max,
                                                     accum_out=col[:, t:t + 1])
                    if n < HEADS:
                        ins.then_inc(sem["scores_read"], 1)
                        dve.wait_ge(sem["scores_read"], n + 1)
                        v.tensor_scalar(col[:, 2:4], col[:, 0:2], -1.0, None, ALU.mult).then_inc(sem["max_ready"], 1)
                    else:
                        link(ins)
                        link(v.tensor_scalar(col[:, 2:4], col[:, 0:2], -1.0, 0.0, ALU.mult, ALU.min))
                        v.tensor_tensor(col[:, 8:10], col[:, 2:4], b_cum[:, :, n - HEADS], ALU.subtract).then_inc(
                            sem["max_ready"], 1)
                    if n + 2 < HEADS + M_HEADS:
                        row(n + 2)
                if step == 1 and 0 <= n < HEADS + M_HEADS:
                    dve.wait_ge(sem["exp_ready"], n + 1)
                    if n < HEADS:
                        link(v.reciprocal(col[:, 10:12], col[:, 4:6]))
                    else:
                        for a, w, t in TILES:
                            ins = v.tensor_tensor_reduce(probs[:, a:a + w], X[:, 1, a:a + w], probs[:, a:a + w],
                                                         scale=float(P) ** -0.5, scalar=0.0, op0=ALU.mult,
                                                         op1=ALU.add, accum_out=col[:, 4 + t:5 + t])
                        ins.then_inc(sem["scores_read"], 1)
                        dve.wait_ge(sem["scores_read"], n + 1)
                        link(v.scalar_tensor_tensor(col[:, 0:2], col[:, 4:6], -1.0, col[:, 4:6], ALU.mult, ALU.max))
                        link(v.tensor_tensor(col[:, 0:2], col[:, 0:2], col[:, 6:8], ALU.max))
                        link(v.reciprocal(col[:, 10:12], col[:, 0:2]))
                    for a, w, t in TILES:
                        ins = v.tensor_scalar(probs[:, a:a + w], probs[:, a:a + w], col[:, 10 + t:11 + t], None, ALU.mult)
                    ins.then_inc(sem["probs_ready"], 1)
                m = n - 1 - HEADS
                if step == 0 and 0 <= m < M_HEADS:
                    dve.wait_ge(sem["hm_sq_ready"], m + 1)
                    buf, _, read = group_waits("side", 0, 6 + m // 2)
                    dve.wait_ge(group_read[buf], read)
                    gate = mo[:, 2 * m:2 * m + 2, :].rearrange("p a b -> p (a b)")
                    if m >= 2:
                        dve.wait_ge(sem["m_done"], m - 1)
                    v.scalar_tensor_tensor(hm_pair[m % 2][:], gate, 1.0, OUT[:], ALU.add, ALU.mult).then_inc(
                        sem["m_values_read"], 1)
                if step == 2 and 0 <= m < M_HEADS:
                    dve.wait_ge(sem["m_sums_ready"], m + 1)
                    mean_square(m_ms[:], OUT[:, 0:2], 2 * P).then_inc(sem["m_ms_ready"], 1)
                if step == 3 and 0 <= m < M_HEADS:
                    dve.wait_ge(sem["m_rstd_ready"], m + 1)
                    if m:
                        dve.wait_ge(sem["m_spread_ready"], m)
                    diagonals(m_diag, m_rstd).then_inc(sem["m_diag_ready"], 1)
                m = n - 2 - HEADS
                if step == 1 and 0 <= m < M_HEADS:
                    dve.wait_ge(sem["m_spread_ready"], m + 1)
                    for e in range(2):
                        ins = v.scalar_tensor_tensor(am[:, 8 + 2 * m + e, :], hm_pair[m % 2][:, e * S:(e + 1) * S],
                                                     m_gain[:, 2 * m + e:2 * m + e + 1], PT[:, 0:S], ALU.mult, ALU.mult)
                    ins.then_inc(sem["m_done"], 1)
                if c in AM_SPLITS:
                    q = AM_SPLITS.index(c)
                    low(am_lo[:, 4 * q:4 * q + 4, :], am[:, 4 * q:4 * q + 4, :], am_hi[:, 4 * q:4 * q + 4, :],
                        "am_hi_ready", q + 1, "am_lo_ready")

            with dve.Fori(0, TURNS["merge"]) as i:
                for j in range(2):
                    flat = [gate[:].rearrange("p a b -> p (a b)") for gate in (gate_a, gate_m)]
                    splits("merge", i, 3 * j)
                    splits("merge", i, 3 * j + 1)
                    product, read_a, read = done("merge", i, 3 * j + 1)
                    at_g = bass.ds(i * 8 + 4 * j, 4)
                    v.scalar_tensor_tensor(gate_a[:], ga[:, at_g, :], 1.0, product[:].rearrange("p (b s) -> p b s", b=4),
                                           ALU.add, ALU.mult).then_inc(read_a, 1)
                    dve.wait_ge(read_a, read)
                    splits("merge", i, 3 * j + 2)
                    buf, _, read = group_waits("merge", i, 3 * j)
                    dve.wait_ge(group_read[buf], read)
                    product, read_m, read = done("merge", i, 3 * j + 2)
                    v.scalar_tensor_tensor(flat[1], flat[1], 1.0, product[:], ALU.add, ALU.mult).then_inc(read_m, 1)
                    dve.wait_ge(read_m, read)
                    v.tensor_tensor(gate_a[:], gate_a[:], gate_m[:], ALU.add).then_inc(sem["merged_ready"], 1)
                    count = i * 2 + (j + 1)
                    dve.wait_ge(sem["merged_hi_ready"], count)
                    v.scalar_tensor_tensor(g_lo[:, at_g, :], gate_a[:], 0.5, g_hi[:, at_g, :].bitcast(F32),
                                           ALU.mult, ALU.subtract).then_inc(sem["merged_lo_ready"], 1)
                    dve.wait_ge(sem["merged_lo_ready"], count)

            for q in range(4):
                residual("out2", q // 2, q % 2, norm_mlp, lambda k: param("norm2", k), 8, 12, 1)
            dve.sem_inc(sem["sums_ready"], 1)

            def conv_taps(turn, g, to):
                product, read, value = done("up", turn, g)
                dve.wait_ge(sem[("conv_g_started", "conv_v_started")[g]], turn + 1)
                for tap, late_by in (("conv1", 1), ("conv0", 2)):
                    for b in range(4):
                        ins = v.scalar_tensor_tensor(to[:, b, late_by:S], product[:, b * S:(b + 1) * S - late_by],
                                                     param(tap, turn * 4 + (b + g * KF)), to[:, b, late_by:S],
                                                     ALU.mult, ALU.add)
                    if late_by == 1:
                        link(ins)
                ins.then_inc(read, 1)
                dve.wait_ge(read, value)
                if g == 0:
                    dve.sem_inc(sem["cg_ready"], 1)

            def silu_times(turn):
                dve.wait_ge(sem["silu_t_ready"], turn + 1)
                link(v.scalar_tensor_tensor(cg[:], silu_t[:], 1.0, cg[:], ALU.add, ALU.mult))

            def f_product():
                v.scalar_tensor_tensor(cv[:], cv[:], 0.5, cg[:], ALU.mult, ALU.mult).then_inc(sem["f_ready"], 1)

            def f_low(turn):
                at_f = bass.ds(turn * 4, 4)
                low(f_lo[:, at_f, :], cv[:], f_hi[:, at_f, :], "f_hi_ready", turn + 1, "f_lo_ready")

            def scaled(g):
                product, _, _ = done("up", 0, g)
                for b in range(4):
                    at_b = product[:, b * S:(b + 1) * S]
                    ins = v.tensor_tensor(at_b, at_b, r_sbuf[:], ALU.mult)
                ins.then_inc(sem["scaled_ready"], 1)

            for c in range(16):
                split("up", 0, c)
                if c == 3:
                    dve.wait_ge(sem["stat_ready"], 3)
                    mean_square(n_ms[:, 0:2], X[:, 0, 0:2], D).then_inc(sem["ms_ready"], 1)
                if c == 4:
                    dve.wait_ge(sem["rstd_ready"], 4)
                    diagonals(diag[0], n_rstd[:, 0:2]).then_inc(sem["diag_ready"], 1)
                if c == 6:
                    dve.wait_ge(sem["spread_ready"], 3)
                    link(v.tensor_copy(r_sbuf[:], X[:, 1, 0:S]))
                if c in (9, 11, 13, 15):
                    low_h((c - 9) // 2, norm_mlp.values, 8)
                if c in (7, 9, 11, 13):
                    normalise((c - 7) // 2, norm_mlp.values, lambda k: param("norm2", k), r_sbuf[:], 8)
                if c == 8:
                    scaled(0)
                if c == 10:
                    conv_taps(0, 0, cg)
                if c == 12:
                    silu_times(0)
                if c == 15:
                    scaled(1)
            with dve.Fori(1, TURNS["up"]) as i:
                steps.enter(i, 3, 1)
                for k in range(16):
                    split("up", i, k)
                    if k == 1:
                        conv_taps(i - 1, 1, cv)
                    if k == 2:
                        f_product()
                    if k == 4:
                        f_low(i - 1)
                    if k == 9:
                        conv_taps(i, 0, cg)
                    if k == 11:
                        silu_times(i)
                steps.leave(TURNS["up"] - 1)

            for i in range(TURNS["down"]):
                for k in range(44):
                    split("down", i, k)
                    if i == 0 and k == 1:
                        conv_taps(TURNS["up"] - 1, 1, cv)
                    if i == 0 and k == 2:
                        f_product()
                    if i == 0 and k == 4:
                        f_low(TURNS["up"] - 1)
                    if k % 22 == 21:
                        g = k // 22
                        product, read, value = done("down", i, g)
                        k0 = (2 * i + g) * 4
                        at_x = xres[:, k0:k0 + 4, :]
                        v.tensor_tensor(at_x, product[:].rearrange("p (b s) -> p b s", b=4), at_x,
                                        ALU.add).then_inc(read, 1)

        @block.gpsimd
        def _(pool):
            p = nc.gpsimd

            def rstd(to, of, count, value, after):
                pool.wait_ge(sem[count], value)
                p.tensor_tensor(to, of, minus_half[:, 0:of.shape[1]], ALU.pow).then_inc(sem[after], 1)

            pool.wait_ge(sem["minus_half_ready"], 1)
            rstd(n_rstd[:, 0:2], n_ms[:, 0:2], "ms_ready", 1, "rstd_ready")
            rstd(v_stat[:, 4:6], v_stat[:, 2:4], "v_ms_ready", 1, "v_rstd_ready")
            p.tensor_copy(v_group[:], v_all[:, :, 0:COLS]).then_inc(sem["v_group_ready"], 1)
            with pool.Fori(1, GROUPS) as i:
                pool.wait_ge(sem["sv_ready"], i)
                p.tensor_copy(v_group[:], v_all[:, :, bass.ds(i * COLS, COLS)]).then_inc(sem["v_group_ready"], 1)
            rstd(n_rstd[:, 0:2], n_ms[:, 0:2], "ms_ready", 2, "rstd_ready")
            rstd(n_rstd[:, 2:4], n_ms[:, 2:4], "ms_ready", 3, "rstd_ready")
            for n in range(4):
                rstd(q_rstd[:], q_ms[:], "q_ms_ready", n + 1, "q_rstd_ready")
            for m in range(M_HEADS):
                rstd(m_rstd[:], m_ms[:], "m_ms_ready", m + 1, "m_rstd_ready")
            rstd(n_rstd[:, 0:2], n_ms[:, 0:2], "ms_ready", 4, "rstd_ready")
            for q in range(4):
                buf, _, read = group_waits("down", q // 2, q % 2)
                pool.wait_ge(group_read[buf], read)
                p.dma_start(out[:, 4 * q:4 * q + 4, :], xres[:, 4 * q:4 * q + 4, :]).then_inc(sem["stored"], 16)
            pool.wait_ge(sem["stored"], 64)


def chunks_of(w):
    k, n = w.shape
    w = w.reshape(k // CHUNK_ROWS, ROWS_PER_CHUNK, P, n // COLS, COLS)
    return np.ascontiguousarray(w.transpose(3, 0, 2, 1, 4)).reshape(n // COLS, k // CHUNK_ROWS, P, CHUNK)


CHUNK_ROWS = ROWS_PER_CHUNK * P


def feature_major(a):
    return np.ascontiguousarray(a.T.reshape(-1, P, a.shape[0]).transpose(1, 0, 2))


def lay_out(i):
    w_in, w2, w_up = i["a_w_in"][0], i["w_in_2"][0], i["w_up_2"][0]
    u, v, gate = (chunks_of(w_in[:, k * E:(k + 1) * E]) for k in range(3))
    qk = [chunks_of(w2[:, a:b]) for a, b in ((FQ, FV), (MQ, MV))]
    vv = [chunks_of(w2[:, a:b]) for a, b in ((FV, FG), (MV, MO))]
    ga, gm = chunks_of(w2[:, GA:GM]), chunks_of(w2[:, GM:END])
    pa, pm = chunks_of(i["w_proj_a_2"][0]), chunks_of(i["w_proj_m_2"][0])
    up_g, up_v = chunks_of(w_up[:, :FF]), chunks_of(w_up[:, FF:])
    parts = [v]
    for g in range(GROUPS):
        parts += [u[g], gate[g]]
    parts += [chunks_of(i["a_w_out"][0])] + vv + [qk[0][[0, 2, 1, 3]], qk[1], chunks_of(w2[:, MO:MI]), ga]
    for g in range(4):
        parts += [gm[g], pa[g], pm[g]]
    parts += [chunks_of(i["w_out_2"][0])]
    for g in range(FF // COLS):
        parts += [up_g[g], up_v[g]]
    parts += [chunks_of(i["w_down_2"][0])]
    stream = np.concatenate([a.reshape(-1, P, CHUNK) for a in parts])
    assert stream.shape[0] == CHUNKS

    def cols(a):
        return a.reshape(-1, P).T

    conv = i["conv_w_2"][0]
    bias = np.concatenate([i["fox_f_bias_2"][0], i["m_f_bias_2"][0], i["m_i_bias_2"][0]])
    params = np.concatenate([
        cols(i["a_norm"][0]), cols(i["a_v_gain"][0]), cols(i["final_norm"]), cols(i["norm1_g_2"][0]),
        cols(i["norm2_g_2"][0]), cols(conv[0]), cols(conv[1]), cols(conv[2]), cols(i["conv_b_2"][0]),
        cols(i["q_norm_g_2"][0]), cols(i["k_norm_g_2"][0]), cols(i["m_norm_g_2"][0].reshape(-1)),
        np.broadcast_to(bias, (P, 16))], axis=1)
    w_gates = np.concatenate([w2[:, FG:MQ], w2[:, MF:GA], w2[:, MI:MF]], axis=1)
    gate_w = w_gates.reshape(KD, P, 16).transpose(1, 0, 2).reshape(P, KD * 16)
    t, s = np.arange(P)[:, None], np.arange(P)[None, :]
    consts = np.concatenate([np.zeros((P, P)), np.where(s > t, -1e30, 0.0), np.where(t <= s, 1.0, 0.0)],
                            axis=1).astype(np.float32)
    return {
        "x": feature_major(i["x"][0]),
        "stream": stream,
        "w_s": i["a_w_s"][0].transpose(2, 0, 1),
        "b_s": np.broadcast_to(i["a_b_s"][0], (P, GROUPS, P)),
        "params": params,
        "gate_w": gate_w,
        "identity": np.eye(P, dtype=np.float32),
        "consts": consts,
    }


def kernel(**inputs):
    import concourse.bacc as bacc
    from concourse.bass_utils import run_bass_kernel_spmd

    arrays = {f"in_{k}": np.ascontiguousarray(v) for k, v in
              lay_out({k: np.asarray(v) for k, v in inputs.items()}).items()}
    nc = bacc.Bacc("TRN2", target_bir_lowering=False, num_devices=1)
    args = [nc.dram_tensor(k, v.shape, F32, kind="ExternalInput").ap() for k, v in arrays.items()]
    out = nc.dram_tensor("out", (P, KD, S), F32, kind="ExternalOutput").ap()
    build(nc, *args, out)
    got = run_bass_kernel_spmd(nc, [arrays], core_ids=[0]).results[0]["out"]
    return got.transpose(2, 1, 0).reshape(1, S, D)
```

```python
import concourse.bass as bass
from concourse import mybir
import numpy as np

P = 128
S = 256
D = 2048
E = 4096
FF = 5632
KD, KE, KF = D // P, E // P, FF // P
GROUPS = 8
HEADS = 8
M_HEADS = 4
EPS = 1e-6
COLS = 512
ROWS_PER_CHUNK = 2
CHUNK = ROWS_PER_CHUNK * COLS
RING = 4

F32 = mybir.dt.float32
F32R = mybir.dt.float32r
ACT = mybir.ActivationFunctionType
ALU = mybir.AluOpType

FQ, FK, FV, FG, MQ, MK, MV, MO, MI, MF, GA, GM, END = (
    0, 1024, 2048, 3072, 3080, 3592, 4104, 5128, 6152, 6156, 6160, 8208, 10256)

PHASES = [
    ("v", 4, [8, 8]),
    ("ug", GROUPS, [8, 8]),
    ("out1", 2, [16, 16]),
    ("vv", 2, [8, 8]),
    ("side", 1, [8] * 12),
    ("merge", 2, [8, 4, 4, 8, 4, 4]),
    ("out2", 2, [8, 8]),
    ("up", FF // COLS, [8, 8]),
    ("down", 2, [22, 22]),
]
FIRST_CHUNK, FIRST_GROUP = {}, {}
_c = _g = 0
for _name, _turns, _counts in PHASES:
    FIRST_CHUNK[_name], FIRST_GROUP[_name] = _c, _g
    _c += _turns * sum(_counts)
    _g += _turns * len(_counts)
CHUNKS = _c
COUNTS = {name: counts for name, _, counts in PHASES}
TURNS = {name: turns for name, turns, _ in PHASES}

PARAMS = {}
_n = 0
for _name, _w in (("a_norm", KD), ("v_gain", KE), ("final_norm", KD), ("norm1", KD), ("norm2", KD),
                  ("conv0", 2 * KF), ("conv1", 2 * KF), ("conv2", 2 * KF), ("conv_b", 2 * KF),
                  ("q_norm", 1), ("k_norm", 1), ("m_norm", 2 * M_HEADS), ("gate_bias", 16)):
    PARAMS[_name] = (_n, _n + _w)
    _n += _w
N_PARAMS = _n


class Steps:

    def __init__(self, engine, sem):
        self.engine, self.sem, self.done, self.turn, self.per = engine, sem, 0, None, 0

    def enter(self, turn, per, first=0):
        self.turn, self.per, self.before, self.first = turn, per, self.done, first

    def leave(self, turns):
        assert self.done - self.before == self.per, (self.done - self.before, self.per)
        self.done = self.before + self.per * turns
        self.turn = None

    def link(self, instruction):
        instruction.then_inc(self.sem, 1)
        self.done += 1
        self.engine.wait_ge(self.sem, self.done if self.turn is None else
                            self.turn * self.per + (self.done - self.first * self.per))


HEAD_AT = 22
VV_OUT = (10, 15, 23, 31)
WARM_UP = 22
AM_SPLITS = (80, 82, 84, 86)


def build(nc, x, stream, w_s, b_s, params, gate_w, identity, consts, out):
    kib = 1024
    where = (nc.sbuf_base + 31) // 32 * 32
    at = {}
    for region, size in (("ring", 48 * kib), ("h", 32 * kib), ("x", 16 * kib), ("y", 96 * kib),
                         ("mix", 8 * kib), ("small", 8 * kib - 160)):
        at[region] = where
        where += size
    assert where <= nc.sbuf_usable_end, (where, nc.sbuf_usable_end)

    def sb(name, region, offset, shape, dt=F32):
        return nc.alloc_sbuf_tensor_at(name, shape, dt, offset=at[region] + int(offset))

    raw = sb("raw", "ring", 0, [P, RING, CHUNK])
    w_hi = sb("w_hi", "ring", 16 * kib, [P, RING, CHUNK], F32R)
    w_lo = sb("w_lo", "ring", 32 * kib, [P, RING, CHUNK], F32R)
    h_hi = sb("h_hi", "h", 0, [P, KD, S], F32R)
    h_lo = sb("h_lo", "h", 16 * kib, [P, KD, S], F32R)
    xres = sb("xres", "x", 0, [P, KD, S])

    class Norm:

        def __init__(self, name, gain, own, own_at, tmp, tmp_at):
            self.gain = gain
            self.hi = sb(f"{name}_hi", own, own_at * kib, [P, KD, S], F32R)
            self.lo = sb(f"{name}_lo", own, (own_at + 16) * kib, [P, KD, S], F32R)
            names = ("sum_a", "sum_b", "sq_a", "sq_b")
            t = [sb(f"{name}_{k}", tmp, (tmp_at + 4 * n) * kib, [P, 4, S]) for n, k in enumerate(names)]
            self.sums, self.squares = t[0:2], t[2:4]

    norm_in = Norm("in", lambda k: param("a_norm", k), "y", 0, "y", 32)
    norm_mid = Norm("mid", lambda k: gains[:, k:k + 1], "y", 64, "h", 0)
    norm_mlp = Norm("mlp", lambda k: param("norm2", k), "h", 0, "y", 0)
    normed = [sb(f"normed{k}", "y", (48 + 4 * k) * kib, [P, 4, S]) for k in range(2)]
    u_act = sb("u_act", "x", 0, [P, 4, S])
    t1 = sb("t1", "x", 4 * kib, [P, 4, S])
    t2 = sb("t2", "x", 8 * kib, [P, 4, S])
    v_group = sb("v_group", "x", 12 * kib, [P, 2, COLS])
    y_hi = sb("y_hi", "y", 0, [P, KE, S], F32R)
    y_lo = sb("y_lo", "y", 32 * kib, [P, KE, S], F32R)
    v_all = sb("v_all", "y", 64 * kib, [P, 2, E])
    ws_t = sb("ws_t", "mix", 0, [P, GROUPS, P])
    bs_b = sb("bs_b", "mix", 4 * kib, [P, GROUPS, P])
    qk = sb("qk", "y", 0, [P, 24, S])
    vv = sb("vv", "y", 24 * kib, [P, 2, 2 * 1024])
    mo = sb("mo", "y", 40 * kib, [P, 8, S])
    ga = sb("ga", "y", 48 * kib, [P, KD, S])
    am = sb("am", "y", 64 * kib, [P, KD, S])
    qsq = sb("qsq", "y", 80 * kib, [P, 4 * S])
    hm_sq = sb("hm_sq", "y", 80 * kib, [P, 2 * S])
    q_diag = sb("q_diag", "y", 84 * kib, [P, 8, P])
    m_diag = sb("m_diag", "y", 82 * kib, [P, 2, P])
    hm_pair = [sb(f"hm{k}", "y", (84 + 2 * k) * kib, [P, 2 * S]) for k in range(2)]
    logits = sb("logits", "y", 88 * kib, [P, 384])
    probs = sb("probs", "y", 89.5 * kib, [P, 384])
    probs_t = sb("probs_t", "y", 91 * kib, [P, 384])
    tiny = 93 * kib
    gz = sb("gz", "y", tiny, [P, 2, 16])
    gn = sb("gn", "y", tiny + 128, [P, 2, 16])
    gl = sb("gl", "y", tiny + 256, [P, 2, 16])
    gr = sb("gr", "y", tiny + 736, [P, 2, 32])
    head_pick = sb("head_pick", "y", tiny + 992, [64, 16])
    ones_r = sb("ones_r", "y", tiny + 1088, [64, P], F32R)
    b_cum = sb("b_cum", "y", tiny + 512, [P, 2, M_HEADS])
    col = sb("col", "y", tiny + 544, [P, 16])
    q_ms = sb("q_ms", "y", tiny + 608, [P, 8])
    q_rstd = sb("q_rstd", "y", tiny + 640, [P, 8])
    m_ms = sb("m_ms", "y", tiny + 672, [P, 2])
    m_rstd = sb("m_rstd", "y", tiny + 704, [P, 2])
    gw_raw = sb("gw_raw", "mix", 0, [P, KD * 16])
    gw_hi = sb("gw_hi", "mix", kib, [P, KD, 16], F32R)
    gw_lo = sb("gw_lo", "mix", 2 * kib, [P, KD, 16], F32R)
    late = sb("late", "mix", 3 * kib, [P, 384])
    mask, tri = late[:, 0:256], late[:, 256:384]
    gate_z = sb("gate_z", "mix", 4.5 * kib, [16, S])
    rows_split = sb("rows_split", "mix", 0, [64, S], F32R)
    head_row = [sb(f"head_row{i}", "mix", (5.5 + i) * kib, [64, S], F32R) for i in range(2)]
    am_hi = sb("am_hi", "y", 0, [P, KD, S], F32R)
    am_lo = sb("am_lo", "y", 16 * kib, [P, KD, S], F32R)
    gate_a = sb("gate_a", "y", 32 * kib, [P, 4, S])
    gate_m = sb("gate_m", "y", 36 * kib, [P, 4, S])
    g_hi = sb("g_hi", "y", 64 * kib, [P, KD, S], F32R)
    g_lo = sb("g_lo", "y", 80 * kib, [P, KD, S], F32R)
    f_hi = sb("f_hi", "y", 0, [P, KF, S], F32R)
    f_lo = sb("f_lo", "y", 44 * kib, [P, KF, S], F32R)
    cg = sb("cg", "y", 88 * kib, [P, 4, S])
    cv = sb("cv", "y", 92 * kib, [P, 4, S])
    silu_t = sb("silu_t", "mix", 0, [P, 4, S])
    par = sb("par", "small", 0, [P, N_PARAMS])
    off = (N_PARAMS * 4 + 31) // 32 * 32
    ones = sb("ones", "small", off, [P, P])
    ident = sb("ident", "small", off + 512, [P, P])
    diag = [sb(f"diag{k}", "small", off + kib * (1 + k), [P, 2, P]) for k in range(2)]
    ws_scaled = sb("ws_scaled", "small", off + 3 * kib, [P, 2, P])
    r_sbuf = sb("r_sbuf", "small", off + 4 * kib, [P, S])
    tail = off + 5 * kib
    gains = sb("gains", "small", tail, [P, KD])
    minus_half = sb("minus_half", "small", tail + 64, [P, 8])
    v_stat = sb("v_stat", "small", tail + 96, [P, 8])
    n_ms = sb("n_ms", "small", tail + 128, [P, 8])
    n_rstd = sb("n_rstd", "small", tail + 160, [P, 8])
    q_gain = sb("q_gain", "small", tail + 192, [P, 1])
    m_gain = sb("m_gain", "small", tail + 224, [P, 2 * M_HEADS])

    def param(name, k=0, n=1):
        a, _ = PARAMS[name]
        return par[:, a + k:a + k + n] if isinstance(k, int) else par[:, bass.ds(k + a, n)]

    G = [nc.alloc_psum_tensor(f"g{i}", [P, 4 * S], F32) for i in range(2)]
    X = nc.alloc_psum_tensor("x_banks", [P, 2, COLS], F32)
    SV = nc.alloc_psum_tensor("sv", [P, 4, S], F32)
    PT = SV[:, 0:2, :].rearrange("p a b -> p (a b)")
    OUT = SV[:, 2:4, :].rearrange("p a b -> p (a b)")
    TILES = ((0, P, 0), (P, S, 1))

    class Sems:

        def __init__(self):
            self.made = {}

        def __getitem__(self, name):
            if name not in self.made:
                self.made[name] = nc.alloc_semaphore(name)
            return self.made[name]

    sem = Sems()
    raw_full = [sem[f"raw_full{i}"] for i in range(RING)]
    hi_ready, lo_ready, mm_done = sem["hi_ready"], sem["lo_ready"], sem["mm_done"]
    group_read = [sem["group_read0"], sem["group_read1"]]

    def chunk_of(phase, turn, k):
        return turn * sum(COUNTS[phase]) + (FIRST_CHUNK[phase] + k)

    def slot_of(phase, turn, k):
        return (FIRST_CHUNK[phase] + k + (turn * sum(COUNTS[phase]) if isinstance(turn, int) else 0)) % RING

    def group_waits(phase, turn, g):
        end = chunk_of(phase, turn, sum(COUNTS[phase][:g + 1]))
        half = len(COUNTS[phase]) // 2
        return g % 2, end, turn * half + (FIRST_GROUP[phase] // 2 + g // 2 + 2)

    def load_x(queue, q, first=0, n=4):
        at_b = slice(4 * q + first, 4 * q + first + n)
        queue.dma_start(xres[:, at_b, :], x[:, at_b, :]).then_inc(sem[f"x_in{q}"], 16)

    def store(queue, first, n):
        queue.dma_start(out[:, first:first + n, :], xres[:, first:first + n, :]).then_inc(sem["stored"], 16)

    block = nc.Block()
    with block:

        @block.sync
        def _(sp):
            sp.dma_start(par[:], params).then_inc(sem["params_in"], 16)
            for k in range(RING):
                sp.dma_start(raw[:, k, :], stream[k]).then_inc(raw_full[k], 16)
                if k == 1:
                    load_x(sp, 1)
            load_x(sp, 2)
            load_x(sp, 3)
            with sp.Fori(0, CHUNKS // RING - 1) as i:
                for k in range(RING):
                    sp.wait_ge(lo_ready, i * RING + (k + 1))
                    sp.dma_start(raw[:, k, :], stream[i * RING + (RING + k)]).then_inc(raw_full[k], 16)
            sp.wait_ge(sem["last_half_ready"], 1)
            store(sp, 12, 2)
            sp.wait_ge(sem["stored"], 16 * 5)

        @block.tensor
        def _(pe):
            mm = nc.tensor.matmul

            def features(a_hi, a_lo, quads=None, before=0):
                def chunk(buf, slot, k, last):
                    if quads and k % 2 == 0:
                        pe.wait_ge(sem[quads], before + k // 2 + 1)
                    for b in range(4):
                        for j in range(ROWS_PER_CHUNK):
                            kt = k * ROWS_PER_CHUNK + j
                            at_w = slice(j * COLS + b * P, j * COLS + (b + 1) * P)
                            to = G[buf][:, b * S:(b + 1) * S]
                            for n, (w, a) in enumerate(((w_hi, a_hi), (w_hi, a_lo), (w_lo, a_hi))):
                                ins = mm(to, w[:, slot, at_w], a[:, kt, :],
                                         start=(kt == 0 and n == 0 and b % 2 == 0),
                                         stop=(last and j == ROWS_PER_CHUNK - 1 and n == 2),
                                         skip_group_check=True)
                    return ins
                return chunk

            def tokens(a_hi, a_lo, quads=None, before=0):
                def chunk(buf, slot, k, last):
                    if quads and k % 2 == 0:
                        pe.wait_ge(sem[quads], before + k // 2 + 1)
                    for j in range(ROWS_PER_CHUNK):
                        kt = k * ROWS_PER_CHUNK + j
                        for t in range(2):
                            to = G[buf][:, t * COLS:(t + 1) * COLS]
                            at_t = slice(t * P, (t + 1) * P)
                            for n, (a, w) in enumerate(((a_hi, w_hi), (a_hi, w_lo), (a_lo, w_hi))):
                                ins = mm(to, a[:, kt, at_t], w[:, slot, j * COLS:(j + 1) * COLS],
                                         start=(kt == 0 and n == 0),
                                         stop=(last and j == ROWS_PER_CHUNK - 1 and n == 2))
                    return ins
                return chunk

            def one(phase, turn, g, k, chunk):
                buf, end, read = group_waits(phase, turn, g)
                n = COUNTS[phase][g]
                if k == 0:
                    pe.wait_ge(group_read[buf], read - 1)
                pe.wait_ge(lo_ready, end + (k + 1 - n))
                slot = slot_of(phase, turn, sum(COUNTS[phase][:g]) + k)
                chunk(buf, slot, k, k == n - 1).then_inc(mm_done, 1)

            def group(phase, turn, g, chunk):
                for k in range(COUNTS[phase][g]):
                    one(phase, turn, g, k, chunk)

            def token_sums(to, parts):
                for t in range(2):
                    for n, part in enumerate(parts):
                        ins = mm(to[:, t:t + 1], part[:, t * P:(t + 1) * P], ones[:, 0:1],
                                 start=(n == 0), stop=(n == len(parts) - 1))
                return ins

            def spread(to, diagonal):
                for t in range(2):
                    ins = mm(to[:, t * P:(t + 1) * P], ones[:], diagonal[:, t, :], start=True, stop=True)
                return ins

            pe.wait_ge(sem["ones_ready"], 1)
            for _ in range(WARM_UP):
                mm(X[:, 0, 0:P], ones[:], ones[:], start=True, stop=True)
            for c in range(16):
                one("v", 0, c // 8, c % 8, tokens(norm_in.hi, norm_in.lo, "g_lo_ready" if c < 8 else None))
                if c == 8:
                    pe.wait_ge(sem["sums_ready"], 1)
                    token_sums(X[:, 0, 0:2], [norm_in.sums[0][:, 0, :]]).then_inc(sem["stat_ready"], 1)
                if c == 11:
                    pe.wait_ge(sem["diag_ready"], 1)
                    spread(X[:, 1, 0:S], diag[0]).then_inc(sem["spread_ready"], 1)
            with pe.Fori(1, TURNS["v"]) as i:
                group("v", i, 0, tokens(norm_in.hi, norm_in.lo))
                group("v", i, 1, tokens(norm_in.hi, norm_in.lo))

            with pe.Fori(0, TURNS["ug"]) as i:
                group("ug", i, 0, features(h_hi, h_lo, "h_lo_ready"))
                pe.wait_ge(sem["ws_scaled"], i + 1)
                pe.wait_ge(sem["v_group_ready"], i + 1)
                for t in range(2):
                    for b in range(4):
                        ins = mm(SV[:, b, t * P:(t + 1) * P], v_group[:, t, b * P:(b + 1) * P],
                                 ws_scaled[:, t, :], start=True, stop=True)
                ins.then_inc(sem["sv_ready"], 1)
                group("ug", i, 1, features(h_hi, h_lo))

            with pe.Fori(0, TURNS["out1"]) as i:
                group("out1", i, 0, features(y_hi, y_lo, "y_lo_ready"))
                group("out1", i, 1, features(y_hi, y_lo))

            for c in range(32):
                one("vv", c // 16, c // 8 % 2, c % 8,
                    tokens(norm_mid.hi, norm_mid.lo, "g_lo_ready" if c < 8 else None, 4))
                if c == 7:
                    pe.wait_ge(sem["sums_ready"], 2)
                    token_sums(X[:, 0, 0:2], [norm_mid.sums[0][:, 0, :]])
                    token_sums(X[:, 0, 2:4], [norm_mid.sums[1][:, 0, :]]).then_inc(sem["stat_ready"], 1)
                if c == 11:
                    pe.wait_ge(sem["diag_ready"], 2)
                    spread(X[:, 0, 0:S], diag[0])
                    spread(X[:, 1, 0:S], diag[1]).then_inc(sem["spread_ready"], 1)

            def gate_logits():
                pe.wait_ge(sem["gw_ready"], 1)
                for kt in range(KD):
                    for n, (w, a) in enumerate(((gw_hi, h_hi), (gw_hi, h_lo), (gw_lo, h_hi))):
                        ins = mm(OUT[0:16, 0:S], w[:, kt, :], a[:, kt, :],
                                 start=(kt == 0 and n == 0), stop=(kt == KD - 1 and n == 2))
                ins.then_inc(sem["gate_z_ready"], 1)

            def gates_by_token():
                pe.wait_ge(sem["gate_z_read"], 1)
                for t in range(2):
                    ins = nc.tensor.transpose(PT[:, t * 16:(t + 1) * 16], gate_z[:, t * P:(t + 1) * P], ident[0:16, 0:16])
                ins.then_inc(sem["gz_ready"], 1)

            def running_sums():
                pe.wait_ge(sem["gl_ready"], 1)
                pe.wait_ge(sem["late_in"], 16)
                mm(OUT[:, 0:12], tri, gl[:, 0, 0:12], start=True, stop=True)
                mm(OUT[:, 16:28], ones[:], gl[:, 0, 0:12], start=True, stop=False)
                mm(OUT[:, 16:28], tri, gl[:, 1, 0:12], start=False, stop=True).then_inc(sem["cum_ready"], 1)

            def gate_rows():
                pe.wait_ge(sem["gr_ready"], 1)
                for t in range(2):
                    ins = nc.tensor.transpose(OUT[0:32, t * P:(t + 1) * P], gr[:, t, :], ident[:])
                ins.then_inc(sem["rows_t_ready"], 1)

            def q_sums(n):
                pe.wait_ge(sem["qsq_ready"], n + 1)
                if n == 0:
                    pe.wait_ge(sem["rows_ready"], 1)
                if (8 * n + 9 - HEAD_AT - 4) // 4 >= 0:
                    pe.wait_ge(sem["fox_read"], (8 * n + 9 - HEAD_AT - 4) // 4 + 1)
                for b in range(4):
                    ins = token_sums(OUT[:, 2 * b:2 * b + 2], [qsq[:, b * S:(b + 1) * S]])
                ins.then_inc(sem["q_sums_ready"], 1)

            def q_spread(n):
                pe.wait_ge(sem["q_diag_ready"], n + 1)
                if 8 * n + 13 > HEAD_AT:
                    pe.wait_ge(sem["scores_read"], (8 * n + 13 - HEAD_AT) // 4 + 1)
                for b in range(4):
                    ins = spread(X[:, b // 2, b % 2 * S:b % 2 * S + S], q_diag[:, 2 * b:2 * b + 2, :])
                ins.then_inc(sem["q_spread_ready"], 1)

            def scores(n):
                pe.wait_ge(sem["head_row_ready"], n + 1)
                if n:
                    pe.wait_ge(sem["scores_read"], n)
                if n < HEADS:
                    pe.wait_ge(sem["qk_normed"], min(4, (HEAD_AT + 4 * n - 13) // 8 + 1))
                    q, k = qk[:, n, :], qk[:, 8 + n, :]
                else:
                    buf, _, read = group_waits("side", 0, 5)
                    pe.wait_ge(group_read[buf], read)
                    q, k = qk[:, 8 + n, :], qk[:, 12 + n, :]
                pe.wait_ge(sem["ones_r_ready"], 1)
                for a, w, t in TILES:
                    ins = mm(X[:, 0, t * S:(t + 1) * S], ones_r[:], head_row[n % 2][:], start=True, stop=n >= HEADS,
                             skip_group_check=True)
                    to = X[:, 0, t * S:t * S + w] if n < HEADS else X[:, 1, a:a + w]
                    ins = mm(to, q[:, t * P:(t + 1) * P], k[:, 0:w], start=n >= HEADS, stop=True,
                             skip_group_check=True)
                ins.then_inc(sem["scores_ready"], 1)

            def transposes(n):
                pe.wait_ge(sem["probs_ready"], n + 1)
                if n:
                    pe.wait_ge(sem["probs_t_ready"], n)
                if n - HEADS >= 2:
                    pe.wait_ge(sem["m_done"], n - HEADS - 1)
                for a in range(0, 384, P):
                    ins = nc.tensor.transpose(PT[:, a:a + P], probs[:, a:a + P], ident[:])
                ins.then_inc(sem["probs_t_psum"], 1)

            def values(n):
                pe.wait_ge(sem["probs_t_ready"], n + 1)
                pe.wait_ge(sem["q_ms_ready"], min(4, (HEAD_AT + 4 + 4 * n - 9) // 8 + 1))
                if 0 < n <= HEADS:
                    pe.wait_ge(sem["fox_read"], n)
                elif n:
                    pe.wait_ge(sem["m_values_read"], n - HEADS)
                    pe.wait_ge(sem["m_ms_ready"], n - HEADS)
                for e in range(1 if n < HEADS else 2):
                    c = n * P if n < HEADS else 1024 + (n - HEADS) * S + e * P
                    mm(OUT[:, e * S:(e + 1) * S], vv[:, 0, c:c + P], probs_t[:, 0:S], start=True, stop=False)
                    ins = mm(OUT[:, e * S + P:(e + 1) * S], vv[:, 1, c:c + P], probs_t[:, S:S + P],
                             start=False, stop=True)
                ins.then_inc(sem["head_ready"], 1)

            def m_sums(m):
                pe.wait_ge(sem["m_values_read"], m + 1)
                token_sums(OUT[:, 0:2], [hm_sq[:, 0:S], hm_sq[:, S:2 * S]]).then_inc(sem["m_sums_ready"], 1)

            def m_spread(m):
                pe.wait_ge(sem["m_diag_ready"], m + 1)
                pe.wait_ge(sem["probs_t_ready"], min(HEADS + M_HEADS, HEADS + m + 2))
                spread(PT[:, 0:S], m_diag).then_inc(sem["m_spread_ready"], 1)

            side = [features(h_hi, h_lo, "h_lo_ready", 4)] + [features(h_hi, h_lo)] * 11
            for c in range(96):
                one("side", 0, c // 8, c % 8, side[c // 8])
                if c == 1:
                    gate_logits()
                if c == 2:
                    gates_by_token()
                if c == 6:
                    running_sums()
                if c == 8:
                    gate_rows()
                if c % 8 == 1 and 9 <= c <= 33:
                    q_sums(c // 8 - 1)
                if c % 8 == 5 and 13 <= c <= 37:
                    q_spread(c // 8 - 1)
                n, step = divmod(c - HEAD_AT, 4)
                if step == 0 and 0 <= n < HEADS + M_HEADS:
                    scores(n)
                if step == 3 and 0 <= n < HEADS + M_HEADS:
                    transposes(n)
                if step == 0 and 0 <= n - 1 < HEADS + M_HEADS:
                    values(n - 1)
                if step == 2 and 0 <= n - 1 - HEADS < M_HEADS:
                    m_sums(n - 1 - HEADS)
                if step == 1 and 0 <= n - 2 - HEADS < M_HEADS:
                    m_spread(n - 2 - HEADS)

            with pe.Fori(0, TURNS["merge"]) as i:
                for j in range(2):
                    group("merge", i, 3 * j, features(h_hi, h_lo))
                    group("merge", i, 3 * j + 1, features(am_hi[:, 0:8, :], am_lo[:, 0:8, :], "am_lo_ready"))
                    group("merge", i, 3 * j + 2, features(am_hi[:, 8:16, :], am_lo[:, 8:16, :], "am_lo_ready", 2))
            with pe.Fori(0, TURNS["out2"]) as i:
                group("out2", i, 0, features(g_hi, g_lo, "merged_lo_ready"))
                group("out2", i, 1, features(g_hi, g_lo))
            for c in range(16):
                one("up", 0, c // 8, c % 8,
                    features(norm_mlp.hi, norm_mlp.lo, "g_lo_ready" if c < 8 else None, 8))
                if c == 6:
                    pe.wait_ge(sem["sums_ready"], 3)
                    token_sums(X[:, 0, 0:2], [norm_mlp.sums[0][:, 0, :]]).then_inc(sem["stat_ready"], 1)
                if c == 8:
                    pe.wait_ge(sem["diag_ready"], 3)
                    spread(X[:, 1, 0:S], diag[0]).then_inc(sem["spread_ready"], 1)
            with pe.Fori(1, TURNS["up"]) as i:
                group("up", i, 0, features(norm_mlp.hi, norm_mlp.lo))
                group("up", i, 1, features(norm_mlp.hi, norm_mlp.lo))
            with pe.Fori(0, TURNS["down"]) as i:
                group("down", i, 0, features(f_hi, f_lo, "f_lo_ready"))
                group("down", i, 1, features(f_hi, f_lo))

        @block.scalar
        def _(act):
            activation = nc.scalar.activation
            steps = Steps(act, sem["act_step"])

            def split(phase, turn, k):
                now = chunk_of(phase, turn, k)
                if isinstance(now, int) and now + RING >= CHUNKS:
                    return
                slot = slot_of(phase, turn, k)
                if isinstance(turn, int):
                    act.wait_ge(raw_full[slot], 16 * (now // RING + 2))
                else:
                    act.wait_ge(raw_full[slot], turn * (16 * sum(COUNTS[phase]) // RING)
                                + 16 * ((FIRST_CHUNK[phase] + k) // RING + 2))
                act.wait_ge(mm_done, now + 1)
                activation(w_hi[:, slot, :], raw[:, slot, :], ACT.Copy).then_inc(hi_ready, 1)

            def splits(phase, turn, g):
                for k in range(COUNTS[phase][g]):
                    split(phase, turn, sum(COUNTS[phase][:g]) + k)

            def done(phase, turn, g):
                buf, end, read = group_waits(phase, turn, g)
                act.wait_ge(mm_done, end)
                return G[buf], group_read[buf], read

            def high(to, of, count, value, after, **kw):
                act.wait_ge(sem[count], value)
                activation(to, of, ACT.Copy, **kw).then_inc(sem[after], 1)

            def high_h(q, before):
                high(h_hi[:, 4 * q:4 * q + 4, :], normed[q % 2][:], "norm_ready", before + q + 1, "h_hi_ready")

            def squares(norm, q, n):
                to = (norm.squares if q else norm.sums)[n]
                if n == 0:
                    ins = activation(to[:], xres[:, 4 * q:4 * q + 4, :], ACT.Square)
                else:
                    for b in range(4):
                        ins = activation(to[:, b, :], xres[:, 4 * q + b, :], ACT.Square,
                                         scale=param("final_norm", 4 * q + b))
                ins.then_inc(sem["sq_ready"], 1)

            def gained_high(norm, q, blocks=range(4)):
                for b in blocks:
                    ins = activation(norm.hi[:, 4 * q + b, :], xres[:, 4 * q + b, :], ACT.Copy, scale=norm.gain(4 * q + b))
                ins.then_inc(sem["g_hi_ready"], 1)

            def high_of_first(q):
                act.wait_ge(raw_full[q], 16)
                activation(w_hi[:, q, :], raw[:, q, :], ACT.Copy).then_inc(hi_ready, 1)

            load_x(act, 0)
            act.wait_ge(sem["minus_half_ready"], 1)
            activation(v_stat[:], minus_half[:], ACT.Copy).then_inc(sem["tables_in"], 1)
            act.wait_ge(sem["params_in"], 16)
            act.wait_ge(sem["x_in0"], 16)
            gained_high(norm_in, 0)
            high_of_first(0)
            high_of_first(1)
            act.wait_ge(sem["x_in1"], 16)
            gained_high(norm_in, 1)
            high_of_first(2)
            high_of_first(3)
            act.wait_ge(sem["x_in2"], 16)
            gained_high(norm_in, 2)

            def v_out(turn, g):
                product, read, _ = done("v", turn, g)
                for t in range(2):
                    at_v = (v_all[:, t, (2 * turn + g) * COLS:(2 * turn + g + 1) * COLS] if isinstance(turn, int) else
                            v_all[:, t, bass.ds(turn * (2 * COLS) + g * COLS, COLS)])
                    ins = activation(at_v, product[:, t * COLS:(t + 1) * COLS], ACT.Gelu_apprx_tanh,
                                     scale=n_rstd[:, t:t + 1])
                ins.then_inc(read, 1)

            for c in range(16):
                split("v", 0, c)
                if c == 0:
                    act.wait_ge(sem["x_in3"], 16)
                    gained_high(norm_in, 3)
                if c == 1:
                    act.dma_start(ident[:], identity).then_inc(sem["ident_in"], 16)
                if c == 6:
                    act.dma_start(ws_t[:], w_s).then_inc(sem["ws_in"], 16)
                    act.dma_start(bs_b[:], b_s).then_inc(sem["bs_in"], 16)
                if 1 <= c < 5:
                    if c >= 3:
                        act.wait_ge(sem["sq_added"], c - 2)
                    squares(norm_in, c - 1, 0)
                if c == 10:
                    act.wait_ge(sem["rstd_ready"], 1)
                    v_out(0, 0)
                if c in (12, 14):
                    high_h((c - 12) // 2, 0)
            v_out(0, 1)
            high_h(2, 0)
            high_h(3, 0)
            with act.Fori(1, TURNS["v"]) as i:
                for g in range(2):
                    splits("v", i, g)
                    v_out(i, g)
            for buf in range(2):
                act.wait_ge(group_read[buf], 1 + TURNS["v"])
            activation(y_hi[:, 0:16, :], v_all[:, 0, :], ACT.Square,
                       accum_out=v_stat[:, 0:1]).then_inc(sem["v_sq_ready"], 1)

            with act.Fori(0, TURNS["ug"]) as i:
                splits("ug", i, 0)
                product, read, _ = done("ug", i, 0)
                activation(u_act[:], product[:], ACT.Gelu_apprx_tanh).then_inc(read, 1)
                splits("ug", i, 1)
                product, read, _ = done("ug", i, 1)
                activation(t2[:], product[:], ACT.Tanh, scale=0.5).then_inc(sem["gate_t_ready"], 1)
                high(y_hi[:, bass.ds(i * 4, 4), :], t1[:], "y_ready", i + 1, "y_hi_ready")

            act.wait_ge(sem["y_lo_ready"], GROUPS)
            act.dma_start(xres[:], x).then_inc(sem["x_again"], 16)
            act.dma_start(gw_raw[:], gate_w).then_inc(sem["gw_in"], 16)
            act.dma_start(late[:], consts).then_inc(sem["late_in"], 16)

            def residual(phase, q, k, norm, n_squares):
                if k == 1:
                    buf, _, read = group_waits(phase, q // 2, q % 2)
                    act.wait_ge(group_read[buf], read)
                    gained_high(norm, q)
                if 2 <= k < 2 + n_squares:
                    squares(norm, q, k - 2)

            for c in range(64):
                split("out1", 0, c)
                if c >= 16:
                    residual("out1", c // 16 - 1, c % 16, norm_mid, 2)

            for c in range(32):
                split("vv", c // 16, c % 16)
                if c < 8:
                    residual("out1", 3, c, norm_mid, 2)
                if c in VV_OUT:
                    group = VV_OUT.index(c)
                    product, read, _ = done("vv", group // 2, group % 2)
                    if c == VV_OUT[0]:
                        act.wait_ge(sem["rstd_both_ready"], 1)
                    for t in range(2):
                        ins = activation(vv[:, t, group * COLS:(group + 1) * COLS],
                                         product[:, t * COLS:(t + 1) * COLS], ACT.Copy, scale=n_rstd[:, 4 + t:5 + t])
                    ins.then_inc(read, 1)
                if c in (12, 14, 16, 18):
                    high_h((c - 12) // 2, 4)

            side_out = ([(qk, 4 * b, ACT.Copy, 1.0) for b in (0, 2, 1, 3, 4, 5)]
                        + [(mo, 4 * b, ACT.Tanh, 0.5) for b in range(2)] + [(ga, 4 * b, ACT.Tanh, 0.5) for b in range(4)])
            for c in range(96):
                split("side", 0, c)
                if c == 0:
                    act.wait_ge(sem["gw_in"], 16)
                    activation(gw_hi[:], gw_raw[:], ACT.Copy).then_inc(sem["gw_hi_ready"], 1)
                if c == 1:
                    act.wait_ge(sem["gate_z_ready"], 1)
                    activation(gate_z[:], OUT[0:16, 0:S], ACT.Copy).then_inc(sem["gate_z_read"], 1)
                    activation(ones_r[:], ones[0:64, :], ACT.Copy).then_inc(sem["ones_r_ready"], 1)
                if c == 3:
                    act.wait_ge(sem["gn_ready"], 1)
                    steps.link(activation(gl[:], gn[:], ACT.Exp))
                    activation(gl[:], gl[:], ACT.Ln, bias=1.0).then_inc(sem["ln_ready"], 1)
                if c == 8:
                    act.wait_ge(sem["rows_t_ready"], 1)
                    activation(rows_split[0:32, :], OUT[0:32, 0:S], ACT.Copy).then_inc(sem["rows_hi_ready"], 1)
                if c % 8 == 7:
                    product, read, _ = done("side", 0, c // 8)
                    to, b, func, scale = side_out[c // 8]
                    activation(to[:, b:b + 4, :], product[:], func, scale=scale).then_inc(read, 1)
                if c % 8 == 0 and 8 <= c <= 32:
                    n = c // 8 - 1
                    buf, _, read = group_waits("side", 0, n)
                    act.wait_ge(group_read[buf], read)
                    if n:
                        act.wait_ge(sem["q_sums_ready"], n)
                    b = side_out[n][1]
                    activation(qsq[:], qk[:, b:b + 4, :], ACT.Square).then_inc(sem["qsq_ready"], 1)
                n, step = divmod(c - HEAD_AT, 4)
                if step == 1 and 0 <= n < HEADS + M_HEADS:
                    act.wait_ge(sem["max_ready"], n + 1)
                    if n:
                        act.wait_ge(sem["probs_t_psum"], n)
                    for a, w, t in TILES:
                        ins = activation(probs[:, a:a + w], logits[:, a:a + w], ACT.Exp, bias=col[:, 2 + t:3 + t],
                                         accum_out=col[:, 4 + t:5 + t] if n < HEADS else None)
                    if n >= HEADS:
                        ins = activation(col[:, 6:8], col[:, 8:10], ACT.Exp)
                    ins.then_inc(sem["exp_ready"], 1)
                if step == 3 and 0 <= n < HEADS + M_HEADS:
                    act.wait_ge(sem["probs_t_psum"], n + 1)
                    if n:
                        act.wait_ge(sem["head_ready"], n)
                    activation(probs_t[:], PT[:, 0:384], ACT.Copy).then_inc(sem["probs_t_ready"], 1)
                if step == 0 and 0 <= n - 1 < HEADS + M_HEADS:
                    n -= 1
                    act.wait_ge(sem["head_ready"], n + 1)
                    if n < HEADS:
                        activation(am[:, n, :], OUT[:, 0:S], ACT.Copy).then_inc(sem["fox_read"], 1)
                    else:
                        if n > HEADS:
                            act.wait_ge(sem["m_sums_ready"], n - HEADS)
                        activation(hm_sq[:], OUT[:], ACT.Square).then_inc(sem["hm_sq_ready"], 1)
                if c in AM_SPLITS:
                    q = AM_SPLITS.index(c)
                    act.wait_ge(sem["m_done"], M_HEADS)
                    activation(am_hi[:, 4 * q:4 * q + 4, :], am[:, 4 * q:4 * q + 4, :],
                               ACT.Copy).then_inc(sem["am_hi_ready"], 1)

            with act.Fori(0, TURNS["merge"]) as i:
                for j in range(2):
                    splits("merge", i, 3 * j)
                    product, read, _ = done("merge", i, 3 * j)
                    activation(gate_m[:], product[:], ACT.Tanh, scale=0.5).then_inc(read, 1)
                    splits("merge", i, 3 * j + 1)
                    splits("merge", i, 3 * j + 2)
                    high(g_hi[:, bass.ds(i * 8 + 4 * j, 4), :], gate_a[:], "merged_ready", i * 2 + (j + 1),
                         "merged_hi_ready", scale=0.5)
            for c in range(32):
                split("out2", 0, c)
                if c >= 8:
                    residual("out2", c // 8 - 1, c % 8, norm_mlp, 1)

            def conv_start(turn, g, to):
                product = G[g]
                act.wait_ge(sem[("scaled_g_ready", "scaled_v_ready")[g]], turn + 1)
                for b in range(4):
                    k = turn * 4 + (b + g * KF)
                    ins = activation(to[:, b, :], product[:, b * S:(b + 1) * S], ACT.Identity,
                                     scale=param("conv2", k), bias=param("conv_b", k))
                ins.then_inc(sem[("conv_g_started", "conv_v_started")[g]], 1)

            def gate_tanh(turn):
                act.wait_ge(sem["cg_ready"], turn + 1)
                activation(silu_t[:], cg[:], ACT.Tanh, scale=0.5).then_inc(sem["silu_t_ready"], 1)

            def f_high(turn):
                high(f_hi[:, bass.ds(turn * 4, 4), :], cv[:], "f_ready", turn + 1, "f_hi_ready")

            for c in range(16):
                split("up", 0, c)
                if c < 8:
                    residual("out2", 3, c, norm_mlp, 1)
                if c == 10:
                    conv_start(0, 0, cg)
                if c == 12:
                    gate_tanh(0)
            with act.Fori(1, TURNS["up"]) as i:
                for k in range(16):
                    split("up", i, k)
                    if k == 1:
                        conv_start(i - 1, 1, cv)
                    if k == 4:
                        f_high(i - 1)
                    if k == 9:
                        conv_start(i, 0, cg)
                    if k == 11:
                        gate_tanh(i)
            for i in range(TURNS["down"]):
                for k in range(44):
                    split("down", i, k)
                    if i == 0 and k == 1:
                        conv_start(TURNS["up"] - 1, 1, cv)
                    if i == 0 and k == 4:
                        f_high(TURNS["up"] - 1)
                    if k == 23 or i and k == 1:
                        q = 2 * i + k // 22 - 1
                        buf, _, read = group_waits("down", q // 2, q % 2)
                        act.wait_ge(group_read[buf], read)
                        store(act, 4 * q, 4)
            buf, _, read = group_waits("down", 1, 1)
            act.wait_ge(group_read[buf], read)
            store(act, 14, 2)

        @block.vector
        def _(dve):
            v = nc.vector
            steps = Steps(dve, sem["dve_step"])
            link = steps.link

            def split(phase, turn, k):
                now = chunk_of(phase, turn, k)
                if isinstance(now, int) and now + RING >= CHUNKS:
                    return
                low_of_chunk(slot_of(phase, turn, k), now + (RING + 1))

            def low_of_chunk(slot, count):
                dve.wait_ge(hi_ready, count)
                v.tensor_tensor(w_lo[:, slot, :], raw[:, slot, :], w_hi[:, slot, :].bitcast(F32),
                                ALU.subtract).then_inc(lo_ready, 1)

            def splits(phase, turn, g):
                for k in range(COUNTS[phase][g]):
                    split(phase, turn, sum(COUNTS[phase][:g]) + k)

            def done(phase, turn, g):
                buf, end, read = group_waits(phase, turn, g)
                dve.wait_ge(mm_done, end)
                return G[buf], group_read[buf], read

            def low(to, of, hi, count, value, after):
                dve.wait_ge(sem[count], value)
                return v.tensor_tensor(to, of, hi.bitcast(F32), ALU.subtract).then_inc(sem[after], 1)

            def mean_square(to, of, n):
                return v.tensor_scalar(to, of, 1.0 / n, EPS, ALU.mult, ALU.add)

            def diagonals(to, rstd):
                for t in range(2):
                    ins = v.tensor_scalar(to[:, t, :], ident[:], rstd[:, t:t + 1], None, ALU.mult)
                return ins

            def gained_low(norm, q, before):
                dve.wait_ge(sem["g_hi_ready"], before + q + 1)
                for b in range(4):
                    k = 4 * q + b
                    ins = v.scalar_tensor_tensor(norm.lo[:, k, :], xres[:, k, :], norm.gain(k),
                                                 norm.hi[:, k, :].bitcast(F32), ALU.mult, ALU.subtract)
                ins.then_inc(sem["g_lo_ready"], 1)

            def fold(sums):
                link(v.tensor_tensor(sums[:, 0:2, :], sums[:, 0:2, :], sums[:, 2:4, :], ALU.add))
                link(v.tensor_tensor(sums[:, 0, :], sums[:, 0, :], sums[:, 1, :], ALU.add))

            def normalise(q, gain, scale, before):
                if q >= 2:
                    dve.wait_ge(sem["h_lo_ready"], before + q - 1)
                for b in range(4):
                    ins = v.scalar_tensor_tensor(normed[q % 2][:, b, :], xres[:, 4 * q + b, :], gain(4 * q + b), scale,
                                                 ALU.mult, ALU.mult)
                ins.then_inc(sem["norm_ready"], 1)

            def low_h(q, before):
                low(h_lo[:, 4 * q:4 * q + 4, :], normed[q % 2][:], h_hi[:, 4 * q:4 * q + 4, :],
                    "h_hi_ready", before + q + 1, "h_lo_ready")

            v.memset(ones[:], 1.0).then_inc(sem["ones_ready"], 1)
            v.memset(minus_half[:], -0.5).then_inc(sem["minus_half_ready"], 1)
            for buf in range(2):
                dve.sem_inc(group_read[buf], 1)
            dve.wait_ge(sem["params_in"], 16)
            link(v.tensor_tensor(gains[:], param("final_norm", 0, KD), param("norm1", 0, KD), ALU.mult))
            link(v.tensor_scalar(q_gain[:], param("q_norm"), float(P) ** -0.5, None, ALU.mult))
            link(v.tensor_scalar(m_gain[:], param("m_norm", 0, 2 * M_HEADS), 0.5, None, ALU.mult))

            gained_low(norm_in, 0, 0)
            low_of_chunk(0, 1)
            low_of_chunk(1, 2)
            gained_low(norm_in, 1, 0)
            low_of_chunk(2, 3)
            low_of_chunk(3, 4)
            gained_low(norm_in, 2, 0)
            for c in range(16):
                split("v", 0, c)
                if c == 0:
                    gained_low(norm_in, 3, 0)
                if 2 <= c < 5:
                    dve.wait_ge(sem["sq_ready"], c)
                    if c > 2:
                        dve.wait_ge(sem["sq_added"], c - 2)
                    v.tensor_tensor(norm_in.sums[0][:], norm_in.sums[0][:], norm_in.squares[0][:],
                                    ALU.add).then_inc(sem["sq_added"], 1)
                if c == 4:
                    dve.wait_ge(sem["sq_added"], 3)
                    fold(norm_in.sums[0])
                    dve.sem_inc(sem["sums_ready"], 1)
                if c == 8:
                    dve.wait_ge(sem["stat_ready"], 1)
                    mean_square(n_ms[:, 0:2], X[:, 0, 0:2], D).then_inc(sem["ms_ready"], 1)
                if c == 9:
                    dve.wait_ge(sem["rstd_ready"], 1)
                    dve.wait_ge(sem["ident_in"], 16)
                    diagonals(diag[0], n_rstd[:, 0:2]).then_inc(sem["diag_ready"], 1)
                if c in (13, 15):
                    low_h((c - 13) // 2, 0)
                if c in (11, 13, 15):
                    if c == 11:
                        dve.wait_ge(sem["spread_ready"], 1)
                    normalise((c - 11) // 2, norm_in.gain, X[:, 1, 0:S], 0)
            normalise(3, norm_in.gain, X[:, 1, 0:S], 0)
            low_h(2, 0)
            low_h(3, 0)
            with dve.Fori(1, TURNS["v"]) as i:
                splits("v", i, 0)
                splits("v", i, 1)
            for buf in range(2):
                dve.wait_ge(group_read[buf], 1 + TURNS["v"])
            dve.wait_ge(sem["h_lo_ready"], 4)
            link(v.tensor_tensor_reduce(y_lo[:, 0:16, :].rearrange("p a b -> p (a b)"), v_all[:, 1, :],
                                        v_all[:, 1, :], scale=1.0, scalar=0.0, op0=ALU.mult, op1=ALU.add,
                                        accum_out=v_stat[:, 1:2]))
            dve.wait_ge(sem["v_sq_ready"], 1)
            mean_square(v_stat[:, 2:4], v_stat[:, 0:2], E).then_inc(sem["v_ms_ready"], 1)
            dve.wait_ge(sem["v_rstd_ready"], 1)
            dve.wait_ge(sem["ws_in"], 16)
            dve.wait_ge(sem["bs_in"], 16)

            with dve.Fori(0, TURNS["ug"]) as i:
                steps.enter(i, 2)
                for k in range(16):
                    split("ug", i, k)
                    if k == 3:
                        for t in range(2):
                            ins = v.tensor_scalar(ws_scaled[:, t, :],
                                                  ws_t[:, bass.ds(i, 1), :].rearrange("p a b -> p (a b)"),
                                                  v_stat[:, 4 + t:5 + t], None, ALU.mult)
                        ins.then_inc(sem["ws_scaled"], 1)
                    if k == 9:
                        dve.wait_ge(sem["sv_ready"], i + 1)
                        bias = bs_b[:, bass.ds(i, 1), :].rearrange("p a b -> p (a b)")
                        for b in range(4):
                            for t in range(2):
                                ins = v.scalar_tensor_tensor(t1[:, b, t * P:(t + 1) * P], SV[:, b, t * P:(t + 1) * P],
                                                             param("v_gain", i * 4 + b), bias, ALU.mult, ALU.add)
                        link(ins)
                    if k == 11:
                        _, _, read = group_waits("ug", i, 0)
                        dve.wait_ge(group_read[0], read)
                        link(v.tensor_tensor(t1[:], t1[:], u_act[:], ALU.mult))
                product, gate_read, read = done("ug", i, 1)
                dve.wait_ge(sem["gate_t_ready"], i + 1)
                v.scalar_tensor_tensor(t2[:].rearrange("p a b -> p (a b)"), t2[:].rearrange("p a b -> p (a b)"), 1.0,
                                       product[:], ALU.add, ALU.mult).then_inc(gate_read, 1)
                dve.wait_ge(gate_read, read)
                v.scalar_tensor_tensor(t1[:], t1[:], 0.5, t2[:], ALU.mult, ALU.mult).then_inc(sem["y_ready"], 1)
                low(y_lo[:, bass.ds(i * 4, 4), :], t1[:], y_hi[:, bass.ds(i * 4, 4), :], "y_hi_ready", i + 1,
                    "y_lo_ready")
                dve.wait_ge(sem["y_lo_ready"], i + 1)
                steps.leave(TURNS["ug"])

            def residual(phase, q, k, norm, before, sq_before, n_squares):
                if k == 0:
                    product, read, value = done(phase, q // 2, q % 2)
                    at_x = xres[:, 4 * q:4 * q + 4, :]
                    v.tensor_tensor(at_x, product[:].rearrange("p (b s) -> p b s", b=4), at_x,
                                    ALU.add).then_inc(read, 1)
                    dve.wait_ge(read, value)
                if k == 2:
                    gained_low(norm, q, before)
                if k == 4:
                    dve.wait_ge(sem["sq_ready"], sq_before + (q + 1) * n_squares)
                    for n in range(n_squares if q else 0):
                        link(v.tensor_tensor(norm.sums[n][:], norm.sums[n][:], norm.squares[n][:], ALU.add))
                    if q == 3:
                        for n in range(n_squares):
                            fold(norm.sums[n])
                        dve.sem_inc(sem["sums_ready"], 1)

            for c in range(64):
                split("out1", 0, c)
                if c == 16:
                    dve.wait_ge(sem["x_again"], 16)
                if c >= 16:
                    residual("out1", c // 16 - 1, c % 16, norm_mid, 4, 4, 2)

            for c in range(32):
                split("vv", c // 16, c % 16)
                if c < 8:
                    residual("out1", 3, c, norm_mid, 4, 4, 2)
                if c == 7:
                    dve.wait_ge(sem["stat_ready"], 2)
                    mean_square(n_ms[:, 0:2], X[:, 0, 0:2], D).then_inc(sem["ms_ready"], 1)
                if c == 8:
                    dve.wait_ge(sem["rstd_ready"], 2)
                    link(v.tensor_tensor(n_ms[:, 4:6], n_rstd[:, 0:2], n_rstd[:, 0:2], ALU.mult))
                    link(v.scalar_tensor_tensor(n_ms[:, 6:8], X[:, 0, 2:4], 1.0 / D, n_ms[:, 4:6], ALU.mult, ALU.mult))
                    v.tensor_scalar(n_ms[:, 2:4], n_ms[:, 6:8], EPS, None, ALU.add).then_inc(sem["ms_ready"], 1)
                if c == 9:
                    dve.wait_ge(sem["rstd_ready"], 3)
                    v.tensor_tensor(n_rstd[:, 4:6], n_rstd[:, 0:2], n_rstd[:, 2:4], ALU.mult).then_inc(
                        sem["rstd_both_ready"], 1)
                    dve.wait_ge(sem["rstd_both_ready"], 1)
                    diagonals(diag[0], n_rstd[:, 4:6])
                    diagonals(diag[1], n_rstd[:, 0:2]).then_inc(sem["diag_ready"], 1)
                if c in (13, 15, 17, 19):
                    low_h((c - 13) // 2, 4)
                if c in (11, 13, 15, 17):
                    if c == 11:
                        dve.wait_ge(sem["spread_ready"], 2)
                    normalise((c - 11) // 2, norm_mid.gain, X[:, 0, 0:S], 4)
                if c in (20, 22, 24, 26):
                    for b in range(4):
                        k = 2 * (c - 20) + b
                        ins = v.scalar_tensor_tensor(xres[:, k, :], xres[:, k, :], param("final_norm", k),
                                                     X[:, 1, 0:S], ALU.mult, ALU.mult)
                    link(ins)

            def row(n):
                v.tensor_scalar(head_row[n % 2][:], rows_split[:].bitcast(F32), head_pick[:, n:n + 1], None, ALU.mult).then_inc(
                    sem["head_row_ready"], 1)

            for c in range(96):
                split("side", 0, c)
                if c == 0:
                    low(gw_lo[:].rearrange("p a b -> p (a b)"), gw_raw[:], gw_hi[:].rearrange("p a b -> p (a b)"),
                        "gw_hi_ready", 1, "gw_ready")
                if c == 2:
                    dve.wait_ge(sem["gz_ready"], 1)
                    for t in range(2):
                        ins = v.tensor_tensor(gz[:, t, :], PT[:, t * 16:(t + 1) * 16], param("gate_bias", 0, 16), ALU.add)
                    link(ins)
                    v.scalar_tensor_tensor(gn[:], gz[:], -1.0, gz[:], ALU.mult, ALU.min).then_inc(sem["gn_ready"], 1)
                if c == 5:
                    dve.wait_ge(sem["ln_ready"], 1)
                    v.scalar_tensor_tensor(gl[:], gz[:], 0.0, gl[:], ALU.min, ALU.subtract).then_inc(sem["gl_ready"], 1)
                if c == 7:
                    dve.wait_ge(sem["cum_ready"], 1)
                    cum = OUT[:, 0:32].rearrange("p (t c) -> p t c", t=2)
                    v.tensor_scalar(gr[:, :, 0:8], cum[:, :, 0:8], -1.0, None, ALU.mult)
                    v.tensor_copy(b_cum[:], cum[:, :, 8:12])
                    v.tensor_copy(gr[:, :, 12:16], gz[:, :, 12:16])
                    v.tensor_tensor(gr[:, :, 8:12], gz[:, :, 12:16], cum[:, :, 8:12],
                                    ALU.subtract).then_inc(sem["gr_ready"], 1)
                if c == 3:
                    v.memset(gr[:, :, 16:32], 0.0)
                    v.tensor_tensor(head_pick[:], ident[0:64, 0:16], ident[0:64, 32:48], ALU.add)
                if c == 8:
                    low(rows_split[32:64, :], OUT[0:32, 0:S], rows_split[0:32, :], "rows_hi_ready", 1, "rows_ready")
                if c == 10:
                    dve.wait_ge(sem["rows_ready"], 1)
                    dve.wait_ge(sem["late_in"], 16)
                    row(0)
                    row(1)
                if c % 8 == 1 and 9 <= c <= 33:
                    dve.wait_ge(sem["q_sums_ready"], c // 8)
                    mean_square(q_ms[:], OUT[:, 0:8], P).then_inc(sem["q_ms_ready"], 1)
                if c % 8 == 2 and 10 <= c <= 34:
                    n = c // 8 - 1
                    dve.wait_ge(sem["q_rstd_ready"], n + 1)
                    for k in range(8):
                        ins = v.tensor_scalar(q_diag[:, k, :], ident[:], q_rstd[:, k:k + 1], None, ALU.mult)
                    ins.then_inc(sem["q_diag_ready"], 1)
                if c % 8 == 5 and 13 <= c <= 37:
                    n = c // 8 - 1
                    dve.wait_ge(sem["q_spread_ready"], n + 1)
                    at_q = qk[:, 4 * (0, 2, 1, 3)[n]:4 * (0, 2, 1, 3)[n] + 4, :].rearrange("p a b -> p (a b)")
                    gain = q_gain[:, 0:1] if n % 2 == 0 else param("k_norm")
                    v.scalar_tensor_tensor(at_q, at_q, gain, X[:].rearrange("p a b -> p (a b)"),
                                           ALU.mult, ALU.mult).then_inc(sem["qk_normed"], 1)
                n, step = divmod(c - HEAD_AT, 4)
                if step == 0 and 0 <= n < HEADS + M_HEADS:
                    dve.wait_ge(sem["scores_ready"], n + 1)
                    if n:
                        dve.wait_ge(sem["exp_ready"], n)
                        dve.wait_ge(sem["probs_ready"], n)
                    for a, w, t in TILES:
                        ins = v.tensor_tensor_reduce(logits[:, a:a + w], X[:, 0, t * S:t * S + w], mask[:, S - w:S],
                                                     scale=1.0, scalar=-3e38, op0=ALU.add, op1=ALU.max,
                                                     accum_out=col[:, t:t + 1])
                    if n < HEADS:
                        ins.then_inc(sem["scores_read"], 1)
                        dve.wait_ge(sem["scores_read"], n + 1)
                        v.tensor_scalar(col[:, 2:4], col[:, 0:2], -1.0, None, ALU.mult).then_inc(sem["max_ready"], 1)
                    else:
                        link(ins)
                        link(v.tensor_scalar(col[:, 2:4], col[:, 0:2], -1.0, 0.0, ALU.mult, ALU.min))
                        v.tensor_tensor(col[:, 8:10], col[:, 2:4], b_cum[:, :, n - HEADS], ALU.subtract).then_inc(
                            sem["max_ready"], 1)
                    if n + 2 < HEADS + M_HEADS:
                        row(n + 2)
                if step == 1 and 0 <= n < HEADS + M_HEADS:
                    dve.wait_ge(sem["exp_ready"], n + 1)
                    if n < HEADS:
                        link(v.reciprocal(col[:, 10:12], col[:, 4:6]))
                    else:
                        for a, w, t in TILES:
                            ins = v.tensor_tensor_reduce(probs[:, a:a + w], X[:, 1, a:a + w], probs[:, a:a + w],
                                                         scale=float(P) ** -0.5, scalar=0.0, op0=ALU.mult,
                                                         op1=ALU.add, accum_out=col[:, 4 + t:5 + t])
                        ins.then_inc(sem["scores_read"], 1)
                        dve.wait_ge(sem["scores_read"], n + 1)
                        link(v.scalar_tensor_tensor(col[:, 0:2], col[:, 4:6], -1.0, col[:, 4:6], ALU.mult, ALU.max))
                        link(v.tensor_tensor(col[:, 0:2], col[:, 0:2], col[:, 6:8], ALU.max))
                        link(v.reciprocal(col[:, 10:12], col[:, 0:2]))
                    for a, w, t in TILES:
                        ins = v.tensor_scalar(probs[:, a:a + w], probs[:, a:a + w], col[:, 10 + t:11 + t], None, ALU.mult)
                    ins.then_inc(sem["probs_ready"], 1)
                m = n - 1 - HEADS
                if step == 0 and 0 <= m < M_HEADS:
                    dve.wait_ge(sem["hm_sq_ready"], m + 1)
                    buf, _, read = group_waits("side", 0, 6 + m // 2)
                    dve.wait_ge(group_read[buf], read)
                    gate = mo[:, 2 * m:2 * m + 2, :].rearrange("p a b -> p (a b)")
                    if m >= 2:
                        dve.wait_ge(sem["m_done"], m - 1)
                    v.scalar_tensor_tensor(hm_pair[m % 2][:], gate, 1.0, OUT[:], ALU.add, ALU.mult).then_inc(
                        sem["m_values_read"], 1)
                if step == 2 and 0 <= m < M_HEADS:
                    dve.wait_ge(sem["m_sums_ready"], m + 1)
                    mean_square(m_ms[:], OUT[:, 0:2], 2 * P).then_inc(sem["m_ms_ready"], 1)
                if step == 3 and 0 <= m < M_HEADS:
                    dve.wait_ge(sem["m_rstd_ready"], m + 1)
                    if m:
                        dve.wait_ge(sem["m_spread_ready"], m)
                    diagonals(m_diag, m_rstd).then_inc(sem["m_diag_ready"], 1)
                m = n - 2 - HEADS
                if step == 1 and 0 <= m < M_HEADS:
                    dve.wait_ge(sem["m_spread_ready"], m + 1)
                    for e in range(2):
                        ins = v.scalar_tensor_tensor(am[:, 8 + 2 * m + e, :], hm_pair[m % 2][:, e * S:(e + 1) * S],
                                                     m_gain[:, 2 * m + e:2 * m + e + 1], PT[:, 0:S], ALU.mult, ALU.mult)
                    ins.then_inc(sem["m_done"], 1)
                if c in AM_SPLITS:
                    q = AM_SPLITS.index(c)
                    low(am_lo[:, 4 * q:4 * q + 4, :], am[:, 4 * q:4 * q + 4, :], am_hi[:, 4 * q:4 * q + 4, :],
                        "am_hi_ready", q + 1, "am_lo_ready")

            with dve.Fori(0, TURNS["merge"]) as i:
                for j in range(2):
                    flat = [gate[:].rearrange("p a b -> p (a b)") for gate in (gate_a, gate_m)]
                    splits("merge", i, 3 * j)
                    splits("merge", i, 3 * j + 1)
                    product, read_a, read = done("merge", i, 3 * j + 1)
                    at_g = bass.ds(i * 8 + 4 * j, 4)
                    v.scalar_tensor_tensor(gate_a[:], ga[:, at_g, :], 1.0, product[:].rearrange("p (b s) -> p b s", b=4),
                                           ALU.add, ALU.mult).then_inc(read_a, 1)
                    dve.wait_ge(read_a, read)
                    splits("merge", i, 3 * j + 2)
                    buf, _, read = group_waits("merge", i, 3 * j)
                    dve.wait_ge(group_read[buf], read)
                    product, read_m, read = done("merge", i, 3 * j + 2)
                    v.scalar_tensor_tensor(flat[1], flat[1], 1.0, product[:], ALU.add, ALU.mult).then_inc(read_m, 1)
                    dve.wait_ge(read_m, read)
                    v.tensor_tensor(gate_a[:], gate_a[:], gate_m[:], ALU.add).then_inc(sem["merged_ready"], 1)
                    count = i * 2 + (j + 1)
                    dve.wait_ge(sem["merged_hi_ready"], count)
                    v.scalar_tensor_tensor(g_lo[:, at_g, :], gate_a[:], 0.5, g_hi[:, at_g, :].bitcast(F32),
                                           ALU.mult, ALU.subtract).then_inc(sem["merged_lo_ready"], 1)
                    dve.wait_ge(sem["merged_lo_ready"], count)

            for c in range(32):
                split("out2", 0, c)
                if c >= 8:
                    residual("out2", c // 8 - 1, c % 8, norm_mlp, 8, 12, 1)

            def scaled(turn, g):
                product, _, _ = done("up", turn, g)
                for b in range(4):
                    at_b = product[:, b * S:(b + 1) * S]
                    ins = v.tensor_tensor(at_b, at_b, r_sbuf[:], ALU.mult)
                ins.then_inc(sem[("scaled_g_ready", "scaled_v_ready")[g]], 1)

            def conv_taps(turn, g, to):
                _, _, value = group_waits("up", turn, g)
                product, read = G[g], group_read[g]
                dve.wait_ge(sem[("conv_g_started", "conv_v_started")[g]], turn + 1)
                for tap, late_by in (("conv1", 1), ("conv0", 2)):
                    for b in range(4):
                        ins = v.scalar_tensor_tensor(to[:, b, late_by:S], product[:, b * S:(b + 1) * S - late_by],
                                                     param(tap, turn * 4 + (b + g * KF)), to[:, b, late_by:S],
                                                     ALU.mult, ALU.add)
                    if late_by == 1:
                        link(ins)
                ins.then_inc(read, 1)
                dve.wait_ge(read, value)
                if g == 0:
                    dve.sem_inc(sem["cg_ready"], 1)

            def silu_times(turn):
                dve.wait_ge(sem["silu_t_ready"], turn + 1)
                link(v.scalar_tensor_tensor(cg[:], silu_t[:], 1.0, cg[:], ALU.add, ALU.mult))

            def f_product():
                v.scalar_tensor_tensor(cv[:], cv[:], 0.5, cg[:], ALU.mult, ALU.mult).then_inc(sem["f_ready"], 1)

            def f_low(turn):
                at_f = bass.ds(turn * 4, 4)
                low(f_lo[:, at_f, :], cv[:], f_hi[:, at_f, :], "f_hi_ready", turn + 1, "f_lo_ready")

            for c in range(16):
                split("up", 0, c)
                if c < 8:
                    residual("out2", 3, c, norm_mlp, 8, 12, 1)
                if c == 6:
                    dve.wait_ge(sem["stat_ready"], 3)
                    mean_square(n_ms[:, 0:2], X[:, 0, 0:2], D).then_inc(sem["ms_ready"], 1)
                if c == 7:
                    dve.wait_ge(sem["rstd_ready"], 4)
                    diagonals(diag[0], n_rstd[:, 0:2]).then_inc(sem["diag_ready"], 1)
                if c == 9:
                    dve.wait_ge(sem["spread_ready"], 3)
                    link(v.tensor_copy(r_sbuf[:], X[:, 1, 0:S]))
                    scaled(0, 0)
                if c == 11:
                    conv_taps(0, 0, cg)
                if c == 13:
                    silu_times(0)
            with dve.Fori(1, TURNS["up"]) as i:
                steps.enter(i, 3, 1)
                for k in range(16):
                    split("up", i, k)
                    if k == 0:
                        scaled(i - 1, 1)
                    if k == 2:
                        conv_taps(i - 1, 1, cv)
                    if k == 3:
                        f_product()
                    if k == 5:
                        f_low(i - 1)
                    if k == 8:
                        scaled(i, 0)
                    if k == 10:
                        conv_taps(i, 0, cg)
                    if k == 12:
                        silu_times(i)
                steps.leave(TURNS["up"] - 1)

            for i in range(TURNS["down"]):
                for k in range(44):
                    split("down", i, k)
                    if i == 0 and k == 0:
                        scaled(TURNS["up"] - 1, 1)
                    if i == 0 and k == 2:
                        conv_taps(TURNS["up"] - 1, 1, cv)
                    if i == 0 and k == 3:
                        f_product()
                    if i == 0 and k == 5:
                        f_low(TURNS["up"] - 1)
                    if k % 22 == 21:
                        g = k // 22
                        product, read, value = done("down", i, g)
                        k0 = (2 * i + g) * 4
                        at_x = xres[:, k0:k0 + 4, :]
                        product = product[:].rearrange("p (b s) -> p b s", b=4)
                        if k0 + 4 < KD:
                            v.tensor_tensor(at_x, product, at_x, ALU.add).then_inc(read, 1)
                        else:
                            for at_h, done_sem in ((slice(0, 2), sem["last_half_ready"]), (slice(2, 4), read)):
                                v.tensor_tensor(at_x[:, at_h, :], product[:, at_h, :], at_x[:, at_h, :],
                                                ALU.add).then_inc(done_sem, 1)

        @block.gpsimd
        def _(pool):
            p = nc.gpsimd

            def rstd(to, of, count, value, after):
                pool.wait_ge(sem[count], value)
                p.tensor_tensor(to, of, minus_half[:, 0:of.shape[1]], ALU.pow).then_inc(sem[after], 1)

            pool.wait_ge(sem["minus_half_ready"], 1)
            rstd(n_rstd[:, 0:2], n_ms[:, 0:2], "ms_ready", 1, "rstd_ready")
            rstd(v_stat[:, 4:6], v_stat[:, 2:4], "v_ms_ready", 1, "v_rstd_ready")
            p.tensor_copy(v_group[:], v_all[:, :, 0:COLS]).then_inc(sem["v_group_ready"], 1)
            with pool.Fori(1, GROUPS) as i:
                pool.wait_ge(sem["sv_ready"], i)
                p.tensor_copy(v_group[:], v_all[:, :, bass.ds(i * COLS, COLS)]).then_inc(sem["v_group_ready"], 1)
            rstd(n_rstd[:, 0:2], n_ms[:, 0:2], "ms_ready", 2, "rstd_ready")
            rstd(n_rstd[:, 2:4], n_ms[:, 2:4], "ms_ready", 3, "rstd_ready")
            for n in range(4):
                rstd(q_rstd[:], q_ms[:], "q_ms_ready", n + 1, "q_rstd_ready")
            for m in range(M_HEADS):
                rstd(m_rstd[:], m_ms[:], "m_ms_ready", m + 1, "m_rstd_ready")
            rstd(n_rstd[:, 0:2], n_ms[:, 0:2], "ms_ready", 4, "rstd_ready")


def chunks_of(w):
    k, n = w.shape
    w = w.reshape(k // CHUNK_ROWS, ROWS_PER_CHUNK, P, n // COLS, COLS)
    return np.ascontiguousarray(w.transpose(3, 0, 2, 1, 4)).reshape(n // COLS, k // CHUNK_ROWS, P, CHUNK)


CHUNK_ROWS = ROWS_PER_CHUNK * P


def feature_major(a):
    return np.ascontiguousarray(a.T.reshape(-1, P, a.shape[0]).transpose(1, 0, 2))


def lay_out(i):
    w_in, w2, w_up = i["a_w_in"][0], i["w_in_2"][0], i["w_up_2"][0]
    u, v, gate = (chunks_of(w_in[:, k * E:(k + 1) * E]) for k in range(3))
    qk = [chunks_of(w2[:, a:b]) for a, b in ((FQ, FV), (MQ, MV))]
    vv = [chunks_of(w2[:, a:b]) for a, b in ((FV, FG), (MV, MO))]
    ga, gm = chunks_of(w2[:, GA:GM]), chunks_of(w2[:, GM:END])
    pa, pm = chunks_of(i["w_proj_a_2"][0]), chunks_of(i["w_proj_m_2"][0])
    up_g, up_v = chunks_of(w_up[:, :FF]), chunks_of(w_up[:, FF:])
    parts = [v]
    for g in range(GROUPS):
        parts += [u[g], gate[g]]
    parts += [chunks_of(i["a_w_out"][0])] + vv + [qk[0][[0, 2, 1, 3]], qk[1], chunks_of(w2[:, MO:MI]), ga]
    for g in range(4):
        parts += [gm[g], pa[g], pm[g]]
    parts += [chunks_of(i["w_out_2"][0])]
    for g in range(FF // COLS):
        parts += [up_g[g], up_v[g]]
    parts += [chunks_of(i["w_down_2"][0])]
    stream = np.concatenate([a.reshape(-1, P, CHUNK) for a in parts])
    assert stream.shape[0] == CHUNKS

    def cols(a):
        return a.reshape(-1, P).T

    conv = i["conv_w_2"][0]
    bias = np.concatenate([i["fox_f_bias_2"][0], i["m_f_bias_2"][0], i["m_i_bias_2"][0]])
    params = np.concatenate([
        cols(i["a_norm"][0]), cols(i["a_v_gain"][0]), cols(i["final_norm"]), cols(i["norm1_g_2"][0]),
        cols(i["norm2_g_2"][0]), cols(conv[0]), cols(conv[1]), cols(conv[2]), cols(i["conv_b_2"][0]),
        cols(i["q_norm_g_2"][0]), cols(i["k_norm_g_2"][0]), cols(i["m_norm_g_2"][0].reshape(-1)),
        np.broadcast_to(bias, (P, 16))], axis=1)
    w_gates = np.concatenate([w2[:, FG:MQ], w2[:, MF:GA], w2[:, MI:MF]], axis=1)
    gate_w = w_gates.reshape(KD, P, 16).transpose(1, 0, 2).reshape(P, KD * 16)
    t, s = np.arange(P)[:, None], np.arange(P)[None, :]
    consts = np.concatenate([np.zeros((P, P)), np.where(s > t, -1e30, 0.0), np.where(t <= s, 1.0, 0.0)],
                            axis=1).astype(np.float32)
    return {
        "x": feature_major(i["x"][0]),
        "stream": stream,
        "w_s": i["a_w_s"][0].transpose(2, 0, 1),
        "b_s": np.broadcast_to(i["a_b_s"][0], (P, GROUPS, P)),
        "params": params,
        "gate_w": gate_w,
        "identity": np.eye(P, dtype=np.float32),
        "consts": consts,
    }


def kernel(**inputs):
    import concourse.bacc as bacc
    from concourse.bass_utils import run_bass_kernel_spmd

    arrays = {f"in_{k}": np.ascontiguousarray(v) for k, v in
              lay_out({k: np.asarray(v) for k, v in inputs.items()}).items()}
    nc = bacc.Bacc("TRN2", target_bir_lowering=False, num_devices=1)
    args = [nc.dram_tensor(k, v.shape, F32, kind="ExternalInput").ap() for k, v in arrays.items()]
    out = nc.dram_tensor("out", (P, KD, S), F32, kind="ExternalOutput").ap()
    build(nc, *args, out)
    got = run_bass_kernel_spmd(nc, [arrays], core_ids=[0]).results[0]["out"]
    return got.transpose(2, 1, 0).reshape(1, S, D)
```
